# Optimizing a Trainium2 kernel written in Bass

```python
import math
import jax
import jax.numpy as jnp
from jax import lax
import numpy as np

D_MODEL = 1024
BATCH = 1
SEQ = 512
DEPTH = 1
DEC_BATCH = 8
DEC_SEQ = 8
PAST_LEN = 512
PAGE_SIZE = 128

NSA_HEADS = 8
NSA_KV_HEADS = 2
NSA_GROUP = NSA_HEADS // NSA_KV_HEADS
HEAD_DIM = 64
CMP_LEN = 32
CMP_STRIDE = 16
CMP_HIDDEN = 4 * HEAD_DIM
SEL_BLOCK = 64
SEL_TOP = 16
WINDOW = 512
WIN_Q_BLOCK = 128
SEL_Q_BLOCK = 64
DN_HEADS = 8
DN_HEAD_DIM = 64
CONV_W = 4
DN_CHUNK = 64
NUM_BUCKETS = 32
MAX_DISTANCE = 128
N_GROUPS = 4
EXPERTS_PER_GROUP = 8
N_EXPERTS = N_GROUPS * EXPERTS_PER_GROUP
TOP_K_IN_GROUP = 2
D_EXPERT = D_MODEL // 4

EPS = 1e-6
NEG_INF = -1e30
F32 = jnp.float32

NSA_Q_DIM = NSA_HEADS * HEAD_DIM
NSA_KV_DIM = NSA_KV_HEADS * HEAD_DIM
DN_DIM = DN_HEADS * DN_HEAD_DIM
DN_CONV_DIM = 3 * DN_DIM
MIX_WIDTH = NSA_Q_DIM + DN_DIM
IN_SPLITS = (NSA_Q_DIM, NSA_KV_DIM, NSA_KV_DIM, NSA_KV_DIM, NSA_KV_DIM, NSA_KV_DIM, NSA_KV_DIM,
             3 * NSA_HEADS, DN_CONV_DIM, DN_HEADS, DN_HEADS, DN_DIM)
IN_DIM = sum(IN_SPLITS)

kernel_name = 'hymba_nsa_gdn_hiermoe_step'

def rmsnorm(x, g):
    xf = x.astype(F32)
    y = xf * lax.rsqrt(jnp.mean(xf * xf, axis=-1, keepdims=True) + EPS)
    return (y * g.astype(F32)).astype(x.dtype)

def l2norm(x):
    xf = x.astype(F32)
    return (xf * lax.rsqrt(jnp.sum(xf * xf, axis=-1, keepdims=True) + EPS)).astype(x.dtype)

def t5_bucket(rel):
    n = jnp.maximum(rel, 0)
    max_exact = NUM_BUCKETS // 2
    nf = jnp.maximum(n, 1).astype(F32)
    large = max_exact + (jnp.log(nf / max_exact) / math.log(MAX_DISTANCE / max_exact)
                         * (NUM_BUCKETS - max_exact)).astype(jnp.int32)
    large = jnp.minimum(large, NUM_BUCKETS - 1)
    return jnp.where(n < max_exact, n, large)

def rel_bias_heads(rel, rel_bias):
    b = rel_bias.astype(F32)[t5_bucket(rel)]
    b = jnp.moveaxis(b, -1, -3)
    return b.reshape(b.shape[:-3] + (NSA_KV_HEADS, NSA_GROUP) + b.shape[-2:])

def attend(q, k, v, bias, mask):
    s = jnp.einsum('bntkgd,bnlkd->bnkgtl', q, k).astype(F32) * HEAD_DIM ** -0.5 + bias
    m = mask[:, None, None]
    p = jax.nn.softmax(jnp.where(m, s, NEG_INF), axis=-1)
    p = jnp.where(m, p, 0.0)
    o = jnp.einsum('bnkgtl,bnlkd->bntkgd', p.astype(v.dtype), v)
    return o, p

def compress_rows(rows, pos_emb, w1, w2):
    B, L = rows.shape[:2]
    n_cmp = (L - CMP_LEN) // CMP_STRIDE + 1
    idx = jnp.arange(n_cmp)[:, None] * CMP_STRIDE + jnp.arange(CMP_LEN)[None, :]
    blk = rows[:, idx] + pos_emb[:, None, :]
    blk = jnp.swapaxes(blk, 2, 3).reshape(B, n_cmp, NSA_KV_HEADS, CMP_LEN * HEAD_DIM)
    return jax.nn.silu(blk @ w1) @ w2

def nsa_cmp_sel(q, q_pos, kc_rows, vc_rows, ks_rows, vs_rows, lp, rel_bias):
    B, Tq = q.shape[:2]
    L = kc_rows.shape[1]
    kc = compress_rows(kc_rows, lp['cmp_pos_k'], lp['cmp_w1_k'], lp['cmp_w2_k'])
    vc = compress_rows(vc_rows, lp['cmp_pos_v'], lp['cmp_w1_v'], lp['cmp_w2_v'])
    n_cmp = kc.shape[1]
    cmp_end = jnp.arange(n_cmp) * CMP_STRIDE + CMP_LEN - 1
    rel_c = q_pos[:, None] - cmp_end[None, :]
    o_cmp, p_cmp = attend(q[:, None], kc[:, None], vc[:, None],
                          rel_bias_heads(rel_c[None], rel_bias), (rel_c >= 0)[None])
    o_cmp = o_cmp[:, 0]
    n_sel = -(-L // SEL_BLOCK)
    c_start = jnp.arange(n_cmp) * CMP_STRIDE
    s_start = jnp.arange(n_sel) * SEL_BLOCK
    overlap = jnp.clip(jnp.minimum(c_start[:, None] + CMP_LEN, s_start[None] + SEL_BLOCK)
                       - jnp.maximum(c_start[:, None], s_start[None]), 0, None).astype(F32) / CMP_LEN
    imp = jnp.einsum('bkgtc,cs->btks', p_cmp[:, 0], overlap)
    q_blk = q_pos // SEL_BLOCK
    sb = jnp.arange(n_sel)
    forced = (sb[None] == 0) | (sb[None] == q_blk[:, None]) | (sb[None] == q_blk[:, None] - 1)
    avail = s_start[None] <= q_pos[:, None]
    score = jnp.where(forced[None, :, None], 1e9, jnp.where(avail[None, :, None], imp, NEG_INF))
    n_top = min(SEL_TOP, n_sel)
    _, sel_idx = lax.top_k(score, n_top)
    pad = n_sel * SEL_BLOCK - L
    def to_blocks(r):
        r = jnp.pad(r, ((0, 0), (0, pad), (0, 0), (0, 0)))
        return r.reshape(B, n_sel, SEL_BLOCK, NSA_KV_HEADS, HEAD_DIM).transpose(0, 3, 1, 2, 4)
    ks_b = to_blocks(ks_rows)
    vs_b = to_blocks(vs_rows)
    bi = jnp.arange(B)[:, None, None, None]
    ki = jnp.arange(NSA_KV_HEADS)[None, None, :, None]
    tbl = rel_bias.astype(F32).reshape(NUM_BUCKETS, NSA_KV_HEADS, NSA_GROUP).transpose(1, 0, 2)
    qb = SEL_Q_BLOCK if Tq % SEL_Q_BLOCK == 0 else Tq
    nqb = Tq // qb

    def sel_block(args):
        q_i, pos_i, idx_i = args
        kg = ks_b[bi, ki, idx_i]
        vg = vs_b[bi, ki, idx_i]
        k_pos = idx_i[..., None] * SEL_BLOCK + jnp.arange(SEL_BLOCK)
        rel = pos_i[None, :, None, None, None] - k_pos
        bias = tbl[ki[..., None], t5_bucket(rel)]
        s = jnp.einsum('bqkgd,bqknsd->bqkgns', q_i, kg).astype(F32) * HEAD_DIM ** -0.5 + jnp.moveaxis(bias, -1, 3)
        mask = (rel >= 0)[:, :, :, None]
        s = jnp.where(mask, s, NEG_INF).reshape(B, qb, NSA_KV_HEADS, NSA_GROUP, n_top * SEL_BLOCK)
        p = jax.nn.softmax(s, axis=-1)
        p = jnp.where(mask.reshape(B, qb, NSA_KV_HEADS, 1, n_top * SEL_BLOCK), p, 0.0)
        return jnp.einsum('bqkgl,bqkld->bqkgd', p.astype(vg.dtype),
                          vg.reshape(B, qb, NSA_KV_HEADS, n_top * SEL_BLOCK, HEAD_DIM))

    q_m = q.reshape(B, nqb, qb, NSA_KV_HEADS, NSA_GROUP, HEAD_DIM).swapaxes(0, 1)
    pos_m = q_pos.reshape(nqb, qb)
    idx_m = sel_idx.reshape(B, nqb, qb, NSA_KV_HEADS, n_top).swapaxes(0, 1)
    o_sel = lax.map(sel_block, (q_m, pos_m, idx_m))
    o_sel = o_sel.swapaxes(0, 1).reshape(B, Tq, NSA_KV_HEADS, NSA_GROUP, HEAD_DIM)
    return o_cmp, o_sel

def window_prompt(q, k, v, rel_bias):
    B, T = q.shape[:2]
    nb = T // WIN_Q_BLOCK
    span = WINDOW + WIN_Q_BLOCK
    kidx = jnp.arange(nb)[:, None] * WIN_Q_BLOCK + jnp.arange(span)[None]
    padw = ((0, 0), (WINDOW, 0), (0, 0), (0, 0))
    kb = jnp.pad(k, padw)[:, kidx]
    vb = jnp.pad(v, padw)[:, kidx]
    k_pos = kidx - WINDOW
    q_pos = jnp.arange(T).reshape(nb, WIN_Q_BLOCK)
    rel = q_pos[:, :, None] - k_pos[:, None, :]
    mask = (rel >= 0) & (rel < WINDOW) & (k_pos[:, None, :] >= 0)
    o, _ = attend(q.reshape(B, nb, WIN_Q_BLOCK, NSA_KV_HEADS, NSA_GROUP, HEAD_DIM), kb, vb,
                  rel_bias_heads(rel, rel_bias), mask)
    return o.reshape(B, T, NSA_KV_HEADS, NSA_GROUP, HEAD_DIM)

def window_sample(q, q_pos, k, v, k_pos, rel_bias):
    rel = q_pos[:, None] - k_pos[None]
    mask = (rel >= 0) & (rel < WINDOW)
    o, _ = attend(q[:, None], k[:, None], v[:, None], rel_bias_heads(rel[None], rel_bias), mask[None])
    return o[:, 0]

def combine_branches(gate_logit, o_cmp, o_sel, o_win):
    B, T = gate_logit.shape[:2]
    g = jax.nn.sigmoid(gate_logit.astype(F32)).reshape(B, T, NSA_KV_HEADS, NSA_GROUP, 3).astype(o_cmp.dtype)
    o = g[..., 0:1] * o_cmp + g[..., 1:2] * o_sel + g[..., 2:3] * o_win
    return o.reshape(B, T, NSA_Q_DIM)

def causal_conv(x_hist, x_new, w):
    xc = jnp.concatenate([x_hist, x_new], axis=1)
    y = lax.conv_general_dilated(xc, w[:, None, :], window_strides=(1,), padding='VALID',
                                 dimension_numbers=('NWC', 'WIO', 'NWC'), feature_group_count=xc.shape[-1])
    return jax.nn.silu(y), xc[:, -(CONV_W - 1):]

def gated_delta_rule(q, k, v, g, beta, s0):
    B, T, H, DK = q.shape
    C = DN_CHUNK if T >= DN_CHUNK else T
    n = -(-T // C)
    pad = n * C - T

    def prep(a):
        a = jnp.pad(a.astype(F32), ((0, 0), (0, pad)) + ((0, 0),) * (a.ndim - 2))
        a = a.reshape((B, n, C) + a.shape[2:])
        return jnp.moveaxis(a, (1, 3), (0, 2))

    qc, kc, vc, gc, bc = prep(q), prep(k), prep(v), prep(g), prep(beta)
    gcum = jnp.cumsum(gc, axis=-1)
    ii = jnp.arange(C)
    incl = ii[:, None] >= ii[None, :]
    strict = ii[:, None] > ii[None, :]
    diff = gcum[..., :, None] - gcum[..., None, :]
    decay = jnp.where(incl, jnp.exp(jnp.where(incl, diff, 0.0)), 0.0)
    kb = kc * bc[..., None]
    a_mat = jnp.where(strict, jnp.einsum('...id,...jd->...ij', kb, kc) * decay, 0.0)
    eye_plus = a_mat + jnp.eye(C, dtype=F32)
    u = lax.linalg.triangular_solve(eye_plus, vc * bc[..., None], left_side=True, lower=True, unit_diagonal=True)
    w = lax.linalg.triangular_solve(eye_plus, kb * jnp.exp(gcum)[..., None], left_side=True, lower=True, unit_diagonal=True)
    qk = jnp.where(incl, jnp.einsum('...id,...jd->...ij', qc, kc) * decay, 0.0)
    qg = qc * jnp.exp(gcum)[..., None]
    kg = kc * jnp.exp(gcum[..., -1:] - gcum)[..., None]
    glast = jnp.exp(gcum[..., -1])

    def step(S, xs):
        u_i, w_i, qk_i, qg_i, kg_i, gl_i = xs
        v_new = u_i - jnp.einsum('bhck,bhkv->bhcv', w_i, S)
        o = jnp.einsum('bhck,bhkv->bhcv', qg_i, S) + jnp.einsum('bhij,bhjv->bhiv', qk_i, v_new)
        S = S * gl_i[..., None, None] + jnp.einsum('bhck,bhcv->bhkv', kg_i, v_new)
        return S, o

    S, o = lax.scan(step, s0.astype(F32), (u, w, qk, qg, kg, glast))
    o = o.transpose(1, 0, 3, 2, 4).reshape(B, n * C, H, v.shape[-1])[:, :T]
    return o, S

def deltanet_mixer(qkv_raw, b_logit, a_logit, gate, conv_hist, s0, lp):
    B, T = qkv_raw.shape[:2]
    qkv, new_hist = causal_conv(conv_hist, qkv_raw, lp['conv_w'])
    q, k, v = jnp.split(qkv, 3, axis=-1)
    q = l2norm(q.reshape(B, T, DN_HEADS, DN_HEAD_DIM)) * DN_HEAD_DIM ** -0.5
    k = l2norm(k.reshape(B, T, DN_HEADS, DN_HEAD_DIM))
    v = v.reshape(B, T, DN_HEADS, DN_HEAD_DIM)
    beta = jax.nn.sigmoid(b_logit.astype(F32))
    g = -jnp.exp(lp['dn_a_log'].astype(F32)) * jax.nn.softplus(a_logit.astype(F32) + lp['dn_dt_bias'].astype(F32))
    o, s_new = gated_delta_rule(q, k, v, g, beta, s0)
    o = rmsnorm(o, lp['dn_norm_g']) * jax.nn.silu(gate.astype(F32).reshape(B, T, DN_HEADS, DN_HEAD_DIM))
    return o.astype(qkv_raw.dtype).reshape(B, T, DN_DIM), s_new.astype(s0.dtype), new_hist

def hier_moe(h, lp):
    B, T, D = h.shape
    x = h.reshape(B * T, D)
    lg = (x @ lp['router_group_w'] + lp['router_group_b']).astype(F32)
    pg = jax.nn.softmax(lg, axis=-1)
    grp = jnp.argmax(lg, axis=-1)
    wg = jnp.take_along_axis(pg, grp[:, None], axis=-1)
    le = (x @ lp['router_expert_w'] + lp['router_expert_b']).astype(F32).reshape(-1, N_GROUPS, EXPERTS_PER_GROUP)
    le = jnp.take_along_axis(le, grp[:, None, None], axis=1)[:, 0]
    pe, ie = lax.top_k(jax.nn.softmax(le, axis=-1), TOP_K_IN_GROUP)
    pe = pe / jnp.sum(pe, axis=-1, keepdims=True)
    eid = grp[:, None] * EXPERTS_PER_GROUP + ie
    gates = jnp.sum(jax.nn.one_hot(eid, N_EXPERTS, dtype=F32) * (wg * pe)[..., None], axis=1).astype(x.dtype)
    y = jnp.zeros_like(x)
    for e in range(N_EXPERTS):
        he = jax.nn.silu(x @ lp['w_gate'][e]) * (x @ lp['w_up'][e])
        y = y + gates[:, e:e + 1] * (he @ lp['w_down'][e])
    return y.reshape(B, T, D)

def modulation(c, lp):
    mod = jax.nn.silu(c) @ lp['w_ada'] + lp['b_ada']
    return jnp.split(mod[:, None, :], 6, axis=-1)

def modulate(x, g, shift, scale):
    return rmsnorm(x, g) * (1 + scale) + shift

def split_projection(h, lp):
    z = h @ lp['w_in']
    return jnp.split(z, np.cumsum(IN_SPLITS)[:-1].tolist(), axis=-1)

def finish_layer(x, o_nsa, o_dn, g1, sh2, sc2, g2, lp):
    x = x + g1 * (jnp.concatenate([o_nsa, o_dn], axis=-1) @ lp['w_out'])
    return x + g2 * hier_moe(modulate(x, lp['norm_ffn_g'], sh2, sc2), lp)

def layer_prompt(x, c, lp, rel_bias):
    B, T, _ = x.shape
    sh1, sc1, g1, sh2, sc2, g2 = modulation(c, lp)
    h = modulate(x, lp['norm_mix_g'], sh1, sc1)
    q, ck, cv, sk, sv, wk, wv, gl, qkv_raw, bl, al, dg = split_projection(h, lp)
    kv = lambda r: r.reshape(B, T, NSA_KV_HEADS, HEAD_DIM)
    ck, cv, sk, sv, wk, wv = kv(ck), kv(cv), kv(sk), kv(sv), kv(wk), kv(wv)
    q = q.reshape(B, T, NSA_KV_HEADS, NSA_GROUP, HEAD_DIM)
    pos = jnp.arange(T)
    o_cmp, o_sel = nsa_cmp_sel(q, pos, ck, cv, sk, sv, lp, rel_bias)
    o_win = window_prompt(q, wk, wv, rel_bias)
    o_nsa = combine_branches(gl, o_cmp, o_sel, o_win)
    conv_hist = jnp.zeros((B, CONV_W - 1, DN_CONV_DIM), x.dtype)
    s0 = jnp.zeros((B, DN_HEADS, DN_HEAD_DIM, DN_HEAD_DIM), x.dtype)
    o_dn, s_new, conv_new = deltanet_mixer(qkv_raw, bl, al, dg, conv_hist, s0, lp)
    x = finish_layer(x, o_nsa, o_dn, g1, sh2, sc2, g2, lp)
    w_keep = min(WINDOW, T)
    return x, (ck, cv, sk, sv, wk[:, -w_keep:], wv[:, -w_keep:], s_new, conv_new)

def layer_sample(x, c, cmp_k_pool, cmp_v_pool, sel_k_pool, sel_v_pool, win_k, win_v, s0, conv_hist,
                 page_table, lp, rel_bias):
    B, T, _ = x.shape
    past = page_table.shape[1] * PAGE_SIZE
    sh1, sc1, g1, sh2, sc2, g2 = modulation(c, lp)
    h = modulate(x, lp['norm_mix_g'], sh1, sc1)
    q, ck, cv, sk, sv, wk, wv, gl, qkv_raw, bl, al, dg = split_projection(h, lp)
    kv = lambda r: r.reshape(B, T, NSA_KV_HEADS, HEAD_DIM)
    ck, cv, sk, sv, wk, wv = kv(ck), kv(cv), kv(sk), kv(sv), kv(wk), kv(wv)
    q = q.reshape(B, T, NSA_KV_HEADS, NSA_GROUP, HEAD_DIM)

    def with_past(pool, new):
        rows = pool[page_table].reshape(B, past, NSA_KV_HEADS, HEAD_DIM)
        return jnp.concatenate([rows, new], axis=1)

    pos = past + jnp.arange(T)
    o_cmp, o_sel = nsa_cmp_sel(q, pos, with_past(cmp_k_pool, ck), with_past(cmp_v_pool, cv),
                               with_past(sel_k_pool, sk), with_past(sel_v_pool, sv), lp, rel_bias)
    W = win_k.shape[1]
    wk_all = jnp.concatenate([win_k, wk], axis=1)
    wv_all = jnp.concatenate([win_v, wv], axis=1)
    o_win = window_sample(q, pos, wk_all, wv_all, past - W + jnp.arange(W + T), rel_bias)
    o_nsa = combine_branches(gl, o_cmp, o_sel, o_win)
    o_dn, s_new, conv_new = deltanet_mixer(qkv_raw, bl, al, dg, conv_hist, s0, lp)
    x = finish_layer(x, o_nsa, o_dn, g1, sh2, sc2, g2, lp)
    w_keep = min(WINDOW, W + T)
    return x, (ck, cv, sk, sv, wk_all[:, -w_keep:], wv_all[:, -w_keep:], s_new, conv_new)

def setup_inputs(seed: int = 0) -> dict:
    key = jax.random.key(seed)
    ks = jax.random.split(key, 48)

    def nrm(i, shape, scale=1.0):
        return jax.random.normal(ks[i], shape, jnp.float32) * scale

    n_pages = PAST_LEN // PAGE_SIZE
    n_pool = (DEC_BATCH * n_pages * 5) // 4
    win_rows = min(WINDOW, PAST_LEN)
    kv_row = (NSA_KV_HEADS, HEAD_DIM)
    page_table = jax.random.permutation(ks[40], n_pool)[:DEC_BATCH * n_pages].reshape(DEC_BATCH, n_pages).astype(jnp.int32)
    dt = jnp.exp(jax.random.uniform(ks[41], (DEPTH, DN_HEADS), jnp.float32, math.log(1e-3), math.log(1e-1)))
    dt_bias = dt + jnp.log(-jnp.expm1(-dt))
    a_log = jnp.log(jax.random.uniform(ks[42], (DEPTH, DN_HEADS), jnp.float32, 1.0, 16.0))
    return {
        'x_prompt': nrm(0, (BATCH, SEQ, D_MODEL)),
        'x_sample': nrm(1, (DEC_BATCH, DEC_SEQ, D_MODEL)),
        'cache_cmp_k': nrm(2, (DEPTH, n_pool, PAGE_SIZE) + kv_row),
        'cache_cmp_v': nrm(3, (DEPTH, n_pool, PAGE_SIZE) + kv_row),
        'cache_sel_k': nrm(4, (DEPTH, n_pool, PAGE_SIZE) + kv_row),
        'cache_sel_v': nrm(5, (DEPTH, n_pool, PAGE_SIZE) + kv_row),
        'cache_win_k': nrm(6, (DEPTH, DEC_BATCH, win_rows) + kv_row),
        'cache_win_v': nrm(7, (DEPTH, DEC_BATCH, win_rows) + kv_row),
        'state_delta': nrm(8, (DEPTH, DEC_BATCH, DN_HEADS, DN_HEAD_DIM, DN_HEAD_DIM), 0.3),
        'state_conv': nrm(9, (DEPTH, DEC_BATCH, CONV_W - 1, DN_CONV_DIM)),
        'page_table': page_table,
        'c_prompt': nrm(10, (BATCH, D_MODEL)),
        'c_sample': nrm(11, (DEC_BATCH, D_MODEL)),
        'rel_bias': nrm(12, (NUM_BUCKETS, NSA_HEADS), 0.5),
        'w_ada': nrm(13, (DEPTH, D_MODEL, 6 * D_MODEL), 0.5 * D_MODEL ** -0.5),
        'b_ada': nrm(14, (DEPTH, 6 * D_MODEL), 0.01),
        'norm_mix_g': 1.0 + nrm(15, (DEPTH, D_MODEL), 0.05),
        'norm_ffn_g': 1.0 + nrm(16, (DEPTH, D_MODEL), 0.05),
        'w_in': nrm(17, (DEPTH, D_MODEL, IN_DIM), D_MODEL ** -0.5),
        'cmp_pos_k': nrm(18, (DEPTH, CMP_LEN, HEAD_DIM), 0.1),
        'cmp_w1_k': nrm(19, (DEPTH, CMP_LEN * HEAD_DIM, CMP_HIDDEN), (CMP_LEN * HEAD_DIM) ** -0.5),
        'cmp_w2_k': nrm(20, (DEPTH, CMP_HIDDEN, HEAD_DIM), CMP_HIDDEN ** -0.5),
        'cmp_pos_v': nrm(21, (DEPTH, CMP_LEN, HEAD_DIM), 0.1),
        'cmp_w1_v': nrm(22, (DEPTH, CMP_LEN * HEAD_DIM, CMP_HIDDEN), (CMP_LEN * HEAD_DIM) ** -0.5),
        'cmp_w2_v': nrm(23, (DEPTH, CMP_HIDDEN, HEAD_DIM), CMP_HIDDEN ** -0.5),
        'conv_w': nrm(24, (DEPTH, CONV_W, DN_CONV_DIM), CONV_W ** -0.5),
        'dn_a_log': a_log,
        'dn_dt_bias': dt_bias,
        'dn_norm_g': 1.0 + nrm(25, (DEPTH, DN_HEAD_DIM), 0.05),
        'w_out': nrm(26, (DEPTH, MIX_WIDTH, D_MODEL), MIX_WIDTH ** -0.5),
        'router_group_w': nrm(27, (DEPTH, D_MODEL, N_GROUPS), D_MODEL ** -0.5),
        'router_group_b': nrm(28, (DEPTH, N_GROUPS), 0.01),
        'router_expert_w': nrm(29, (DEPTH, D_MODEL, N_EXPERTS), D_MODEL ** -0.5),
        'router_expert_b': nrm(30, (DEPTH, N_EXPERTS), 0.01),
        'expert_w_gate': nrm(31, (DEPTH, N_EXPERTS, D_MODEL, D_EXPERT), D_MODEL ** -0.5),
        'expert_w_up': nrm(32, (DEPTH, N_EXPERTS, D_MODEL, D_EXPERT), D_MODEL ** -0.5),
        'expert_w_down': nrm(33, (DEPTH, N_EXPERTS, D_EXPERT, D_MODEL), D_EXPERT ** -0.5),
        'final_norm_g': 1.0 + nrm(34, (D_MODEL,), 0.05),
    }

def reference(x_prompt, x_sample, cache_cmp_k, cache_cmp_v, cache_sel_k, cache_sel_v, cache_win_k, cache_win_v,
              state_delta, state_conv, page_table, c_prompt, c_sample, rel_bias, w_ada, b_ada, norm_mix_g,
              norm_ffn_g, w_in, cmp_pos_k, cmp_w1_k, cmp_w2_k, cmp_pos_v, cmp_w1_v, cmp_w2_v, conv_w, dn_a_log,
              dn_dt_bias, dn_norm_g, w_out, router_group_w, router_group_b, router_expert_w, router_expert_b,
              expert_w_gate, expert_w_up, expert_w_down, final_norm_g):
    xp, xs = x_prompt, x_sample
    new_p, new_s = [], []
    for l in range(DEPTH):
        lp = dict(w_ada=w_ada[l], b_ada=b_ada[l], norm_mix_g=norm_mix_g[l], norm_ffn_g=norm_ffn_g[l],
                  w_in=w_in[l], cmp_pos_k=cmp_pos_k[l], cmp_w1_k=cmp_w1_k[l], cmp_w2_k=cmp_w2_k[l],
                  cmp_pos_v=cmp_pos_v[l], cmp_w1_v=cmp_w1_v[l], cmp_w2_v=cmp_w2_v[l], conv_w=conv_w[l],
                  dn_a_log=dn_a_log[l], dn_dt_bias=dn_dt_bias[l], dn_norm_g=dn_norm_g[l], w_out=w_out[l],
                  router_group_w=router_group_w[l], router_group_b=router_group_b[l],
                  router_expert_w=router_expert_w[l], router_expert_b=router_expert_b[l],
                  w_gate=expert_w_gate[l], w_up=expert_w_up[l], w_down=expert_w_down[l])
        xp, st_p = layer_prompt(xp, c_prompt, lp, rel_bias)
        xs, st_s = layer_sample(xs, c_sample, cache_cmp_k[l], cache_cmp_v[l], cache_sel_k[l], cache_sel_v[l],
                                cache_win_k[l], cache_win_v[l], state_delta[l], state_conv[l], page_table,
                                lp, rel_bias)
        new_p.append(st_p)
        new_s.append(st_s)
    y_prompt = rmsnorm(xp, final_norm_g)
    y_sample = rmsnorm(xs, final_norm_g)

    def stk(states, i):
        return jnp.stack([s[i] for s in states])

    return (y_prompt, y_sample,
            stk(new_p, 0), stk(new_p, 1), stk(new_p, 2), stk(new_p, 3),
            stk(new_p, 4), stk(new_p, 5), stk(new_p, 6), stk(new_p, 7),
            stk(new_s, 0), stk(new_s, 1), stk(new_s, 2), stk(new_s, 3),
            stk(new_s, 4), stk(new_s, 5), stk(new_s, 6), stk(new_s, 7))


_drawn_inputs = setup_inputs


def setup_inputs(seed=0):
    import zlib

    import numpy as np

    out = dict(_drawn_inputs(seed))
    spreads = {}
    factors = {'cache_cmp_k': 5.151,
     'cache_cmp_v': 2.999,
     'cache_sel_k': 3.996,
     'cache_sel_v': 3.299,
     'rel_bias': 3.307,
     'norm_ffn_g': 3.176,
     'cmp_pos_k': 8.0,
     'cmp_w1_k': 4.477,
     'cmp_w2_k': 4.418,
     'cmp_pos_v': 5.92,
     'dn_norm_g': 6.672,
     'router_group_b': 8.0,
     'router_expert_b': 8.0}
    for name, (base, spread) in spreads.items():
        noise = np.random.default_rng([zlib.crc32(name.encode()), seed]).standard_normal(out[name].shape)
        drawn = base * np.exp(spread * noise) if base else spread * noise
        out[name] = jnp.asarray(drawn.astype(out[name].dtype))
    for name, factor in factors.items():
        out[name] = (out[name] * factor).astype(out[name].dtype)
    return out
```

```python
from contextlib import ExitStack
import math

import numpy as np
import concourse.bass as bass
from concourse import mybir

F32 = mybir.dt.float32
I32 = mybir.dt.int32
ALU = mybir.AluOpType
ACT = mybir.ActivationFunctionType
AX = mybir.AxisListType.X

P = 128
D = 1024
KD = D // P
SEQ = 512
NB = 8
TS = 8
NTOK = SEQ + NB * TS
TILES = 5
PT = SEQ // P
PAST = 512
LS = PAST + TS
PAGE = 128
PAGES = PAST // PAGE
NPOOL = NB * PAGES * 5 // 4
H = 8
KV = 2
G = H // KV
HD = 64
CMP_LEN = 32
CMP_STRIDE = 16
NCMP = (SEQ - CMP_LEN) // CMP_STRIDE + 1
assert NCMP == (LS - CMP_LEN) // CMP_STRIDE + 1
CMP_HIDDEN = 256
BUCKETS = 32
MAXDIST = 128
DNH = 8
CONVD = 3 * DNH * HD
CW = 4
NE = 32
NG = 4
EPG = NE // NG
DE = D // 4
EPS = 1e-6
NEG = -1e30
SCALE = HD ** -0.5
IN_DIM = 3368
Q0, KV0, GL0, QKV0, BETA0, GATE0 = 0, 512, 1280, 1304, 2840, 2856
ZA = QKV0 - KV0
ZB = IN_DIM - BETA0
ZW = ZA + ZB
Z_GL, Z_B, Z_A, Z_DG = 768, ZA, ZA + 8, ZA + 16
NSEQ = NB + 1
RB_C = 519
RB_W = 1040
STRIP = 896
VAR = [0] * PT + [1]
ROWS = [P] * PT + [NB * TS]


def bucket_edges():
    half = BUCKETS // 2
    edges, last = [], -1
    for n in range(RB_C + 1):
        b = n if n < half else min(BUCKETS - 1, half + int(math.log(n / half) / math.log(MAXDIST / half) * half + 1e-9))
        if b != last:
            assert b == last + 1
            edges.append(n)
            last = b
    assert len(edges) == BUCKETS
    return edges


class Chain:

    def __init__(self, eng, sem):
        self.eng, self.sem, self.n = eng, sem, 0

    def __call__(self, ins):
        self.n += 1
        ins.then_inc(self.sem, 1)
        self.eng.wait_ge(self.sem, self.n)


class Bufs:
    pass


def stage_modulation(nc, m, sb, sem, t):
    PS = m.PS
    c_in, const, ada_in, bada_in, rb_in = sem("c_in"), sem("const"), [sem(f"ada_in{i}") for i in range(4)], sem("bada_in"), sem("rb_in")
    ident_ok, silu_ok, cT_ps, cT_ok = sem("ident_ok"), sem("silu_ok"), sem("cT_ps"), sem("cT_ok")
    mod_ps, mod_ok, mod_out = sem("mod_ps"), sem("mod_ok"), sem("mod_out")
    rb_ok, rb_out, pchain, bias_in = sem("rb_ok"), sem("rb_out"), sem("m_pchain"), sem("bias_in")
    edges = bucket_edges()
    GROUPS = 6 * D // 512

    with ExitStack() as ctx:
        crow = ctx.enter_context(nc.sbuf_tensor("crow", [NSEQ, D], F32))
        cT = ctx.enter_context(nc.sbuf_tensor("cT", [P, KD, NSEQ], F32))
        bada = ctx.enter_context(nc.sbuf_tensor("bada", [NSEQ, 6 * D], F32))
        modrows = ctx.enter_context(nc.sbuf_tensor("modrows", [NSEQ, 6 * D], F32))
        wada = ctx.enter_context(nc.sbuf_tensor("wada", [P, 4, KD, 512], F32))
        gains = ctx.enter_context(nc.sbuf_tensor("gains", [NSEQ, 2, D], F32))
        rbT = ctx.enter_context(nc.sbuf_tensor("rbT", [H, BUCKETS], F32))
        rrow = ctx.enter_context(nc.sbuf_tensor("rrow", [H, 2, RB_W], F32))
        block = ctx.enter_context(nc.Block())

        @block.sync
        def _(sp):
            sp.dma_start(crow[0:1, :], t["c_prompt"]).then_inc(c_in, 16)
            sp.dma_start(crow[1:NSEQ, :], t["c_sample"]).then_inc(c_in, 16)
            with nc.allow_non_contiguous_dma(reason="256 words, transposed"):
                sp.dma_start(rbT[:, :], t["rel_bias"].rearrange("b h -> h b")).then_inc(rb_in, 16)
            wv = t["w_ada"][0].rearrange("(k p) n -> p k n", p=P)
            for g in range(GROUPS):
                if g >= 4:
                    sp.wait_ge(mod_ps, g - 3)
                sp.dma_start(wada[:, g % 4], wv[:, :, g * 512:(g + 1) * 512]).then_inc(ada_in[g % 4], 16)
                if g == 0:
                    sp.dma_start(bada[:, :], t["b_ada"][0].partition_broadcast(NSEQ)).then_inc(bada_in, 16)
                    sp.dma_start(gains[:, 0, :], t["norm_mix_g"][0].partition_broadcast(NSEQ)).then_inc(bada_in, 16)
                    sp.dma_start(gains[:, 1, :], t["norm_ffn_g"][0].partition_broadcast(NSEQ)).then_inc(bada_in, 16)
            sp.wait_ge(mod_ok, GROUPS + 4)
            sp.dma_start(m.mod_dram.ap(), modrows[:, :]).then_inc(mod_out, 16)
            sp.wait_ge(mod_out, 16)

        @block.gpsimd
        def _(pool):
            link = Chain(pool, pchain)
            link(nc.gpsimd.memset(m.ident[:], 0.0))
            nc.gpsimd.affine_select(out=m.ident[:], in_=m.ident[:], compare_op=ALU.not_equal, fill=1.0, base=0,
                                    pattern=[[-1, P]], channel_multiplier=1).then_inc(ident_ok, 1)
            link(nc.gpsimd.memset(m.ones[:], 1.0))
            link(nc.gpsimd.affine_select(out=m.before[:], in_=m.ones[:], compare_op=ALU.is_gt, fill=0.0, base=0,
                                         pattern=[[1, P]], channel_multiplier=-1))
            link(nc.gpsimd.affine_select(out=m.seen[:], in_=m.ones[:, 0:1], compare_op=ALU.is_ge, fill=0.0, base=1 - CMP_LEN,
                                         pattern=[[0, 1]], channel_multiplier=1))
            nc.gpsimd.memset(m.eps[:, 0:1], EPS)
            nc.gpsimd.memset(m.eps[:, 1:2], EPS * HD)
            nc.gpsimd.memset(m.eps[:, 2:3], 1.0).then_inc(const, 1)
            pool.wait_ge(rb_ok, 2 * (BUCKETS + 1) + 1)
            pool.dma_start(m.rb_dram.ap().rearrange("v h w -> h v w"), rrow[:, :, :]).then_inc(rb_out, 16)
            pool.wait_ge(rb_out, 16)
            rows = m.rb_dram.ap().rearrange("v h w -> v (h w)")
            pool.dma_start(m.rb_rep.ap()[0:P, :], rows[0].partition_broadcast(P)).then_inc(rb_out, 16)
            pool.dma_start(m.rb_rep.ap()[P:P + TS, :], rows[1].partition_broadcast(TS)).then_inc(rb_out, 16)
            pool.wait_ge(rb_out, 48)

        @block.tensor
        def _(pe):
            pe.wait_ge(silu_ok, 1)
            pe.wait_ge(ident_ok, 1)
            for k in range(KD):
                last = nc.tensor.transpose(PS[:, 6, k * NSEQ:(k + 1) * NSEQ], crow[:, k * P:(k + 1) * P], m.ident[0:NSEQ, 0:NSEQ])
            last.then_inc(cT_ps, 1)
            pe.wait_ge(cT_ok, 1)
            for g in range(GROUPS):
                pe.wait_ge(ada_in[g % 4], 16 * (g // 4 + 1))
                if g >= 2:
                    pe.wait_ge(mod_ok, g - 1)
                for k in range(KD):
                    last = nc.tensor.matmul(PS[0:NSEQ, g % 2, :], cT[:, k, :], wada[:, g % 4, k, :], start=(k == 0), stop=(k == KD - 1))
                last.then_inc(mod_ps, 1)

        @block.scalar
        def _(act):
            act.wait_ge(c_in, 32)
            nc.scalar.activation(crow[:, :], crow[:, :], ACT.Silu).then_inc(silu_ok, 1)

        @block.vector
        def _(dve):
            dve.wait_ge(cT_ps, 1)
            nc.vector.tensor_copy(cT[:, :, :], PS[:, 6, 0:KD * NSEQ].rearrange("p (k s) -> p k s", s=NSEQ)).then_inc(cT_ok, 1)
            dve.wait_ge(rb_in, 16)
            bias = Chain(dve, rb_ok)
            for v in range(2):
                bias(nc.vector.memset(rrow[:, v, :], NEG))
                for b in range(BUCKETS):
                    lo = edges[b]
                    hi = edges[b + 1] if b + 1 < BUCKETS else RB_C + 1
                    a, z = RB_C - hi + 1, RB_C - lo + 1
                    nc.vector.tensor_copy(rrow[:, v, a:z], rbT[:, b:b + 1].to_broadcast([H, z - a])).then_inc(rb_ok, 1)
                bias.n += BUCKETS
                dve.wait_ge(rb_ok, bias.n)
            bias(nc.vector.memset(rrow[:, 1, 0:RB_C - SEQ + 1], NEG))
            dve.wait_ge(bada_in, 48)
            for g in range(GROUPS):
                dve.wait_ge(mod_ps, g + 1)
                c = g * 512
                nc.vector.tensor_tensor(modrows[:, c:c + 512], PS[0:NSEQ, g % 2, :], bada[:, c:c + 512], ALU.add).then_inc(mod_ok, 1)
            dve.wait_ge(mod_ok, GROUPS)
            for g in (2, 3, 8, 9):
                c = g * 512
                nc.vector.scalar_tensor_tensor(out=modrows[:, c:c + 512], in0=modrows[:, c:c + 512], scalar=1.0,
                                               in1=gains[:, g // 6, (g % 2) * 512:(g % 2 + 1) * 512],
                                               op0=ALU.add, op1=ALU.mult).then_inc(mod_ok, 1)


def spread_rows(eng, m, dst, first, n, done):
    eng.dma_start(dst[:, 0].rearrange("p a d -> p (a d)"), m.mod_dram.ap()[0, first * D:(first + n) * D].partition_broadcast(P)).then_inc(done, 16)
    for b in range(NB):
        eng.dma_start(dst[b * TS:(b + 1) * TS, 1].rearrange("p a d -> p (a d)"),
                      m.mod_dram.ap()[1 + b, first * D:(first + n) * D].partition_broadcast(TS)).then_inc(done, 16)


SPREAD_DMAS = 1 + NB


def stage_projection(nc, m, sb, sem, t, outs):
    PS = m.PS
    x_in, h_ok, hT_ps, hT_ok = sem("x_in"), sem("h_ok"), sem("hT_ps"), sem("hT_ok")
    mod_in, masks, zeroed = sem("mod_in"), sem("masks"), sem("zeroed")
    w_in = [sem(f"w_in{i}") for i in range(3)]
    z_ps, z_v, z_a, sq, rt, dch, rows_out = sem("z_ps"), sem("z_v"), sem("z_a"), sem("sq"), sem("rt"), sem("p_dch"), sem("rows_out")
    hist_in, hist_ps, hist_ok = sem("hist_in"), sem("hist_ps"), sem("hist_ok")
    groups = [(KV0, ZA // 2, False), (KV0 + ZA // 2, ZA // 2, False), (BETA0, ZB, False),
              (QKV0, 512, True), (QKV0 + 512, 512, True), (QKV0 + 1024, 512, True), (Q0, 512, True)]
    QG = 6
    slot_dmas = [[], [], []]
    for g in range(len(groups)):
        slot_dmas[g % 3].append(KD * KV if g == QG else 1)
    units = []
    for g, (c, w, chan) in enumerate(groups):
        for i in range(4 if chan else TILES):
            units.append((g, i))
    last_unit = [max(n for n, u in enumerate(units) if u[0] == g) + 1 for g in range(len(groups))]
    own = ["v" if n % 2 else "a" for n in range(len(units))]
    before = lambda n, e: sum(o == e for o in own[:n + 1])

    with ExitStack() as ctx:
        wring = ctx.enter_context(nc.sbuf_tensor("wring", [P, 3, KD, ZB], F32))
        ssq = ctx.enter_context(nc.sbuf_tensor("ssq", [P, 3, TILES], F32))
        hT = ctx.enter_context(nc.sbuf_tensor("hT", [P, KD, NTOK], F32))
        hist = ctx.enter_context(nc.sbuf_tensor("hist", [NB * (CW - 1), CONVD], F32))
        x = ctx.enter_context(nc.sbuf_tensor("x", [P, TILES, D], F32))
        mod = ctx.enter_context(nc.sbuf_tensor("mod01", [P, 2, 2, D], F32))
        zero = m.mixT[0:T, :, :].rearrange("p c n -> p (c n)")[:, 0:D]
        convw = ctx.enter_context(nc.sbuf_tensor("convw", [CW, CONVD], F32))
        block = ctx.enter_context(nc.Block())

        def evacuate(eng, n, copy, done):
            g, i = units[n]
            c, w, chan = groups[g]
            b = 2 * (n % 3)
            if chan:
                if g == QG:
                    copy(m.qT[:, i, :], PS[:, b:b + 2, :].rearrange("p b n -> p (b n)")[:, 0:NTOK]).then_inc(done, 1)
                else:
                    ch = (g - 3) * 4 + i
                    copy(m.xc[:, ch, CW - 1:CW - 1 + SEQ], PS[:, b, :])
                    copy(m.xc[:, ch, CW - 1 + SEQ:].rearrange("p (b j) -> p b j", j=TS + CW - 1)[:, :, CW - 1:],
                         PS[:, b + 1, 0:NB * TS].rearrange("p (b j) -> p b j", j=TS)).then_inc(done, 1)
            else:
                r = ROWS[i]
                o = (0, ZA // 2, ZA)[g]
                src = PS[0:r, b, 0:w] if w <= 512 else PS[0:r, b:b + 2, 0:w // 2]
                dst = m.z[0:r, i, o:o + w]
                if w > 512:
                    dst = dst.rearrange("p (b n) -> p b n", b=2)
                copy(dst, src).then_inc(done, 1)

        def copy_hT(dve, i):
            r, b = ROWS[i], 2 * (i % 2)
            dve.wait_ge(hT_ps, i + 1)
            nc.vector.tensor_copy(hT[:, :, i * P:i * P + r], PS[:, b:b + 2, :].rearrange("p b (k n) -> p (b k) n", n=P)[:, :, 0:r]).then_inc(hT_ok, 1)

        @block.sync
        def _(sp):
            for i in range(PT):
                sp.dma_start(x[:, i, :], t["x_prompt"][0, i * P:(i + 1) * P, :]).then_inc(x_in, 16)
            sp.dma_start(x[0:NB * TS, PT, :], t["x_sample"].rearrange("b j d -> (b j) d")).then_inc(x_in, 16)
            spread_rows(sp, m, mod, 0, 2, mod_in)
            sp.dma_start(hist[:, :], t["state_conv"][0].rearrange("b j c -> (b j) c")).then_inc(hist_in, 16)
            sp.dma_start(convw[:, :], t["conv_w"][0]).then_inc(hist_in, 16)
            wv = t["w_in"][0].rearrange("(k p) n -> p k n", p=P)
            for g, (c, w, chan) in enumerate(groups):
                if g >= 3:
                    sp.wait_ge(z_ps, last_unit[g - 3])
                if g == QG:
                    for k in range(KD):
                        for v in range(KV):
                            sp.dma_start(wring[:, g % 3, k, 0:512].rearrange("p (g v d) -> p g v d", v=KV, g=G)[:, :, v],
                                         wv[:, k, v * G * HD:(v + 1) * G * HD].rearrange("p (g d) -> p g d", g=G)).then_inc(w_in[g % 3], 16)
                else:
                    sp.dma_start(wring[:, g % 3, :, 0:w], wv[:, :, c:c + w]).then_inc(w_in[g % 3], 16)

        @block.gpsimd
        def _(pool):
            link = Chain(pool, masks)
            link(nc.gpsimd.memset(zero, 0.0))
            xs = m.xs_dram.ap().rearrange("(j p) d -> j p d", p=T)
            for j in range(NT):
                pool.dma_start(xs[j], zero).then_inc(zeroed, 16)
            for i, c in enumerate((HD, TS)):
                nb = P // c
                u = m.same[:, i, :].rearrange("p (b j) -> p b j", j=c)
                link(nc.gpsimd.memset(m.same[:, i, :], 1.0))
                link(nc.gpsimd.affine_select(out=u, in_=u, compare_op=ALU.is_ge, fill=0.0, base=0,
                                             pattern=[[-c, nb], [0, c]], channel_multiplier=1))
                link(nc.gpsimd.affine_select(out=u, in_=u, compare_op=ALU.is_ge, fill=0.0, base=c - 1,
                                             pattern=[[c, nb], [0, c]], channel_multiplier=-1))
                link(nc.gpsimd.affine_select(out=m.upinc[:, i, :], in_=m.same[:, i, :], compare_op=ALU.is_ge,
                                             fill=0.0, base=0, pattern=[[1, P]], channel_multiplier=-1))
                link(nc.gpsimd.tensor_scalar(m.upneg[:, i, :], m.upinc[:, i, :], 1.0, 1e30, ALU.subtract, ALU.mult))
            for c in range(2):
                link(nc.gpsimd.tensor_copy(m.chunk[:, c, :].rearrange("p (a j) -> p a j", j=HD),
                                           m.same[:, 0, c * HD:(c + 1) * HD].unsqueeze(1).to_broadcast([P, 2, HD])))
            link(nc.gpsimd.tensor_copy(m.bmask[:, :], m.same[:, 1, 0:NB * TS:TS]))
            for l in range(6):
                w = 2 ** l
                nb = P // (2 * w)
                link(nc.gpsimd.memset(m.level[:, l, :], 1.0))
                u = m.level[:, l, :].rearrange("p (b s j) -> p b s j", s=2, j=w)
                link(nc.gpsimd.affine_select(out=u, in_=u, compare_op=ALU.is_ge, fill=0.0, base=-w,
                                             pattern=[[-2 * w, nb], [-P, 2], [0, w]], channel_multiplier=1))
                link(nc.gpsimd.affine_select(out=u, in_=u, compare_op=ALU.is_ge, fill=0.0, base=2 * w - 1,
                                             pattern=[[2 * w, nb], [0, 2], [0, w]], channel_multiplier=-1))
            pool.wait_ge(zeroed, 16 * NT)

        @block.scalar
        def _(act):
            for i in range(TILES):
                r = ROWS[i]
                act.wait_ge(x_in, 16 * TILES)
                nc.scalar.activation(PS[0:r, 6:8, :].rearrange("p b n -> p (b n)"), x[0:r, i, :], ACT.Square, accum_out=ssq[0:r, 0, i:i + 1]).then_inc(sq, 1)
                act.wait_ge(sq, i + 1)
                nc.scalar.activation(ssq[0:r, 1, i:i + 1], ssq[0:r, 0, i:i + 1], ACT.Sqrt, scale=1.0 / D, bias=m.eps[0:r, 0:1]).then_inc(rt, 1)
            for n, (g, i) in enumerate(units):
                if own[n] == "a":
                    act.wait_ge(z_ps, n + 1)
                    evacuate(act, n, nc.scalar.copy, z_a)
            act.wait_ge(z_v, before(9, "v"))
            act.wait_ge(z_a, before(9, "a"))
            for j in range(6):
                act.dma_start(outs[2 + j].rearrange("l b (i p) k d -> p (l b i) (k d)", p=P), m.z[:, 0:PT, j * P:(j + 1) * P]).then_inc(rows_out, 16)
                if j < 4:
                    act.dma_start(outs[10 + j].rearrange("l b s k d -> (l b s) (k d)"), m.z[0:NB * TS, PT, j * P:(j + 1) * P]).then_inc(rows_out, 16)
            for j in range(2):
                for b in range(NB):
                    act.dma_start(outs[14 + j][0, b, PAST - TS:PAST].rearrange("s k d -> s (k d)"),
                                  m.z[b * TS:(b + 1) * TS, PT, (4 + j) * P:(5 + j) * P]).then_inc(rows_out, 16)
                    act.dma_start(outs[14 + j][0, b, 0:PAST - TS].rearrange("s k d -> s (k d)"),
                                  t["cache_win_k" if j == 0 else "cache_win_v"][0, b, TS:PAST].rearrange("s k d -> s (k d)")).then_inc(rows_out, 16)
            act.wait_ge(rows_out, 16 * (10 + 4 * NB))

        @block.vector
        def _(dve):
            link = Chain(dve, dch)
            link(nc.vector.memset(m.xc[:, :, 0:CW - 1], 0.0))
            link(nc.vector.memset(m.z[:, PT, :], 0.0))
            dve.wait_ge(mod_in, 16 * SPREAD_DMAS)
            for i in range(TILES):
                r, v = ROWS[i], VAR[i]
                dve.wait_ge(rt, i + 1)
                link(nc.vector.reciprocal(ssq[0:r, 2, i:i + 1], ssq[0:r, 1, i:i + 1]))
                link(nc.vector.scalar_tensor_tensor(out=x[0:r, i, :], in0=x[0:r, i, :], scalar=ssq[0:r, 2, i:i + 1],
                                                    in1=mod[0:r, v, 1, :], op0=ALU.mult, op1=ALU.mult))
                nc.vector.tensor_tensor(x[0:r, i, :], x[0:r, i, :], mod[0:r, v, 0, :], ALU.add).then_inc(h_ok, 1)
                if i >= 1:
                    copy_hT(dve, i - 1)
            copy_hT(dve, TILES - 1)
            dve.wait_ge(hist_ps, 1)
            nh = NB * (CW - 1)
            for c in range(12):
                nc.vector.tensor_copy(m.xc[:, c, CW - 1 + SEQ:].rearrange("p (b j) -> p b j", j=TS + CW - 1)[:, :, 0:CW - 1],
                                      PS[:, 6, c * nh:(c + 1) * nh].rearrange("p (b j) -> p b j", j=CW - 1)).then_inc(hist_ok, 1)
            nc.vector.tensor_copy(m.convwT[:, :, :], PS[:, 7, 0:12 * CW].rearrange("p (c j) -> p c j", j=CW))
            for n, (g, i) in enumerate(units):
                if own[n] == "v":
                    dve.wait_ge(z_ps, n + 1)
                    evacuate(dve, n, nc.vector.tensor_copy, z_v)

        @block.tensor
        def _(pe):
            for i in range(TILES):
                r, b = ROWS[i], 2 * (i % 2)
                pe.wait_ge(h_ok, i + 1)
                if i >= 2:
                    pe.wait_ge(hT_ok, i - 1)
                for k in range(KD):
                    last = nc.tensor.transpose(PS[:, b + k // 4, (k % 4) * P:(k % 4) * P + r], x[0:r, i, k * P:(k + 1) * P], m.ident[0:r, 0:r])
                last.then_inc(hT_ps, 1)
            nh = NB * (CW - 1)
            pe.wait_ge(hist_in, 32)
            for c in range(12):
                last = nc.tensor.transpose(PS[:, 6, c * nh:(c + 1) * nh], hist[:, c * P:(c + 1) * P], m.ident[0:nh, 0:nh])
            for c in range(12):
                last = nc.tensor.transpose(PS[:, 7, c * CW:(c + 1) * CW], convw[:, c * P:(c + 1) * P], m.ident[0:CW, 0:CW])
            last.then_inc(hist_ps, 1)
            pe.wait_ge(hT_ok, TILES)
            for n, (g, i) in enumerate(units):
                c, w, chan = groups[g]
                b = 2 * (n % 3)
                if i == 0:
                    pe.wait_ge(w_in[g % 3], 16 * sum(slot_dmas[g % 3][:g // 3 + 1]))
                if n >= 3:
                    pe.wait_ge(z_v if own[n - 3] == "v" else z_a, before(n - 3, own[n - 3]))
                for k in range(KD):
                    s = dict(start=(k == 0), stop=(k == KD - 1))
                    if chan:
                        lhs = wring[:, g % 3, k, i * P:(i + 1) * P]
                        nc.tensor.matmul(PS[:, b, :], lhs, hT[:, k, 0:SEQ], **s)
                        last = nc.tensor.matmul(PS[:, b + 1, 0:NB * TS], lhs, hT[:, k, SEQ:NTOK], **s)
                    else:
                        r = ROWS[i]
                        lhs = hT[:, k, i * P:i * P + r]
                        if w <= 512:
                            last = nc.tensor.matmul(PS[0:r, b, 0:w], lhs, wring[:, g % 3, k, 0:w], **s)
                        else:
                            nc.tensor.matmul(PS[0:r, b, 0:w // 2], lhs, wring[:, g % 3, k, 0:w // 2], **s)
                            last = nc.tensor.matmul(PS[0:r, b + 1, 0:w // 2], lhs, wring[:, g % 3, k, w // 2:w], **s)
                last.then_inc(z_ps, 1)


NPAD = TILES * P
XS = CW - 1 + SEQ
XW = XS + NB * (TS + CW - 1)


def stage_conv(nc, m, sb, sem, t, outs):
    PS = m.PS
    conv_ok, silu_ok, sq_ok, ss_ps, ss_ok, rt_ok = sem("conv_ok"), sem("csilu_ok"), sem("csq_ok"), sem("ss_ps"), sem("ss_ok"), sem("crt_ok")
    y_ok, kv_ps, kv_ok, chain, chainp = sem("y_ok"), sem("kv_ps"), sem("kv_ok"), sem("c_chain"), sem("c_chainp")
    hc_ok, hc_ps, hc_rows, st_out = sem("hc_ok"), sem("hc_ps"), sem("hc_rows"), sem("st_out")
    NC_ = CONVD // P
    QK = 2 * DNH * HD // P
    N = XW - CW + 1
    nh = NSEQ * (CW - 1)
    with ExitStack() as ctx:
        acc = ctx.enter_context(nc.sbuf_tensor("acc", [P, 2, XW], F32))
        sq = ctx.enter_context(nc.sbuf_tensor("sq", [P, 2, NPAD], F32))
        hc = ctx.enter_context(nc.sbuf_tensor("hc", [P, NC_, nh], F32))
        hrows = ctx.enter_context(nc.sbuf_tensor("hrows", [nh, CONVD], F32))
        ss = m.kvt[:, :, :].rearrange("p i n -> p (i n)").rearrange("p (c n) -> p c n", n=NPAD)
        block = ctx.enter_context(nc.Block())

        def take_sum(dve, c):
            dve.wait_ge(ss_ps, c + 1)
            b = 2 * (c % 2)
            nc.vector.tensor_copy(ss[:, c, :], PS[:, b:b + 2, :].rearrange("p b n -> p (b n)")[:, 0:NPAD]).then_inc(ss_ok, 1)

        @block.gpsimd
        def _(pool):
            nc.gpsimd.tensor_copy(hc[:, :, 0:CW - 1], m.xc[:, :, SEQ:SEQ + CW - 1]).then_inc(hc_ok, 1)
            nc.gpsimd.tensor_copy(hc[:, :, CW - 1:].rearrange("p c (b j) -> p c b j", j=CW - 1),
                                  m.xc[:, :, XS:].rearrange("p c (b j) -> p c b j", j=TS + CW - 1)[:, :, :, TS:]).then_inc(hc_ok, 1)

        @block.scalar
        def _(act):
            for c in range(NC_):
                act.wait_ge(conv_ok, c + 1)
                nc.scalar.activation(m.yT[:, c, 0:SEQ], acc[:, c % 2, 0:SEQ], ACT.Silu).then_inc(silu_ok, 1)
                nc.scalar.activation(m.yT[:, c, SEQ:NTOK].rearrange("p (b j) -> p b j", j=TS),
                                     acc[:, c % 2, XS:].rearrange("p (b j) -> p b j", j=TS + CW - 1)[:, :, 0:TS], ACT.Silu).then_inc(silu_ok, 1)
                if c < QK:
                    act.wait_ge(silu_ok, 2 * c + 2)
                    if c >= 2:
                        act.wait_ge(ss_ps, c - 1)
                    nc.scalar.activation(sq[:, c % 2, :], m.yT[:, c, :], ACT.Square).then_inc(sq_ok, 1)
            for c in range(QK):
                act.wait_ge(ss_ok, c + 1)
                s = float(HD) if c < QK // 2 else 1.0
                nc.scalar.activation(ss[:, c, :], ss[:, c, :], ACT.Sqrt, scale=s, bias=m.eps[:, 1:2] if c < QK // 2 else m.eps[:, 0:1]).then_inc(rt_ok, 1)
            act.wait_ge(hc_ps, 1)
            nc.scalar.activation(hrows[:, :], PS[0:nh, 4:7, :].rearrange("p b n -> p (b n)"), ACT.Copy).then_inc(hc_rows, 1)
            act.wait_ge(hc_rows, 1)
            act.dma_start(outs[9][0, 0], hrows[0:CW - 1, :]).then_inc(st_out, 16)
            act.dma_start(outs[17][0].rearrange("b j c -> (b j) c"), hrows[CW - 1:nh, :]).then_inc(st_out, 16)
            act.wait_ge(st_out, 32)

        @block.vector
        def _(dve):
            link = Chain(dve, chain)
            link(nc.vector.memset(m.yT[:, :, NTOK:NPAD], 0.0))
            for c in range(NC_):
                if c >= 2:
                    dve.wait_ge(silu_ok, 2 * (c - 1))
                a = acc[:, c % 2, 0:N]
                link(nc.vector.tensor_scalar(a, m.xc[:, c, 0:N], m.convwT[:, c, 0:1], None, ALU.mult))
                for j in range(1, CW):
                    ins = nc.vector.scalar_tensor_tensor(out=a, in0=m.xc[:, c, j:j + N], scalar=m.convwT[:, c, j:j + 1], in1=a, op0=ALU.mult, op1=ALU.add)
                    if j < CW - 1:
                        link(ins)
                    else:
                        ins.then_inc(conv_ok, 1)
                if 1 <= c < QK + 1:
                    take_sum(dve, c - 1)
            for c in range(QK):
                dve.wait_ge(rt_ok, c + 1)
                link(nc.vector.reciprocal(ss[:, c, :], ss[:, c, :]))
                nc.vector.tensor_tensor(m.yT[:, c, :], m.yT[:, c, :], ss[:, c, :], ALU.mult).then_inc(y_ok, 1)
            dve.wait_ge(y_ok, QK)
            for i in range(TILES):
                dve.wait_ge(kv_ps, i + 1)
                nc.vector.tensor_copy(m.kvt[:, i, :], PS[:, 2 * (i % 2):2 * (i % 2) + 2, :].rearrange("p b n -> p (b n)")).then_inc(kv_ok, 1)

        @block.tensor
        def _(pe):
            pe.wait_ge(hc_ok, 2)
            for c in range(NC_):
                last = nc.tensor.transpose(PS[0:nh, 4 + c // 4, (c % 4) * P:(c % 4 + 1) * P], hc[:, c, :], m.ident[:, :])
            last.then_inc(hc_ps, 1)
            for c in range(QK):
                pe.wait_ge(sq_ok, c + 1)
                if c >= 2:
                    pe.wait_ge(ss_ok, c - 1)
                b = 2 * (c % 2)
                nc.tensor.matmul(PS[:, b, :], m.same[:, 0, :], sq[:, c % 2, 0:512], start=True, stop=True)
                nc.tensor.matmul(PS[:, b + 1, 0:NPAD - 512], m.same[:, 0, :], sq[:, c % 2, 512:NPAD], start=True, stop=True).then_inc(ss_ps, 1)
            pe.wait_ge(y_ok, QK)
            pe.wait_ge(silu_ok, 2 * NC_)
            for i in range(TILES):
                if i >= 2:
                    pe.wait_ge(kv_ok, i - 1)
                for c in range(KD):
                    last = nc.tensor.transpose(PS[:, 2 * (i % 2) + c // 4, (c % 4) * P:(c % 4 + 1) * P], m.yT[:, QK // 2 + c, i * P:(i + 1) * P], m.ident[:, :])
                last.then_inc(kv_ps, 1)


def heads_em(ap):
    return ap.rearrange("p (m e n) -> p e m n", m=DNH // 2, e=2)


def stage_delta(nc, m, sb, sem, t, outs):
    PS = m.PS
    st_in, gates_a, gch = sem("st_in"), sem("gates_a"), sem("d_gch")
    chain, achain = sem("d_chain"), sem("d_achain")
    cum_ps, cum_ok, gb_rhs, gb_ps, eg_ok, neg_ps, d_in, d_exp = [sem("d_" + x) for x in ("cum_ps", "cum_ok", "gb_rhs", "gb_ps", "eg_ok", "neg_ps", "d_in", "d_exp")]
    kk_ps, bt_ok, qk_ps, qk_ok, ty_ok = [sem("d_" + x) for x in ("kk_ps", "bt_ok", "qk_ps", "qk_ok", "ty_ok")]
    lp_ps, lp_ok, lt_ps, lt_ok = [sem("d_" + x) for x in ("lp_ps", "lp_ok", "lt_ps", "lt_ok")]
    kb_ok, wu_ps, wu_ok, qg_ok = [sem("d_" + x) for x in ("kb_ok", "wu_ps", "wu_ok", "qg_ok")]
    ws_ps, v_ok, so_ps, s_ok, o_ok, vm_ok, o_ss, o_rt, o_fin, o_ps, o_T = [sem("d_" + x) for x in ("ws_ps", "v_ok", "so_ps", "s_ok", "o_ok", "vm_ok", "o_ss", "o_rt", "o_fin", "o_ps", "o_T")]
    sto, mask_ok, su_ps = sem("d_sto"), sem("d_mask_ok"), sem("d_su_ps")
    LEVELS = [6] * PT + [3]
    M4 = DNH // 2

    with ExitStack() as ctx:
        def tb(name, shape):
            return ctx.enter_context(nc.sbuf_tensor(name, shape, F32))

        arow, dtrow, grow = tb("arow", [P, DNH]), tb("dtrow", [P, DNH]), tb("grow", [P, HD])
        beta, g, sp_, sp2 = tb("beta", [P, TILES, DNH]), tb("g", [P, TILES, DNH]), tb("sp_", [P, TILES, DNH]), tb("sp2", [P, TILES, DNH])
        cum = tb("cum", [P, 3, DNH])
        ecum = tb("ecum", [P, 3, DNH])
        bcum = tb("bcum", [P, DNH])
        egl = tb("egl", [P, 2, DNH])
        gbm, egls = tb("gbm", [P, NB, DNH]), tb("egls", [P, NB, DNH])
        wide = [P, 2, M4 * P]
        dm, egb, bt, qk, T, Y, Pm = [tb("w_" + x, wide) for x in ("dm", "egb", "bt", "qk", "T", "Y", "Pm")]
        gu, bi = Pm, T
        kb, vb, kg = tb("kb", [P, 512]), tb("vb", [P, 512]), tb("kg", [P, 512])
        wT, qgT = tb("wT", [P, M4, P]), tb("qgT", [P, M4, P])
        U, vf = tb("U", [P, 512]), tb("vf", [P, 512])
        S = tb("S", [P, M4, HD])
        Ss = tb("Ss", [P, NB, M4, HD])
        o = tb("o_dn", [P, 512])
        osq, oss = vb, tb("oss", [P, 2, DNH])
        dgs = tb("dgs", [P, 512])
        qgm = tb("qgm", [P, M4, NB * 72])
        xcf = m.xc[:, :, :].rearrange("p c n -> p (c n)")
        vm = xcf[:, 0:NB * 512].rearrange("p (b n) -> p b n", b=NB)
        wm = xcf[:, NB * 512:NB * 512 + M4 * NB * 72].rearrange("p (m n) -> p m n", m=M4)
        block = ctx.enter_context(nc.Block())
        sd = t["state_delta"][0]

        @block.sync
        def _(sp):
            sp.dma_start(arow[:, :], t["dn_a_log"][0].partition_broadcast(P)).then_inc(st_in, 16)
            sp.dma_start(dtrow[:, :], t["dn_dt_bias"][0].partition_broadcast(P)).then_inc(st_in, 16)
            sp.dma_start(grow[:, :], t["dn_norm_g"][0].partition_broadcast(P)).then_inc(st_in, 16)
            for e in range(2):
                sp.dma_start(Ss[e * HD:(e + 1) * HD].rearrange("p b m v -> p (b m) v"),
                             sd.rearrange("b (m e) k v -> e k (b m) v", e=2)[e]).then_inc(st_in, 16)
            sp.wait_ge(s_ok, 2 * PT)
            for e in range(2):
                sp.dma_start(outs[8][0, 0].rearrange("(m e) k v -> e k m v", e=2)[e], S[e * HD:(e + 1) * HD]).then_inc(sto, 16)
            sp.wait_ge(s_ok, 2 * PT + 2 * M4)
            for e in range(2):
                sp.dma_start(outs[16][0].rearrange("b (m e) k v -> e k (b m) v", e=2)[e],
                             Ss[e * HD:(e + 1) * HD].rearrange("p b m v -> p (b m) v")).then_inc(sto, 16)
            sp.wait_ge(sto, 64)

        @block.scalar
        def _(act):
            link = Chain(act, gates_a)
            act.wait_ge(st_in, 16 * 5)
            act.wait_ge(gch, 3)
            link(nc.scalar.activation(beta[:, :, :], m.z[:, :, Z_B:Z_B + DNH], ACT.Exp, scale=-1.0))
            link(nc.scalar.activation(sp2[:, :, :], sp2[:, :, :], ACT.Exp, scale=-1.0))
            link(nc.scalar.activation(arow[:, :], arow[:, :], ACT.Exp))
            link(nc.scalar.activation(sp2[:, :, :], sp2[:, :, :], ACT.Ln, bias=m.eps[:, 2:3]))
            for i in range(TILES):
                act.wait_ge(cum_ok, i + 1)
                nc.scalar.activation(ecum[:, :, :], cum[:, :, :], ACT.Exp).then_inc(eg_ok, 1)
                tot = egl if VAR[i] == 0 else egls
                nc.scalar.activation(tot[:, :, :], tot[:, :, :], ACT.Exp).then_inc(eg_ok, 1)
                act.wait_ge(gb_ps, i + 1)
                nc.scalar.activation(egb[:, :, :], PS[:, 0:2, :], ACT.Exp).then_inc(eg_ok, 1)
                act.wait_ge(d_in, i + 1)
                nc.scalar.activation(dm[:, :, :], dm[:, :, :], ACT.Exp).then_inc(d_exp, 1)
                act.wait_ge(o_ok, 2 * (i + 1) if VAR[i] == 0 else 2 * PT + 1)
                nc.scalar.activation(osq[:, :], o[:, :], ACT.Square).then_inc(o_ss, 1)
                nc.scalar.activation(dgs[:, :], m.z[:, i, Z_DG:Z_DG + 512], ACT.Exp, scale=-1.0).then_inc(o_ss, 1)
                act.wait_ge(o_rt, 2 * i + 1)
                nc.scalar.activation(oss[:, 1, :], oss[:, 0, :], ACT.Sqrt, scale=1.0 / HD, bias=m.eps[:, 0:1]).then_inc(o_rt, 1)

        @block.vector
        def _(dve):
            link = Chain(dve, chain)
            V = nc.vector
            al = m.z[:, :, Z_A:Z_A + DNH]
            dve.wait_ge(st_in, 16 * 5)
            link(V.tensor_tensor(sp_[:, :, :], al, dtrow[:, :].unsqueeze(1).to_broadcast([P, TILES, DNH]), ALU.add))
            V.tensor_scalar(sp2[:, :, :], sp_[:, :, :], -1.0, None, ALU.mult).then_inc(gch, 1)
            dve.wait_ge(gch, 1)
            V.tensor_tensor(sp2[:, :, :], sp2[:, :, :], sp_[:, :, :], ALU.max).then_inc(gch, 1)
            dve.wait_ge(gch, 2)
            V.tensor_scalar(sp_[:, :, :], sp_[:, :, :], 0.0, None, ALU.max).then_inc(gch, 1)
            dve.wait_ge(gates_a, 4)
            link(V.tensor_tensor(g[:, :, :], sp_[:, :, :], sp2[:, :, :], ALU.add))
            link(V.tensor_tensor(g[:, :, :], g[:, :, :], arow[:, :].unsqueeze(1).to_broadcast([P, TILES, DNH]), ALU.mult))
            link(V.tensor_scalar(g[:, :, :], g[:, :, :], -1.0, None, ALU.mult))
            link(V.memset(g[NB * TS:P, PT, :], 0.0))
            link(V.tensor_scalar(beta[:, :, :], beta[:, :, :], 1.0, None, ALU.add))
            link(V.reciprocal(beta[:, :, :], beta[:, :, :]))
            link(V.memset(S[:, :, :], 0.0))
            link(V.memset(wm[:, :, :], 0.0))
            link(V.memset(qgm[:, :, :], 0.0))
            V.tensor_tensor(gbm[:, :, :], m.bmask[:, :].unsqueeze(2).to_broadcast([P, NB, DNH]),
                            g[:, PT, :].unsqueeze(1).to_broadcast([P, NB, DNH]), ALU.mult).then_inc(mask_ok, 1)
            dve.wait_ge(mask_ok, 1)
            for i in range(TILES):
                v = VAR[i]
                for h in range(DNH):
                    e, mm = h % 2, h // 2
                    V.tensor_scalar(gu[:, e, mm * P:(mm + 1) * P], m.upinc[:, v, :], g[:, i, h:h + 1], None, ALU.mult)
                    last = V.tensor_scalar(bi[:, e, mm * P:(mm + 1) * P], m.ident[:, :], beta[:, i, h:h + 1], None, ALU.mult)
                last.then_inc(gb_rhs, 1)
                dve.wait_ge(cum_ps, i + 1)
                link(V.tensor_copy(cum[:, 0:2, :], PS[:, 6, 0:2 * DNH].rearrange("p (a h) -> p a h", a=2)))
                if v == 0:
                    link(V.tensor_copy(egl[:, :, :], PS[:, 6, 16:32].rearrange("p (c h) -> p c h", c=2)))
                else:
                    link(V.tensor_copy(egls[:, :, :], PS[:, 6, 16:16 + 64].rearrange("p (b h) -> p b h", b=NB)))
                V.tensor_tensor(cum[:, 2, :], cum[:, 1, :], cum[:, 0, :], ALU.subtract).then_inc(cum_ok, 1)
                dve.wait_ge(neg_ps, i + 1)
                for h in range(DNH):
                    e, mm = h % 2, h // 2
                    last = V.tensor_scalar(dm[:, e, mm * P:(mm + 1) * P], PS[:, e, mm * P:(mm + 1) * P], cum[:, 0, h:h + 1], 0.0, ALU.subtract, ALU.min)
                last.then_inc(d_in, 1)
                dve.wait_ge(eg_ok, 3 * i + 2)
                k3 = m.kvt[:, i, 0:512].rearrange("p (h d) -> p h d", d=HD)
                v3 = m.kvt[:, i, 512:1024].rearrange("p (h d) -> p h d", d=HD)
                bc = lambda a: a.unsqueeze(2).to_broadcast([P, DNH, HD])
                r3 = lambda a: a[:, :].rearrange("p (h d) -> p h d", d=HD)
                link(V.tensor_tensor(bcum[:, :], beta[:, i, :], ecum[:, 0, :], ALU.mult))
                link(V.tensor_tensor(r3(kb), k3, bc(bcum[:, :]), ALU.mult))
                link(V.tensor_tensor(r3(vb), v3, bc(beta[:, i, :]), ALU.mult))
                V.tensor_tensor(r3(kg), k3, bc(ecum[:, 2, :]), ALU.mult).then_inc(kb_ok, 1)
                dve.wait_ge(d_exp, i + 1)
                dve.wait_ge(kk_ps, i + 1)
                link(V.tensor_tensor(bt[:, :, :], PS[:, 4:6, :], dm[:, :, :], ALU.mult))
                V.tensor_tensor(bt[:, :, :], PS[:, 2:4, :], bt[:, :, :], ALU.mult).then_inc(bt_ok, 1)
                link(V.tensor_copy(T[:, :, :].rearrange("p e (m n) -> p (e m) n", n=P), m.ident[:, :].unsqueeze(1).to_broadcast([P, DNH, P])))
                V.tensor_copy(Y[:, :, :].rearrange("p e (m n) -> p (e m) n", n=P), m.ident[:, :].unsqueeze(1).to_broadcast([P, DNH, P])).then_inc(ty_ok, 1)
                dve.wait_ge(qk_ps, i + 1)
                V.tensor_tensor(qk[:, :, :], PS[:, 0:2, :], dm[:, :, :], ALU.mult).then_inc(qk_ok, 1)
                for h2 in range(2):
                    dve.wait_ge(eg_ok, 3 * i + 3)
                    rows = slice(h2 * HD, (h2 + 1) * HD)
                    link(V.tensor_tensor(qgT[rows, :, :], m.yT[rows, 0:M4, i * P:(i + 1) * P], egb[rows, h2, :].rearrange("p (m n) -> p m n", n=P), ALU.mult))
                    if v == 1:
                        link(V.tensor_copy(qgm[rows, :, :].rearrange("p m (b x) -> p m b x", x=72)[:, :, :, 0:TS],
                                           qgT[rows, :, 0:NB * TS].rearrange("p m (b j) -> p m b j", j=TS)))
                for l in range(LEVELS[i]):
                    n = sum(LEVELS[:i]) + l
                    for e in range(2):
                        dve.wait_ge(lp_ps, 2 * n + e + 1)
                        V.tensor_tensor(Pm[:, e, :].rearrange("p (m n) -> p m n", n=P), PS[:, 2 + e, :].rearrange("p (m n) -> p m n", n=P),
                                        m.level[:, l, :].unsqueeze(1).to_broadcast([P, M4, P]), ALU.mult).then_inc(lp_ok, 1)
                    for e in range(2):
                        dve.wait_ge(lt_ps, 2 * n + e + 1)
                        V.tensor_tensor(T[:, e, :], T[:, e, :], PS[:, 4 + e, :], ALU.subtract)
                        V.tensor_tensor(Y[:, e, :], Y[:, e, :], PS[:, 6 + e, :], ALU.subtract).then_inc(lt_ok, 1)
                dve.wait_ge(wu_ps, i + 1)
                for e in range(2):
                    rows = slice(e * HD, (e + 1) * HD)
                    src = PS[rows, e, :].rearrange("p (m n) -> p m n", n=P)
                    link(V.tensor_copy(wT[rows, :, :], src))
                    if v == 1:
                        link(V.tensor_copy(wm[rows, :, :].rearrange("p m (b x) -> p m b x", x=72)[:, :, :, 0:TS],
                                           src[:, :, 0:NB * TS].rearrange("p m (b j) -> p m b j", j=TS)))
                V.tensor_copy(U[:, :], PS[:, 2, :]).then_inc(wu_ok, 1)
                link(V.memset(vf[:, :], 0.0))
                if v == 0:
                    for c in range(2):
                        n = 2 * i + c
                        r = slice(c * HD, (c + 1) * HD)
                        dve.wait_ge(ws_ps, n + 1)
                        if c == 1:
                            link(V.memset(vf[0:HD, :], 0.0))
                        dve.wait_ge(wu_ok, i + 1)
                        V.tensor_tensor(vf[r, :].rearrange("p (e x) -> p e x", e=2), U[r, :].rearrange("p (e x) -> p e x", e=2),
                                        PS[r, 4:6, 0:256], ALU.subtract).then_inc(v_ok, 1)
                        for e in range(2):
                            rows = slice(e * HD, (e + 1) * HD)
                            dve.wait_ge(so_ps, n + 1)
                            link(V.tensor_tensor(S[rows], S[rows], egl[rows, c, e::2].unsqueeze(2).to_broadcast([HD, M4, HD]), ALU.mult))
                            ins = V.tensor_tensor(S[rows], S[rows], PS[rows, 3, :].rearrange("p (m x) -> p m x", x=P)[:, :, e * HD:(e + 1) * HD], ALU.add)
                            if e == 0:
                                link(ins)
                            else:
                                ins.then_inc(s_ok, 1)
                        V.tensor_copy(heads_em(o[r, :])[:, 0], PS[r, 6, 0:256].rearrange("p (m x) -> p m x", x=HD))
                        V.tensor_copy(heads_em(o[r, :])[:, 1], PS[r, 7, 0:256].rearrange("p (m x) -> p m x", x=HD)).then_inc(o_ok, 1)
                else:
                    dve.wait_ge(ws_ps, 2 * PT + 1)
                    dve.wait_ge(wu_ok, i + 1)
                    r = slice(0, NB * TS)
                    V.tensor_tensor(vf[r, :].rearrange("p (e x) -> p e x", e=2), U[r, :].rearrange("p (e x) -> p e x", e=2),
                                    PS[r, 4:6, 0:256], ALU.subtract).then_inc(v_ok, 1)
                    dve.wait_ge(v_ok, 2 * PT + 1)
                    V.tensor_tensor(vm[:, :, :], vf[:, :].unsqueeze(1).to_broadcast([P, NB, 512]),
                                    m.bmask[:, :].unsqueeze(2).to_broadcast([P, NB, 512]), ALU.mult).then_inc(vm_ok, 1)
                    dve.wait_ge(so_ps, 2 * PT + 1)
                    for e in range(2):
                        rows = slice(e * HD, (e + 1) * HD)
                        link(V.tensor_tensor(Ss[rows], Ss[rows], egls[rows, :, e::2].unsqueeze(3).to_broadcast([HD, NB, M4, HD]), ALU.mult))
                    for mm in range(M4):
                        dve.wait_ge(su_ps, mm + 1)
                        for e in range(2):
                            rows = slice(e * HD, (e + 1) * HD)
                            V.tensor_tensor(Ss[rows, :, mm, :], Ss[rows, :, mm, :],
                                            PS[rows, 2 * (mm % 2):2 * (mm % 2) + 2, :].rearrange("p a (b x) -> p (a b) x", x=P)[:, :, e * HD:(e + 1) * HD],
                                            ALU.add).then_inc(s_ok, 1)
                    link(V.memset(o[:, :], 0.0))
                    V.tensor_copy(heads_em(o[r, :])[:, 0], PS[r, 6, 0:256].rearrange("p (m x) -> p m x", x=HD))
                    V.tensor_copy(heads_em(o[r, :])[:, 1], PS[r, 7, 0:256].rearrange("p (m x) -> p m x", x=HD)).then_inc(o_ok, 1)
                o3 = o[:, :].rearrange("p (h d) -> p h d", d=HD)
                dve.wait_ge(o_ss, 2 * i + 2)
                link(V.tensor_scalar(dgs[:, :], dgs[:, :], 1.0, None, ALU.add))
                link(V.reciprocal(dgs[:, :], dgs[:, :]))
                link(V.tensor_tensor(dgs[:, :], dgs[:, :], m.z[:, i, Z_DG:Z_DG + 512], ALU.mult))
                V.reduce_sum(oss[:, 0, :], osq[:, :].rearrange("p (h d) -> p h d", d=HD), AX).then_inc(o_rt, 1)
                dve.wait_ge(o_rt, 2 * i + 2)
                link(V.reciprocal(oss[:, 1, :], oss[:, 1, :]))
                link(V.tensor_tensor(o3, o3, bc(oss[:, 1, :]), ALU.mult))
                link(V.tensor_tensor(o3, o3, grow[:, :].unsqueeze(1).to_broadcast([P, DNH, HD]), ALU.mult))
                V.tensor_tensor(o[:, :], o[:, :], dgs[:, :], ALU.mult).then_inc(o_fin, 1)
                dve.wait_ge(o_ps, i + 1)
                w = ROWS[i]
                V.tensor_copy(m.mixT[:, M4:2 * M4, i * P:i * P + w], PS[:, 0, :].rearrange("p (c n) -> p c n", n=P)[:, :, 0:w]).then_inc(o_T, 1)

        @block.tensor
        def _(pe):
            MM = nc.tensor.matmul
            col = lambda mm: slice(mm * P, (mm + 1) * P)
            pe.wait_ge(mask_ok, 1)
            for i in range(TILES):
                v = VAR[i]
                tok = slice(i * P, (i + 1) * P)
                if i:
                    pe.wait_ge(o_T, i)
                MM(PS[:, 6, 0:DNH], m.upinc[:, v, :], g[:, i, :], start=True, stop=True)
                last = MM(PS[:, 6, DNH:2 * DNH], m.same[:, v, :], g[:, i, :], start=True, stop=True)
                if v == 0:
                    for c in range(2):
                        last = MM(PS[:, 6, 16 + 8 * c:24 + 8 * c], m.chunk[:, c, :], g[:, i, :], start=True, stop=True)
                else:
                    last = MM(PS[:, 6, 16:80], m.ones[:, :], gbm[:, :, :].rearrange("p b h -> p (b h)"), start=True, stop=True)
                last.then_inc(cum_ps, 1)
                pe.wait_ge(gb_rhs, i + 1)
                for e in range(2):
                    last = MM(PS[:, e, :], m.ones[:, :], gu[:, e, :], start=True, stop=False, skip_group_check=True)
                last.then_inc(gb_ps, 1)
                for e in range(2):
                    MM(PS[:, 4 + e, :], m.ones[:, :], bi[:, e, :], start=True, stop=True)
                for h in range(DNH):
                    e, mm = h % 2, h // 2
                    rows = slice(e * HD, (e + 1) * HD)
                    kT = m.yT[rows, M4 + mm, tok]
                    last = MM(PS[:, 2 + e, col(mm)], kT, kT, start=True, stop=True)
                last.then_inc(kk_ps, 1)
                pe.wait_ge(eg_ok, 3 * i + 3)
                for e in range(2):
                    for mm in range(M4):
                        last = MM(PS[:, e, col(mm)], m.ident[:, :], m.upneg[:, v, :], start=False, stop=(mm == M4 - 1), skip_group_check=True)
                last.then_inc(neg_ps, 1)
                pe.wait_ge(d_in, i + 1)
                for h in range(DNH):
                    e, mm = h % 2, h // 2
                    rows = slice(e * HD, (e + 1) * HD)
                    last = MM(PS[:, e, col(mm)], m.yT[rows, M4 + mm, tok], m.yT[rows, mm, tok], start=True, stop=True)
                last.then_inc(qk_ps, 1)
                pe.wait_ge(bt_ok, i + 1)
                pe.wait_ge(ty_ok, i + 1)
                for l in range(LEVELS[i]):
                    n = sum(LEVELS[:i]) + l
                    for e in range(2):
                        if l:
                            pe.wait_ge(lt_ok, 2 * n - 1 + e)
                        for mm in range(M4):
                            last = MM(PS[:, 2 + e, col(mm)], bt[:, e, col(mm)], T[:, e, col(mm)], start=True, stop=True)
                        last.then_inc(lp_ps, 1)
                    for e in range(2):
                        pe.wait_ge(lp_ok, 2 * n + e + 1)
                        for mm in range(M4):
                            MM(PS[:, 4 + e, col(mm)], Y[:, e, col(mm)], Pm[:, e, col(mm)], start=True, stop=True)
                            last = MM(PS[:, 6 + e, col(mm)], Pm[:, e, col(mm)], Y[:, e, col(mm)], start=True, stop=True)
                        last.then_inc(lt_ps, 1)
                pe.wait_ge(lt_ok, 2 * sum(LEVELS[:i + 1]))
                pe.wait_ge(kb_ok, i + 1)
                pe.wait_ge(qk_ok, i + 1)
                for h in range(DNH):
                    e, mm = h % 2, h // 2
                    MM(PS[:, e, col(mm)], kb[:, mm * P:(mm + 1) * P], Y[:, e, col(mm)], start=True, stop=True)
                    last = MM(PS[:, 2, (e * M4 + mm) * HD:(e * M4 + mm + 1) * HD], Y[:, e, col(mm)], vb[:, h * HD:(h + 1) * HD], start=True, stop=True)
                last.then_inc(wu_ps, 1)
                pe.wait_ge(wu_ok, i + 1)
                if v == 0:
                    for c in range(2):
                        n = 2 * i + c
                        if n:
                            pe.wait_ge(s_ok, n)
                        if c == 1:
                            pe.wait_ge(o_ok, n)
                        for h in range(DNH):
                            e, mm = h % 2, h // 2
                            rows = slice(e * HD, (e + 1) * HD)
                            last = MM(PS[:, 4 + e, mm * HD:(mm + 1) * HD], wT[rows, mm, :], S[rows, mm, :], start=True, stop=True)
                        last.then_inc(ws_ps, 1)
                        pe.wait_ge(v_ok, n + 1)
                        for mm in range(M4):
                            last = MM(PS[:, 3, col(mm)], kg[:, col(mm)], vf[:, :].rearrange("p (e m x) -> p m e x", e=2, m=M4)[:, mm], start=True, stop=True)
                        for h in range(DNH):
                            e, mm = h % 2, h // 2
                            rows = slice(e * HD, (e + 1) * HD)
                            dst = PS[:, 6 + e, mm * HD:(mm + 1) * HD]
                            MM(dst, qgT[rows, mm, :], S[rows, mm, :], start=True, stop=False)
                            last = MM(dst, qk[:, e, col(mm)], vf[:, (e * M4 + mm) * HD:(e * M4 + mm + 1) * HD], start=False, stop=True)
                        last.then_inc(so_ps, 1)
                else:
                    R = NB * TS
                    for h in range(DNH):
                        e, mm = h % 2, h // 2
                        rows = slice(e * HD, (e + 1) * HD)
                        for b in range(NB):
                            last = MM(PS[0:R, 4 + e, mm * HD:(mm + 1) * HD], wm[rows, mm, b * R:(b + 1) * R], Ss[rows, b, mm, :], start=(b == 0), stop=(b == NB - 1))
                    last.then_inc(ws_ps, 1)
                    pe.wait_ge(v_ok, 2 * PT + 1)
                    for h in range(DNH):
                        e, mm = h % 2, h // 2
                        rows = slice(e * HD, (e + 1) * HD)
                        dst = PS[0:R, 6 + e, mm * HD:(mm + 1) * HD]
                        for b in range(NB):
                            MM(dst, qgm[rows, mm, b * R:(b + 1) * R], Ss[rows, b, mm, :], start=(b == 0), stop=False)
                        last = MM(dst, qk[:, e, mm * P:mm * P + R], vf[:, (e * M4 + mm) * HD:(e * M4 + mm + 1) * HD], start=False, stop=True)
                    last.then_inc(so_ps, 1)
                    pe.wait_ge(vm_ok, 1)
                    for mm in range(M4):
                        if mm >= 2:
                            pe.wait_ge(s_ok, 2 * PT + 2 * (mm - 1))
                        for half in range(2):
                            last = MM(PS[:, 2 * (mm % 2) + half, :], kg[:, col(mm)],
                                      vm[:, 4 * half:4 * half + 4, :].rearrange("p b (e m x) -> p m b e x", e=2, m=M4)[:, mm], start=True, stop=True)
                        last.then_inc(su_ps, 1)
                pe.wait_ge(o_fin, i + 1)
                for c in range(M4):
                    last = nc.tensor.transpose(PS[:, 0, col(c)], o[:, col(c)], m.ident[:, :])
                last.then_inc(o_ps, 1)


NHC = CMP_HIDDEN // P
LP = CMP_LEN // 2
NPAIR = LS // 2
NCOL = NSEQ * NCMP


def load_pages(nc, eng, pt_sb, done, moves):
    with nc.Fori(0, NB, engines=[eng.engine]) as b:
        for pg in range(PAGES):
            page = eng.value_load(pt_sb[0:1, bass.ds(b * PAGES + pg, 1)], min_val=0, max_val=NPOOL - 1)
            for dst, src in moves(b, pg, page):
                eng.dma_start(dst, src).then_inc(done, 16)


def stage_compress(nc, m, sb, sem, t, outs):
    PS = m.PS
    pt_in, raw_in, new_in, w_in = sem("c_pt_in"), sem("c_raw_in"), sem("c_new_in"), sem("c_w_in")
    pos_ps, pos_ok, tr_ps, tr_a, tr_v = sem("pos_ps"), sem("pos_ok"), sem("tr_ps"), sem("tr_a"), sem("tr_v")
    hid_ps, hb_ok, hid_ok, out_ps, out_ok = sem("hid_ps"), sem("hb_ok"), sem("hid_ok"), sem("out_ps"), sem("out_ok")
    with ExitStack() as ctx:
        def tb(name, shape, dt=F32):
            return ctx.enter_context(nc.sbuf_tensor(name, shape, dt))
        pt = tb("pt", [1, NB * PAGES], I32)
        raw = tb("raw", [P, 2, NB * 2, 2 * P])
        rawp = tb("rawp", [P, 2, 2, 2 * P])
        rawn = tb("rawn", [NB * TS // 2, 2, 2 * P])
        xT = tb("xT", [P, 2, NSEQ, NPAIR])
        w1 = tb("w1", [P, LP, CMP_HIDDEN])
        w1v = tb("w1v", [P, LP, CMP_HIDDEN])
        w2 = tb("w2", [P, NHC, 2 * HD])
        w2v = tb("w2v", [P, NHC, HD])
        pos = tb("cmp_pos", [LP, 2, P])
        posT = tb("posT", [P, 2, LP])
        hb = tb("hb", [P, 2, NHC])
        hid = tb("hid", [P, 2, KV, NHC, NCOL])
        W1 = (w1, w1v)
        block = ctx.enter_context(nc.Block())
        pools = [t["cache_cmp_k"], t["cache_cmp_v"]]

        @block.sync
        def _(sp):
            sp.dma_start(pt[:, :], t["page_table"].rearrange("b p -> (b p)").unsqueeze(0)).then_inc(pt_in, 16)
            for s in range(2):
                sp.dma_start(W1[s][:, :, :], t["cmp_w1_k" if s == 0 else "cmp_w1_v"][0].rearrange("(l p) n -> p l n", p=P)).then_inc(w_in, 16)
                sp.dma_start(pos[:, s, :], t["cmp_pos_k" if s == 0 else "cmp_pos_v"][0].rearrange("(l e) d -> l (e d)", e=2)).then_inc(w_in, 16)
            w2k = t["cmp_w2_k"][0].rearrange("(c p) d -> p c d", p=P)
            sp.dma_start(w2[:, :, 0:HD], w2k).then_inc(w_in, 16)
            sp.dma_start(w2[:, :, HD:2 * HD], w2k).then_inc(w_in, 16)
            sp.dma_start(w2v[:, :, :], t["cmp_w2_v"][0].rearrange("(c p) d -> p c d", p=P)).then_inc(w_in, 16)
            sp.wait_ge(pt_in, 16)

            def moves(b, pg, page):
                for s in range(2):
                    for v in range(KV):
                        src = pools[s][0, bass.ds(page, 1), :, v, :].rearrange("o (q e) d -> q (o e) d", e=2)
                        dst = raw[(pg % 2) * HD:(pg % 2 + 1) * HD, s, bass.ds(b * 2 + pg // 2, 1), v * P:(v + 1) * P]
                        yield dst.rearrange("p o (e d) -> p (o e) d", e=2), src

            load_pages(nc, sp, pt, raw_in, moves)

        @block.gpsimd
        def _(pool):
            for s in range(2):
                for v in range(KV):
                    for j in range(2):
                        pool.dma_start(rawp[:, s, j, v * P:(v + 1) * P].rearrange("p (e d) -> p e d", e=2),
                                       outs[2 + s][0, 0, j * 2 * P:(j + 1) * 2 * P, v, :].rearrange("(q e) d -> q e d", e=2)).then_inc(new_in, 16)
                    pool.dma_start(rawn[:, s, v * P:(v + 1) * P].rearrange("p (e d) -> p e d", e=2),
                                   outs[10 + s][0, :, :, v, :].rearrange("b s d -> (b s) d").rearrange("(q e) d -> q e d", e=2)).then_inc(new_in, 16)
            pool.wait_ge(new_in, 16 * 12)

        tunits = [(v, q) for v in range(KV) for q in range(NB // 2 + 2)]
        NU = len(tunits)

        def evacuate(copy, s, n, done):
            v, q = tunits[n]
            bank = PS[:, n % 4, :]
            if q < NB // 2:
                copy(xT[:, v, 1 + 2 * q:3 + 2 * q, 0:PAST // 2], bank.rearrange("p (b n) -> p b n", b=2)).then_inc(done, 1)
            elif q == NB // 2:
                copy(xT[:, v, 0, 0:SEQ // 2], bank[:, 0:SEQ // 2]).then_inc(done, 1)
            else:
                copy(xT[:, v, 1:, PAST // 2:], bank[:, 0:NB * TS // 2].rearrange("p (b n) -> p b n", b=NB)).then_inc(done, 1)

        @block.tensor
        def _(pe):
            MM = nc.tensor.matmul
            pe.wait_ge(w_in, 16 * 7)
            for s in range(2):
                last = nc.tensor.transpose(PS[:, 7, s * LP:(s + 1) * LP], pos[:, s, :], m.ident[0:LP, 0:LP])
            last.then_inc(pos_ps, 1)
            pe.wait_ge(pos_ok, 1)
            for s in range(2):
                for c in range(NHC):
                    for l in range(LP):
                        last = MM(PS[:, 6, s * NHC + c:s * NHC + c + 1], W1[s][:, l, c * P:(c + 1) * P], posT[:, s, l:l + 1], start=(l == 0), stop=(l == LP - 1))
            last.then_inc(pos_ps, 1)
            pe.wait_ge(new_in, 16 * 12)
            pe.wait_ge(raw_in, 16 * NB * PAGES * 4)
            for s in range(2):
                for n, (v, q) in enumerate(tunits):
                    if n >= 4 or s:
                        prev = s * NU + n - 4
                        pe.wait_ge(tr_v if prev % 2 else tr_a, prev // 2 + 1)
                    if q < NB // 2:
                        for j in range(4):
                            last = nc.tensor.transpose(PS[:, n % 4, j * P:(j + 1) * P], raw[:, s, 4 * q + j, v * P:(v + 1) * P], m.ident[:, :])
                    elif q == NB // 2:
                        for j in range(2):
                            last = nc.tensor.transpose(PS[:, n % 4, j * P:(j + 1) * P], rawp[:, s, j, v * P:(v + 1) * P], m.ident[:, :])
                    else:
                        r = NB * TS // 2
                        last = nc.tensor.transpose(PS[:, n % 4, 0:r], rawn[:, s, v * P:(v + 1) * P], m.ident[0:r, 0:r])
                    last.then_inc(tr_ps, 1)
                pe.wait_ge(tr_v, (s + 1) * NU // 2)
                pe.wait_ge(tr_a, (s + 1) * NU // 2)
                for v in range(KV):
                    for c in range(NHC):
                        u = (s * KV + v) * NHC + c
                        if u >= 2:
                            pe.wait_ge(hid_ok, u - 1)
                        for l in range(LP):
                            last = MM(PS[:, 4 + u % 2, 0:NCOL], W1[s][:, l, c * P:(c + 1) * P],
                                      xT[:, v, :, l:l + (CMP_STRIDE // 2) * (NCMP - 1) + 1:CMP_STRIDE // 2], start=(l == 0), stop=(l == LP - 1))
                        last.then_inc(hid_ps, 1)
            pe.wait_ge(hid_ok, 2 * KV * NHC)
            pe.wait_ge(tr_v, NU)
            pe.wait_ge(tr_a, NU)
            for v in range(KV):
                for c in range(NHC):
                    last = MM(PS[:, v, 0:NCOL], w2[:, c, :], hid[:, 0, v, c, :], start=(c == 0), stop=(c == NHC - 1))
            for q in range(NSEQ):
                for v in range(KV):
                    for c in range(NHC):
                        last = MM(PS[0:NCMP, 2 + q // 4, (q % 4) * P + v * HD:(q % 4) * P + (v + 1) * HD], hid[:, 1, v, c, q * NCMP:(q + 1) * NCMP], w2v[:, c, :],
                                  start=(c == 0), stop=(c == NHC - 1))
            last.then_inc(out_ps, 1)

        @block.scalar
        def _(act):
            for s in range(2):
                for n in range(0, NU, 2):
                    act.wait_ge(tr_ps, s * NU + n + 1)
                    if s == 1 and n == 0:
                        act.wait_ge(hid_ps, KV * NHC)
                    evacuate(nc.scalar.copy, s, n, tr_a)
                if s == 0:
                    act.wait_ge(hb_ok, 1)
                for v in range(KV):
                    for c in range(NHC):
                        u = (s * KV + v) * NHC + c
                        act.wait_ge(hid_ps, u + 1)
                        nc.scalar.activation(hid[:, s, v, c, :], PS[:, 4 + u % 2, 0:NCOL], ACT.Silu, bias=hb[:, s, c:c + 1]).then_inc(hid_ok, 1)

        @block.vector
        def _(dve):
            dve.wait_ge(pos_ps, 1)
            nc.vector.tensor_copy(posT[:, :, :], PS[:, 7, 0:2 * LP].rearrange("p (s l) -> p s l", s=2)).then_inc(pos_ok, 1)
            dve.wait_ge(pos_ps, 2)
            nc.vector.tensor_copy(hb[:, :, :], PS[:, 6, 0:2 * NHC].rearrange("p (s c) -> p s c", s=2)).then_inc(hb_ok, 1)
            for s in range(2):
                for n in range(1, NU, 2):
                    dve.wait_ge(tr_ps, s * NU + n + 1)
                    if s == 1 and n == 1:
                        dve.wait_ge(hid_ps, KV * NHC)
                    evacuate(nc.vector.tensor_copy, s, n, tr_v)
            dve.wait_ge(out_ps, 1)
            for v in range(KV):
                nc.vector.tensor_copy(m.kcT[v * HD:(v + 1) * HD, :], PS[v * HD:(v + 1) * HD, v, 0:NCOL])
            nc.vector.tensor_copy(m.vc[:, :, :], PS[0:NCMP, 2:5, :].rearrange("p a (q n) -> p (a q) n", n=P)[:, 0:NSEQ, :]).then_inc(out_ok, 1)


def stage_keys(nc, m, sb, sem, t, outs):
    PS = m.PS
    pt_in, sel_in, win_in, bias_in = sem("k_pt_in"), sem("sel_in"), sem("win_in"), sem("bias_in2")
    k_ps, k_a, k_v = sem("k_ps"), sem("k_a"), sem("k_v")
    with ExitStack() as ctx:
        pt = ctx.enter_context(nc.sbuf_tensor("pt2", [1, NB * PAGES], I32))
        kraw = ctx.enter_context(nc.sbuf_tensor("kraw", [P, 2, NB * PAGES, P], F32))
        block = ctx.enter_context(nc.Block())
        pools = [t["cache_sel_k"], t["cache_sel_v"]]
        units = [(br, q) for br in range(2) for q in range(NSEQ + 1)]

        @block.sync
        def _(sp):
            sp.dma_start(pt[:, :], t["page_table"].rearrange("b p -> (b p)").unsqueeze(0)).then_inc(pt_in, 16)
            for s, name in enumerate(("cache_win_k", "cache_win_v")):
                dst = kraw[:, 1] if s == 0 else m.V[:, 1]
                sp.dma_start(dst, t[name][0].rearrange("b (g p) k d -> p (b g) (k d)", p=P)).then_inc(win_in, 16)
            sp.wait_ge(pt_in, 16)

            def moves(b, pg, page):
                for s in range(2):
                    dst = (kraw[:, 0] if s == 0 else m.V[:, 0])[:, bass.ds(b * PAGES + pg, 1), :].rearrange("p o n -> p (o n)")
                    yield dst, pools[s][0, bass.ds(page, 1)].rearrange("o p k d -> (o p) (k d)")

            load_pages(nc, sp, pt, sel_in, moves)
            sp.dma_start(m.Vn[:, 0], outs[13][0].rearrange("b s k d -> s b (k d)")).then_inc(win_in, 16)
            sp.dma_start(m.Vn[:, 1], outs[15][0, :, PAST - TS:PAST].rearrange("b s k d -> s b (k d)")).then_inc(win_in, 16)
            sp.dma_start(m.strip[:, :, :], bass.AP(m.rb_rep, RB_C - (SEQ - P), [[H * RB_W - 1, P], [RB_W, H], [1, STRIP]])).then_inc(bias_in, 16)
            for r in range(2):
                for v in range(2):
                    for h in range(H):
                        sp.dma_start(m.biasS[64 * r + TS * h:64 * r + TS * h + TS, v, :],
                                     bass.AP(m.rb_rep, v * P * H * RB_W + h * RB_W + RB_C - PAST, [[H * RB_W - 1, TS], [1, LS]])).then_inc(bias_in, 16)
            sp.wait_ge(sel_in, 16 * NB * PAGES * 2)
            sp.wait_ge(win_in, 64)
            sp.wait_ge(bias_in, 16 * 33)

        def evacuate(copy, n, done):
            br, q = units[n]
            bank = PS[:, n % 6, :]
            if q < NSEQ:
                copy(m.KT[:, br, q, 0:512], bank).then_inc(done, 1)
            else:
                copy(m.KT[:, br, 1:, PAST:], bank[:, 0:NB * TS].rearrange("p (b j) -> p b j", j=TS)).then_inc(done, 1)

        @block.tensor
        def _(pe):
            for n, (br, q) in enumerate(units):
                zc = 256 if br == 0 else 512
                if n >= 6:
                    pe.wait_ge(k_v if (n - 6) % 2 else k_a, (n - 6) // 2 + 1)
                if q == 1:
                    if br == 0:
                        pe.wait_ge(sel_in, 16 * NB * PAGES * 2)
                    else:
                        pe.wait_ge(win_in, 64)
                if q == NSEQ:
                    last = nc.tensor.transpose(PS[:, n % 6, 0:NB * TS], m.z[0:NB * TS, PT, zc:zc + P], m.ident[0:NB * TS, 0:NB * TS])
                else:
                    for j in range(4):
                        src = m.z[:, j, zc:zc + P] if q == 0 else kraw[:, br, (q - 1) * PAGES + j, :]
                        last = nc.tensor.transpose(PS[:, n % 6, j * P:(j + 1) * P], src, m.ident[:, :])
                last.then_inc(k_ps, 1)

        @block.scalar
        def _(act):
            for n in range(0, len(units), 2):
                act.wait_ge(k_ps, n + 1)
                evacuate(nc.scalar.copy, n, k_a)

        @block.vector
        def _(dve):
            for n in range(1, len(units), 2):
                dve.wait_ge(k_ps, n + 1)
                evacuate(nc.vector.tensor_copy, n, k_v)


def stage_attention(nc, m, sb, sem, t, outs):
    PS = m.PS
    gate_out, gate_in, sg, qs_ok = sem("a_gate_out"), sem("a_gate_in"), sem("a_sg"), sem("a_qs_ok")
    s_ps, s_ok, mx_ok, e_ok, pt_ps, pt_a = [sem("a_" + x) for x in ("s_ps", "s_ok", "mx_ok", "e_ok", "pt_ps", "pt_a")]
    o_ps, o_ok, chain, pn_ok = [sem("a_" + x) for x in ("o_ps", "o_ok", "chain", "pn_ok")]
    CMP, SEL, WIN = 0, 1, 2
    units = [("p", br, v, i) for i in range(PT) for v in range(KV) for br in range(3)] + [("s", br, q, 0) for q in range(NB // 2) for br in range(3)]
    NPU = PT * KV * 3
    keys = []
    for kind, br, a, i in units:
        if br == CMP:
            keys.append([NCMP])
        elif kind == "p":
            keys.append([P] * (i + 1))
        else:
            keys.append([P] * 4 + [TS])
    ends = lambda u: units[u][1] == WIN and (units[u][0] == "s" or units[u][2] == KV - 1)
    pieces = []
    for s in range(len(units) + 2):
        if s >= 2 and ends(s - 2):
            pieces.append(("o", s - 2))
        if 1 <= s <= len(units):
            u = s - 1
            groups = [[j] for j in range(len(keys[u]))] if units[u][0] == "p" else [list(range(len(keys[u])))[:4], list(range(len(keys[u])))[4:]]
            pieces += [("k", u, g) for g in groups if g]
    of = lambda kind, u: [n for n, p in enumerate(pieces) if p[0] == kind and p[1] == u]

    with ExitStack() as ctx:
        def tb(name, shape):
            return ctx.enter_context(nc.sbuf_tensor(name, shape, F32))
        gate = tb("gate", [P, TILES, 24])
        gateS = tb("gateS", [P, NB // 2, 3])
        Qs = tb("Qs", [P, NB, P])
        pr = tb("pr", [P, 2, 4 * 512])
        pT = tb("pT", [P, 5, 4 * P])
        mx, l, gr = tb("mx", [P, 2, 4]), tb("l", [P, 2, 4]), tb("gr", [P, 4])
        o, tmp = tb("o_att", [P, 2, 512]), tb("o_tmp", [P, 256])
        oS = tb("oS", [NB * TS, 2, 2, HD])
        block = ctx.enter_context(nc.Block())

        @block.sync
        def _(sp):
            sp.wait_ge(sg, 3)
            sp.dma_start(m.gate_dram.ap(), gate[0:NB * TS, PT, :]).then_inc(gate_out, 16)
            sp.wait_ge(gate_out, 16)
            for r in range(2):
                for h in range(H):
                    sp.dma_start(gateS[64 * r + TS * h:64 * r + TS * h + TS, :, :],
                                 m.gate_dram.ap().rearrange("(q r t) (h c) -> r h t q c", r=2, t=TS, c=3)[r, h]).then_inc(gate_in, 16)

        @block.scalar
        def _(act):
            gates = Chain(act, sg)
            gates(nc.scalar.activation(gate[:, :, :], m.z[:, :, Z_GL:Z_GL + 24], ACT.Exp, scale=-1.0))

            def softmax(u):
                kind, br, a, i = units[u]
                w = sum(keys[u])
                act.wait_ge(mx_ok, u + 1)
                if u >= 2:
                    act.wait_ge(pt_ps, of("k", u - 2)[-1] + 1)
                if kind == "p":
                    for g in range(G):
                        row = pr[:, u % 2, g * 512:g * 512 + w]
                        ins = nc.scalar.activation(row, row, ACT.Exp, bias=mx[:, u % 2, g:g + 1], accum_out=l[:, u % 2, g:g + 1])
                else:
                    row = pr[:, u % 2, 0:w]
                    ins = nc.scalar.activation(row, row, ACT.Exp, bias=mx[:, u % 2, 0:1], accum_out=l[:, u % 2, 0:1])
                ins.then_inc(e_ok, 1)

            def take_pieces(u):
                for n in of("k", u):
                    group = pieces[n][2]
                    kw = keys[u][group[0]]
                    act.wait_ge(pt_ps, n + 1)
                    if u:
                        act.wait_ge(o_ps, u)
                    if units[u][0] == "p":
                        nc.scalar.copy(pT[0:kw, group[0], :], PS[0:kw, 4 + n % 2, :]).then_inc(pt_a, 1)
                    else:
                        nc.scalar.copy(pT[0:kw, group[0]:group[-1] + 1, 0:P], PS[0:kw, 4 + n % 2, 0:len(group) * P].rearrange("p (j n) -> p j n", n=P)).then_inc(pt_a, 1)

            def take_outputs(u):
                kind, br, a, i = units[u]
                n = of("o", u)[0]
                act.wait_ge(pt_ps, n + 1)
                if kind == "p":
                    nc.scalar.copy(m.mixT[:, 0:4, i * P:(i + 1) * P], PS[:, 4 + n % 2, :].rearrange("p (c n) -> p c n", n=P)).then_inc(pt_a, 1)
                else:
                    for e in range(2):
                        rows = slice(e * HD, (e + 1) * HD)
                        last = nc.scalar.copy(m.mixT[rows, 0:4, SEQ + 2 * a * TS:SEQ + 2 * (a + 1) * TS].rearrange("p m (b t) -> p b m t", b=2),
                                              PS[rows, 4 + n % 2, 0:2 * NB * TS].rearrange("p (b m e t) -> p e b m t", b=2, e=2, t=TS)[:, e])
                    last.then_inc(pt_a, 1)

            for s in range(len(units) + 2):
                if s >= 2 and ends(s - 2):
                    take_outputs(s - 2)
                if 1 <= s <= len(units):
                    take_pieces(s - 1)
                if s < len(units):
                    softmax(s)

        @block.vector
        def _(dve):
            V = nc.vector
            link = Chain(dve, chain)
            link(V.memset(Qs[:, :, :], 0.0))
            for v in range(KV):
                rows = slice(v * HD, (v + 1) * HD)
                for r in range(2):
                    base = r * 64 + v * G * TS
                    src = m.qT[rows, :, SEQ:].rearrange("p g (q r t) -> p r q g t", r=2, t=TS)[:, r]
                    for q in range(NB // 2):
                        last = V.tensor_copy(Qs[rows, 2 * q + r, base:base + G * TS].rearrange("p (g t) -> p g t", g=G), src[:, q])
            last.then_inc(qs_ok, 1)
            dve.wait_ge(sg, 1)
            V.tensor_scalar(gate[:, :, :], gate[:, :, :], 1.0, None, ALU.add).then_inc(sg, 1)
            dve.wait_ge(sg, 2)
            V.reciprocal(gate[:, :, :], gate[:, :, :]).then_inc(sg, 1)
            dve.wait_ge(sg, 3)

            def scores(u):
                kind, br, a, i = units[u]
                w = sum(keys[u])
                dve.wait_ge(s_ps, u + 1)
                if u >= 2:
                    dve.wait_ge(pt_ps, of("k", u - 2)[-1] + 1)
                if kind == "p":
                    dst = pr[:, u % 2, :].rearrange("p (g n) -> p g n", g=G)[:, :, 0:w]
                    c = SEQ - P - i * P
                    b = m.strip[:, a * G:(a + 1) * G, c:c + w] if br != CMP else \
                        m.strip[:, a * G:(a + 1) * G, c + CMP_LEN - 1:c + CMP_LEN + CMP_STRIDE * (NCMP - 1):CMP_STRIDE]
                    V.scalar_tensor_tensor(out=dst, in0=PS[:, 0:4, 0:w], scalar=SCALE, in1=b, op0=ALU.mult, op1=ALU.add).then_inc(s_ok, 1)
                    dve.wait_ge(s_ok, u + 1)
                    link(V.tensor_reduce(mx[:, u % 2, :], dst, AX, ALU.max))
                    V.tensor_scalar(mx[:, u % 2, :], mx[:, u % 2, :], -1.0, None, ALU.mult).then_inc(mx_ok, 1)
                else:
                    dst = pr[:, u % 2, 0:w]
                    src = PS[:, 2 * (u % 2):2 * (u % 2) + 2, :].rearrange("p b n -> p (b n)")[:, 0:w]
                    b = m.biasS[:, 1 if br == WIN else 0, 0:w] if br != CMP else \
                        m.biasS[:, 0, CMP_LEN - 1:CMP_LEN + CMP_STRIDE * (NCMP - 1):CMP_STRIDE]
                    V.scalar_tensor_tensor(out=dst, in0=src, scalar=SCALE, in1=b, op0=ALU.mult, op1=ALU.add).then_inc(s_ok, 1)
                    dve.wait_ge(s_ok, u + 1)
                    link(V.tensor_reduce(mx[:, u % 2, 0:1], dst, AX, ALU.max))
                    V.tensor_scalar(mx[:, u % 2, 0:1], mx[:, u % 2, 0:1], -1.0, None, ALU.mult).then_inc(mx_ok, 1)

            def normalise_sample(u):
                kind, br, q, _ = units[u]
                dve.wait_ge(e_ok, u + 1)
                if u == NPU:
                    dve.wait_ge(gate_in, 16 * 2 * H)
                w = sum(keys[u])
                link(V.reciprocal(gr[:, 0:1], l[:, u % 2, 0:1]))
                link(V.tensor_tensor(gr[:, 1:2], gr[:, 0:1], gateS[:, q, br:br + 1], ALU.mult))
                V.tensor_scalar(pr[:, u % 2, 0:w], pr[:, u % 2, 0:w], gr[:, 1:2], None, ALU.mult).then_inc(pn_ok, 1)

            def outputs(u):
                kind, br, a, i = units[u]
                if kind == "p":
                    dve.wait_ge(e_ok, u + 1)
                    link(V.reciprocal(gr[:, :], l[:, u % 2, :]))
                    gt = gate[:, i, :].rearrange("p (h c) -> p h c", c=3)[:, a * G:(a + 1) * G, br]
                    link(V.tensor_tensor(gr[:, :], gr[:, :], gt, ALU.mult))
                    if br == CMP and i == 0:
                        link(V.tensor_scalar(gr[:, :], gr[:, :], m.seen[:, 0:1], None, ALU.mult))
                    dve.wait_ge(o_ps, u + 1)
                    if br == CMP and i >= 2:
                        dve.wait_ge(pt_ps, of("o", u - 2 * 3 * KV + (KV - 1 - a) * 3 + WIN)[0] + 1)
                    oo = o[:, i % 2, a * 256:(a + 1) * 256].rearrange("p (g d) -> p g d", g=G)
                    src = PS[:, 6 + u % 2, 0:256].rearrange("p (g d) -> p g d", g=G)
                    bc = gr[:, :].unsqueeze(2).to_broadcast([P, G, HD])
                    if br == CMP:
                        link_or(V.tensor_tensor(oo, src, bc, ALU.mult), False)
                    else:
                        tt = tmp[:, :].rearrange("p (g d) -> p g d", g=G)
                        link(V.tensor_tensor(tt, src, bc, ALU.mult))
                        link_or(V.tensor_tensor(oo, oo, tt, ALU.add), br == WIN and a == KV - 1)
                elif br == WIN:
                    dve.wait_ge(o_ps, u + 1)
                    if a:
                        dve.wait_ge(pt_ps, of("o", u - 3)[0] + 1)
                    b0 = PS[0:NB * TS, 6 + a % 2, 0:256].rearrange("p (b k d) -> p b k d", b=2, k=KV)
                    for v in range(KV):
                        rows = slice(v * G * TS, (v + 1) * G * TS)
                        for dup in range(2):
                            last = V.tensor_copy(oS[rows, :, dup, :], b0[rows, :, v, :])
                    last.then_inc(o_ok, 1)

            def link_or(ins, signal):
                if signal:
                    ins.then_inc(o_ok, 1)
                else:
                    link(ins)

            for s in range(len(units) + 1):
                if s and units[s - 1][0] == "s":
                    normalise_sample(s - 1)
                if s < len(units):
                    scores(s)
                if s:
                    outputs(s - 1)

        @block.tensor
        def _(pe):
            MM = nc.tensor.matmul

            def scores(u):
                kind, br, a, i = units[u]
                if kind == "p" or u == NPU:
                    if u:
                        pe.wait_ge(s_ok, u)
                else:
                    pe.wait_ge(s_ok, u - 1)
                b0 = 2 * (u % 2)
                if kind == "p":
                    rows = slice(a * HD, (a + 1) * HD)
                    w = sum(keys[u])
                    rhs = m.kcT[rows, 0:NCMP] if br == CMP else m.KT[rows, br - 1, 0, 0:w]
                    for g in range(G):
                        last = MM(PS[:, g, 0:w], m.qT[rows, g, i * P:(i + 1) * P], rhs, start=True, stop=True)
                else:
                    if u == NPU:
                        pe.wait_ge(qs_ok, 1)
                    for r in range(2):
                        b = 2 * a + r
                        s = dict(start=(r == 0), stop=(r == 1))
                        if br == CMP:
                            last = MM(PS[:, b0, 0:NCMP], Qs[:, b, :], m.kcT[:, (1 + b) * NCMP:(2 + b) * NCMP], **s)
                        else:
                            MM(PS[:, b0, :], Qs[:, b, :], m.KT[:, br - 1, 1 + b, 0:512], **s)
                            last = MM(PS[:, b0 + 1, 0:TS], Qs[:, b, :], m.KT[:, br - 1, 1 + b, 512:LS], **s)
                last.then_inc(s_ps, 1)

            def turn(u):
                kind, br, a, i = units[u]
                if kind == "p":
                    pe.wait_ge(e_ok, u + 1)
                else:
                    pe.wait_ge(pn_ok, u - NPU + 1)
                for n in of("k", u):
                    if n >= 2:
                        pe.wait_ge(pt_a, n - 1)
                    for x, j in enumerate(pieces[n][2]):
                        kw = keys[u][j]
                        if kind == "p":
                            for g in range(G):
                                last = nc.tensor.transpose(PS[0:kw, 4 + n % 2, g * P:(g + 1) * P], pr[:, u % 2, g * 512 + j * P:g * 512 + j * P + kw], m.ident[:, :])
                        else:
                            last = nc.tensor.transpose(PS[0:kw, 4 + n % 2, x * P:(x + 1) * P], pr[:, u % 2, j * P:j * P + kw], m.ident[:, :])
                    last.then_inc(pt_ps, 1)

            def values(u):
                kind, br, a, i = units[u]
                pe.wait_ge(pt_a, of("k", u)[-1] + 1)
                pe.wait_ge(s_ok, u + 1)
                nk = len(keys[u])
                if kind == "p":
                    for g in range(G):
                        for j, kw in enumerate(keys[u]):
                            rhs = m.vc[:, 0, a * HD:(a + 1) * HD] if br == CMP else m.z[:, j, (384 if br == SEL else 640) + a * HD:(384 if br == SEL else 640) + (a + 1) * HD]
                            last = MM(PS[:, 6 + u % 2, g * HD:(g + 1) * HD], pT[0:kw, j, g * P:(g + 1) * P], rhs, start=(j == 0), stop=(j == nk - 1))
                else:
                    if a >= 2 and br == CMP:
                        pe.wait_ge(o_ok, PT + a - 1)
                    for r in range(2):
                        b = 2 * a + r
                        for j, kw in enumerate(keys[u]):
                            if br == CMP:
                                rhs = m.vc[:, 1 + b, :]
                            else:
                                rhs = m.V[:, br - 1, b * PAGES + j, :] if j < 4 else m.Vn[:, br - 1, b, :]
                            last = MM(PS[0:64, 6 + a % 2, r * P:(r + 1) * P], pT[0:kw, j, r * 64:(r + 1) * 64], rhs,
                                      start=(br == CMP and r == 0 and j == 0), stop=(br == WIN and j == nk - 1), skip_group_check=True)
                last.then_inc(o_ps, 1)

            def finish(u):
                kind, br, a, i = units[u]
                n = of("o", u)[0]
                pe.wait_ge(pt_a, n - 1)
                pe.wait_ge(o_ok, (i if kind == "p" else PT + a) + 1)
                if kind == "p":
                    for c in range(4):
                        last = nc.tensor.transpose(PS[:, 4 + n % 2, c * P:(c + 1) * P], o[:, i % 2, c * P:(c + 1) * P], m.ident[:, :])
                else:
                    for r in range(2):
                        last = nc.tensor.transpose(PS[:, 4 + n % 2, r * 64:(r + 1) * 64], oS[:, r, :, :].rearrange("p u d -> p (u d)"), m.ident[0:64, 0:64])
                last.then_inc(pt_ps, 1)

            for s in range(len(units) + 2):
                if s < len(units):
                    scores(s)
                if s >= 2 and ends(s - 2):
                    finish(s - 2)
                if 1 <= s <= len(units):
                    turn(s - 1)
                    values(s - 1)


T = 128
TOPK = 2
NT = (TOPK * NTOK + NE * (T - 1)) // T
RING = 4
TURNS = -(-NT // RING)
FRONT = NT - NT // RING


def stage_route(nc, m, sb, sem, t, outs):
    PS = m.PS
    w_in, x_in, mod_in, r_in = sem("r_w_in"), sem("r_x_in"), sem("r_mod_in"), sem("r_r_in")
    y_ps, x2_ok, sq_ok, rt_ok, h_ok, hT_ps, hT_ok, lg_ps = [sem("r_" + x) for x in ("y_ps", "x2_ok", "sq_ok", "rt_ok", "h_ok", "hT_ps", "hT_ok", "lg_ps")]
    chain, pch, exp_in, exp_ok, cnt_ok, cnt_ps = [sem("r_" + x) for x in ("chain", "pch", "exp_in", "exp_ok", "cnt_ok", "cnt_ps")]
    KMAX = -(-NTOK // T)
    with ExitStack() as ctx:
        def tb(name, shape, dt=F32):
            return ctx.enter_context(nc.sbuf_tensor(name, shape, dt))
        wo = tb("wo", [P, 8, D])
        mod = tb("mod_r", [P, 2, 3, D])
        h2 = m.h2
        hT = tb("h2T", [P, 2, KD, P])
        rw = tb("rw", [P, KD, NG + NE])
        rb = tb("rb", [P, NG + NE])
        ssq = tb("ssq_r", [P, 3, TILES])
        lg = tb("lg", [P, TILES, NG + NE])
        it = tb("it", [P, NE], I32)
        down = tb("down", [P, NE])
        kt = tb("kt", [P, KMAX])
        iti = tb("iti", [1, TURNS, RING], I32)
        itf = tb("itf", [1, TURNS * RING])
        a4, oh4, e4 = tb("a4", [P, TILES, NG]), tb("oh4", [P, TILES, NG]), tb("e4", [P, TILES, NG])
        s1, wgt = tb("s1", [P, TILES]), tb("wgt", [P, TILES])
        le, pe8, a8 = tb("le", [P, TILES, EPG]), tb("pe8", [P, TILES, EPG]), tb("a8", [P, TILES, EPG])
        oh8 = tb("oh8", [P, 2, TILES, EPG])
        p12 = tb("p12", [P, 2, TILES])
        E = tb("E", [P, 2, TILES, NE])
        C = tb("C", [P, TILES, NE])
        tmp = tb("tmp_r", [P, TILES, NE])
        big = tb("big", [P, NE, KMAX])
        ends = tb("ends", [P, 2, NE])
        base = tb("base", [P, NE])
        posf = tb("posf", [P, 2, TILES])
        tef = tb("tef", [1, TURNS * RING])
        bige = tb("bige", [1, TURNS * RING, NE])
        block = ctx.enter_context(nc.Block())

        @block.sync
        def _(sp):
            for half in range(2):
                sp.dma_start(wo[:, :, half * 512:(half + 1) * 512], t["w_out"][0].rearrange("(c p) n -> p c n", p=P)[:, :, half * 512:(half + 1) * 512]).then_inc(w_in, 16)
            for i in range(PT):
                sp.dma_start(m.x2[:, i, :], t["x_prompt"][0, i * P:(i + 1) * P, :]).then_inc(x_in, 16)
            sp.dma_start(m.x2[0:NB * TS, PT, :], t["x_sample"].rearrange("b j d -> (b j) d")).then_inc(x_in, 16)
            spread_rows(sp, m, mod, 2, 3, mod_in)
            sp.dma_start(rw[:, :, 0:NG], t["router_group_w"][0].rearrange("(k p) n -> p k n", p=P)).then_inc(r_in, 16)
            sp.dma_start(rw[:, :, NG:], t["router_expert_w"][0].rearrange("(k p) n -> p k n", p=P)).then_inc(r_in, 16)
            sp.dma_start(rb[:, 0:NG], t["router_group_b"][0].partition_broadcast(P)).then_inc(r_in, 16)
            sp.dma_start(rb[:, NG:], t["router_expert_b"][0].partition_broadcast(P)).then_inc(r_in, 16)

        @block.gpsimd
        def _(pool):
            link = Chain(pool, pch)
            link(nc.gpsimd.iota(it[:, :], pattern=[[-1, NE]], base=NE, channel_multiplier=0))
            link(nc.gpsimd.tensor_copy(down[:, :], it[:, :]))
            link(nc.gpsimd.iota(it[:, 0:KMAX], pattern=[[T, KMAX]], base=0, channel_multiplier=0))
            link(nc.gpsimd.tensor_copy(kt[:, :], it[:, 0:KMAX]))
            link(nc.gpsimd.iota(iti[:, :, 0:RING - 1], pattern=[[RING - 1, TURNS], [1, RING - 1]], base=0, channel_multiplier=0))
            link(nc.gpsimd.iota(iti[:, :, RING - 1], pattern=[[1, TURNS]], base=FRONT, channel_multiplier=0))
            link(nc.gpsimd.tensor_copy(itf[:, :], iti[:, :, :].rearrange("p t k -> p (t k)")))

        @block.tensor
        def _(pe):
            MM = nc.tensor.matmul
            pe.wait_ge(w_in, 32)
            for i in range(TILES + 1):
                if i < TILES:
                    r, b = ROWS[i], 2 * (i % 2)
                    if i >= 2:
                        pe.wait_ge(x2_ok, i - 1)
                    for half in range(2):
                        for c in range(8):
                            last = MM(PS[0:r, b + half, :], m.mixT[:, c, i * P:i * P + r], wo[:, c, half * 512:(half + 1) * 512], start=(c == 0), stop=(c == 7))
                    last.then_inc(y_ps, 1)
                if i:
                    j = i - 1
                    r = ROWS[j]
                    pe.wait_ge(h_ok, j + 1)
                    if j:
                        pe.wait_ge(hT_ok, j)
                    for k in range(KD):
                        last = nc.tensor.transpose(PS[:, 4 + k // 4, (k % 4) * P:(k % 4) * P + r], h2[0:r, j, k * P:(k + 1) * P], m.ident[0:r, 0:r])
                    last.then_inc(hT_ps, 1)
                    pe.wait_ge(hT_ok, j + 1)
                    if j == 0:
                        pe.wait_ge(r_in, 64)
                    for k in range(KD):
                        last = MM(PS[0:r, 6, j * 40:j * 40 + NG + NE], hT[:, j % 2, k, 0:r], rw[:, k, :], start=(k == 0), stop=(k == KD - 1))
                    last.then_inc(lg_ps, 1)
            pe.wait_ge(cnt_ok, 1)
            for i in range(TILES):
                for j in range(i + 1):
                    MM(PS[:, 7, i * NE:(i + 1) * NE], m.before[:, :] if j == i else m.ones[:, :], C[:, j, :], start=(j == 0), stop=(j == i))
            for j in range(TILES):
                last = MM(PS[:, 7, TILES * NE:(TILES + 1) * NE], m.ones[:, :], C[:, j, :], start=(j == 0), stop=(j == TILES - 1))
            last.then_inc(cnt_ps, 1)

        @block.scalar
        def _(act):
            for i in range(TILES):
                r = ROWS[i]
                act.wait_ge(x2_ok, i + 1)
                nc.scalar.activation(h2[0:r, i, :], m.x2[0:r, i, :], ACT.Square, accum_out=ssq[0:r, 0, i:i + 1]).then_inc(sq_ok, 1)
                act.wait_ge(sq_ok, i + 1)
                nc.scalar.activation(ssq[0:r, 1, i:i + 1], ssq[0:r, 0, i:i + 1], ACT.Sqrt, scale=1.0 / D, bias=m.eps[0:r, 0:1]).then_inc(rt_ok, 1)
            act.wait_ge(exp_in, 1)
            nc.scalar.activation(e4[:, :, :], e4[:, :, :], ACT.Exp).then_inc(exp_ok, 1)
            act.wait_ge(exp_in, 2)
            nc.scalar.activation(pe8[:, :, :], pe8[:, :, :], ACT.Exp).then_inc(exp_ok, 1)

        @block.vector
        def _(dve):
            V = nc.vector
            link = Chain(dve, chain)
            dve.wait_ge(x_in, 16 * TILES)
            dve.wait_ge(mod_in, 16 * SPREAD_DMAS)
            link(V.memset(lg[:, :, :], 0.0))
            for i in range(TILES):
                r, b, v = ROWS[i], 2 * (i % 2), VAR[i]
                dve.wait_ge(y_ps, i + 1)
                link(V.tensor_tensor(h2[0:r, i, :], PS[0:r, b:b + 2, :].rearrange("p b n -> p (b n)"), mod[0:r, v, 0, :], ALU.mult))
                V.tensor_tensor(m.x2[0:r, i, :], m.x2[0:r, i, :], h2[0:r, i, :], ALU.add).then_inc(x2_ok, 1)
                dve.wait_ge(rt_ok, i + 1)
                link(V.reciprocal(ssq[0:r, 2, i:i + 1], ssq[0:r, 1, i:i + 1]))
                link(V.scalar_tensor_tensor(out=h2[0:r, i, :], in0=m.x2[0:r, i, :], scalar=ssq[0:r, 2, i:i + 1], in1=mod[0:r, v, 2, :], op0=ALU.mult, op1=ALU.mult))
                V.tensor_tensor(h2[0:r, i, :], h2[0:r, i, :], mod[0:r, v, 1, :], ALU.add).then_inc(h_ok, 1)
                dve.wait_ge(hT_ps, i + 1)
                V.tensor_copy(hT[:, i % 2, :, 0:r], PS[:, 4:6, :].rearrange("p b (k n) -> p (b k) n", n=P)[:, :, 0:r]).then_inc(hT_ok, 1)
            dve.wait_ge(lg_ps, TILES)
            for i in range(TILES):
                r = ROWS[i]
                link(V.tensor_tensor(lg[0:r, i, :], PS[0:r, 6, i * 40:i * 40 + NG + NE], rb[0:r, :], ALU.add))
            dve.wait_ge(pch, 7)
            g4 = lg[:, :, 0:NG]
            bc = lambda a, n: a.unsqueeze(2).to_broadcast([P, TILES, n])
            dn = lambda n: down[:, NE - n:].unsqueeze(1).to_broadcast([P, TILES, n])

            def first_of(dst, val, top, tmp_, n):
                link(V.tensor_tensor(tmp_, val, bc(top, n), ALU.is_equal))
                link(V.tensor_tensor(tmp_, tmp_, dn(n), ALU.mult))
                link(V.tensor_reduce(s1[:, :], tmp_, AX, ALU.max))
                link(V.tensor_tensor(dst, tmp_, bc(s1[:, :], n), ALU.is_equal))

            link(V.tensor_reduce(wgt[:, :], g4, AX, ALU.max))
            first_of(oh4[:, :, :], g4, wgt[:, :], a4[:, :, :], NG)
            V.tensor_tensor(e4[:, :, :], g4, bc(wgt[:, :], NG), ALU.subtract).then_inc(exp_in, 1)
            l32 = lg[:, :, NG:].rearrange("p i (g e) -> p i g e", g=NG)
            link(V.tensor_tensor(tmp[:, :, :].rearrange("p i (g e) -> p i g e", g=NG), l32, oh4[:, :, :].unsqueeze(3).to_broadcast([P, TILES, NG, EPG]), ALU.mult))
            link(V.tensor_reduce(le[:, :, :], tmp[:, :, :].rearrange("p i (g e) -> p i e g", g=NG), AX, ALU.add))
            link(V.tensor_reduce(s1[:, :], le[:, :, :], AX, ALU.max))
            V.tensor_tensor(pe8[:, :, :], le[:, :, :], bc(s1[:, :], EPG), ALU.subtract).then_inc(exp_in, 1)
            dve.wait_ge(exp_ok, 1)
            link(V.tensor_reduce(wgt[:, :], e4[:, :, :], AX, ALU.add))
            link(V.reciprocal(wgt[:, :], wgt[:, :]))
            dve.wait_ge(exp_ok, 2)
            link(V.tensor_reduce(s1[:, :], pe8[:, :, :], AX, ALU.add))
            link(V.reciprocal(s1[:, :], s1[:, :]))
            link(V.tensor_tensor(pe8[:, :, :], pe8[:, :, :], bc(s1[:, :], EPG), ALU.mult))
            for c in range(TOPK):
                link(V.tensor_reduce(p12[:, c, :], pe8[:, :, :], AX, ALU.max))
                first_of(oh8[:, c], pe8[:, :, :], p12[:, c, :], a8[:, :, :], EPG)
                if c == 0:
                    link(V.scalar_tensor_tensor(out=pe8[:, :, :], in0=oh8[:, 0], scalar=-2.0, in1=pe8[:, :, :], op0=ALU.mult, op1=ALU.add))
            link(V.tensor_tensor(s1[:, :], p12[:, 0, :], p12[:, 1, :], ALU.add))
            link(V.reciprocal(s1[:, :], s1[:, :]))
            link(V.tensor_tensor(s1[:, :], s1[:, :], wgt[:, :], ALU.mult))
            for c in range(TOPK):
                link(V.tensor_tensor(m.choice[:, c, :], p12[:, c, :], s1[:, :], ALU.mult))
                link(V.tensor_tensor(E[:, c].rearrange("p i (g e) -> p i g e", g=NG), oh4[:, :, :].unsqueeze(3).to_broadcast([P, TILES, NG, EPG]),
                                     oh8[:, c].unsqueeze(2).to_broadcast([P, TILES, NG, EPG]), ALU.mult))
            link(V.memset(E[NB * TS:P, :, PT, :], 0.0))
            V.tensor_tensor(C[:, :, :], E[:, 0], E[:, 1], ALU.add).then_inc(cnt_ok, 1)
            dve.wait_ge(cnt_ps, 1)
            link(V.tensor_tensor(big[:, :, :], PS[:, 7, TILES * NE:(TILES + 1) * NE].unsqueeze(2).to_broadcast([P, NE, KMAX]),
                                 kt[:, :].unsqueeze(1).to_broadcast([P, NE, KMAX]), ALU.is_gt))
            link(V.tensor_reduce(base[:, :], big[:, :, :], AX, ALU.add))
            link(V.tensor_copy(ends[:, 0, :], base[:, :]))
            a = 0
            for s in (1, 2, 4, 8, 16):
                link(V.tensor_copy(ends[:, 1 - a, 0:s], ends[:, a, 0:s]))
                link(V.tensor_tensor(ends[:, 1 - a, s:NE], ends[:, a, s:NE], ends[:, a, 0:NE - s], ALU.add))
                a = 1 - a
            link(V.tensor_tensor(base[:, :], ends[:, a, :], base[:, :], ALU.subtract))
            link(V.tensor_scalar(base[:, :], base[:, :], float(T), None, ALU.mult))
            for c in range(TOPK):
                link(V.tensor_tensor(tmp[:, :, :], PS[:, 7, 0:TILES * NE].rearrange("p (i e) -> p i e", e=NE), base[:, :].unsqueeze(1).to_broadcast([P, TILES, NE]), ALU.add))
                link(V.tensor_tensor(tmp[:, :, :], tmp[:, :, :], E[:, c], ALU.mult))
                link(V.tensor_reduce(posf[:, c, :], tmp[:, :, :], AX, ALU.add))
            link(V.tensor_copy(m.pos[:, :], posf[:, :, :].rearrange("p c i -> p (c i)")))
            link(V.tensor_tensor(bige[:, :, :], ends[0:1, a, :].unsqueeze(1).to_broadcast([1, TURNS * RING, NE]), itf[:, :].unsqueeze(2).to_broadcast([1, TURNS * RING, NE]), ALU.is_le))
            link(V.tensor_reduce(tef[:, :], bige[:, :, :], AX, ALU.add))
            link(V.tensor_scalar(itf[:, :], tef[:, :], float(NE), None, ALU.is_lt))
            link(V.tensor_copy(m.te[:, 1, :], itf[:, :]))
            link(V.tensor_scalar(tef[:, :], tef[:, :], float(NE - 1), None, ALU.min))
            link(V.tensor_copy(m.te[:, 0, :], tef[:, :]))


def stage_experts(nc, m, sb, sem, t, outs):
    PS = m.PS
    w_in = [sem(f"e_w_in{i}") for i in range(RING)]
    xs_out = sem("e_xs_out")
    x_in, y_out = [sem(f"e_x_in{i}") for i in range(2)], [sem(f"e_y_out{i}") for i in range(2)]
    t_ps, t_ok, gu_ps, silu_ok, he_ok, dn_ps, y_a, y_v = [sem("e_" + x) for x in ("t_ps", "t_ok", "gu_ps", "silu_ok", "he_ok", "dn_ps", "y_a", "y_v")]
    DC = DE // P
    with ExitStack() as ctx:
        def tb(name, shape):
            return ctx.enter_context(nc.sbuf_tensor(name, shape, F32))
        wg, wu, wd = tb("wg", [P, RING, KD, DE]), tb("wu", [P, RING, KD, DE]), tb("wd", [P, RING, DC, D])
        xr, xT = tb("xr", [T, 2, D]), tb("xsT", [P, 2, KD, T])
        sg, he = tb("sg", [P, 2, DC * T]), tb("he", [P, 2, DC * T])
        yr = tb("yr", [T, 2, D])
        block = ctx.enter_context(nc.Block())

        @block.sync
        def _(sp):
            def step(s):
                if not s.exists(0):
                    return
                if s.is_step(1):
                    sp.wait_ge(xs_out, 16 * TILES * TOPK)
                s.wait(sp, dn_ps, s.tile(-RING + 1))
                e = sp.value_load(s.at(m.te[0:1, 0, :], 1), min_val=0, max_val=NE - 1)
                skip = {}
                if s.may_be_unused():
                    used = sp.value_load(s.at(m.te[0:1, 1, :], 1), min_val=0, max_val=1)
                    skip = dict(cond=used > 0, cond_hint=True)
                k = s.slot(0, RING)
                sp.dma_start(wg[:, k], t["expert_w_gate"][0, bass.ds(e, 1)].rearrange("o (k p) n -> p (o k) n", p=P), **skip).then_inc(w_in[k], 16)
                sp.dma_start(wu[:, k], t["expert_w_up"][0, bass.ds(e, 1)].rearrange("o (k p) n -> p (o k) n", p=P), **skip).then_inc(w_in[k], 16)
                sp.dma_start(wd[:, k], t["expert_w_down"][0, bass.ds(e, 1)].rearrange("o (c p) n -> p (o c) n", p=P), **skip).then_inc(w_in[k], 16)
            run_steps(nc, sp, step)

        @block.gpsimd
        def _(pool):
            for i in range(TILES):
                r = ROWS[i]
                for c in range(TOPK):
                    pool.indirect_dma_start(m.xs_dram.ap(), bass.IndirectOffsetOnAxis(ap=m.pos[0:r, c * TILES + i:c * TILES + i + 1], axis=0),
                                            m.h2[0:r, i, :], None).then_inc(xs_out, 16)
            pool.wait_ge(xs_out, 16 * TILES * TOPK)

            def step(s):
                if not s.exists(0):
                    return
                s.wait(pool, t_ps, s.tile(-1))
                k = s.slot(0, 2)
                pool.dma_start(xr[:, k, :], s.rows(m.xs_dram, 0)).then_inc(x_in[k], 16)
            run_steps(nc, pool, step)

        @block.tensor
        def _(pe):
            MM = nc.tensor.matmul

            def rows_in(s, d):
                s.wait(pe, x_in[s.slot(d, 2)], s.fills(d, 2) * 16)

            def turn(s, d):
                k = s.slot(d, 2)
                for c in range(KD):
                    last = nc.tensor.transpose(PS[:, c // 4, (c % 4) * P:(c % 4) * P + T], xr[:, k, c * P:(c + 1) * P], m.ident[0:T, 0:T])
                last.then_inc(t_ps, 1)

            def gate_up(s):
                k, k2 = s.slot(0, RING), s.slot(0, 2)
                s.wait(pe, t_ok, s.tile(1))
                s.wait(pe, w_in[k], s.fills(0, RING) * 48)
                s.wait(pe, he_ok, s.tile(-1))
                for j, w in enumerate((wg, wu)):
                    for c in range(DC):
                        for q in range(KD):
                            last = MM(PS[:, 2 + k2, (j * DC + c) * T:(j * DC + c + 1) * T], w[:, k, q, c * P:(c + 1) * P], xT[:, k2, q, :], start=(q == 0), stop=(q == KD - 1))
                last.then_inc(gu_ps, 1)

            def down(s):
                k, k2 = s.slot(-1, RING), s.slot(-1, 2)
                s.wait(pe, he_ok, s.tile(0))
                s.wait(pe, y_a, s.tile(-2))
                s.wait(pe, y_v, s.tile(-2))
                for half in range(2):
                    for c in range(DC):
                        last = MM(PS[0:T, 4 + 2 * k2 + half, :], he[:, k2, c * T:(c + 1) * T], wd[:, k, c, half * 512:(half + 1) * 512], start=(c == 0), stop=(c == DC - 1))
                last.then_inc(dn_ps, 1)

            def step(s):
                if s.is_step(0):
                    rows_in(s, 0)
                    turn(s, 0)
                if s.exists(0):
                    gate_up(s)
                if s.exists(1):
                    rows_in(s, 1)
                    turn(s, 1)
                if s.exists(-1):
                    down(s)
            run_steps(nc, pe, step)

        @block.scalar
        def _(act):
            def step(s):
                if s.exists(0):
                    k = s.slot(0, 2)
                    s.wait(act, gu_ps, s.tile(1))
                    s.wait(act, he_ok, s.tile(-1))
                    nc.scalar.activation(sg[:, k, :], PS[:, 2 + k, 0:DC * T], ACT.Silu).then_inc(silu_ok, 1)
                if s.exists(-1):
                    k = s.slot(-1, 2)
                    s.wait(act, dn_ps, s.tile(0))
                    s.wait(act, y_out[k], (s.fills(-1, 2) - 1) * 16)
                    nc.scalar.copy(yr[:, k, 0:512], PS[0:T, 4 + 2 * k, :]).then_inc(y_a, 1)
                    s.wait(act, y_a, s.tile(0))
                    s.wait(act, y_v, s.tile(0))
                    act.dma_start(s.rows(m.ys_dram, -1), yr[:, k, :]).then_inc(y_out[k], 16)
            run_steps(nc, act, step)
            for k in range(2):
                act.wait_ge(y_out[k], 16 * ((NT - k + 1) // 2))

        @block.vector
        def _(dve):
            V = nc.vector

            def take_x(s, d):
                k = s.slot(d, 2)
                s.wait(dve, t_ps, s.tile(d + 1))
                s.wait(dve, gu_ps, s.tile(d - 1))
                V.tensor_copy(xT[:, k], PS[:, 0:2, :].rearrange("p b (c n) -> p (b c) n", n=P)[:, :, 0:T]).then_inc(t_ok, 1)

            def step(s):
                if s.is_step(0):
                    take_x(s, 0)
                if s.exists(0):
                    k = s.slot(0, 2)
                    s.wait(dve, silu_ok, s.tile(1))
                    s.wait(dve, dn_ps, s.tile(-1))
                    V.tensor_tensor(he[:, k, :], sg[:, k, :], PS[:, 2 + k, DC * T:2 * DC * T], ALU.mult).then_inc(he_ok, 1)
                if s.exists(1):
                    take_x(s, 1)
                if s.exists(-1):
                    k = s.slot(-1, 2)
                    s.wait(dve, dn_ps, s.tile(0))
                    s.wait(dve, y_out[k], (s.fills(-1, 2) - 1) * 16)
                    V.tensor_copy(yr[:, k, 512:], PS[0:T, 5 + 2 * k, :]).then_inc(y_v, 1)
            run_steps(nc, dve, step)


class Step:

    def __init__(self, turn, k):
        self.turn, self.k = turn, k

    def tile(self, d):
        return self.turn * RING + (self.k + d)

    def slot(self, d, ring):
        return (self.k + d) % ring

    def fills(self, d, ring):
        return self.turn * (RING // ring) + ((self.k + d) // ring + 1)

    def is_step(self, n):
        return isinstance(self.turn, int) and self.tile(0) == n

    def exists(self, d):
        return not isinstance(self.turn, int) or 0 <= self.tile(d) < NT

    def may_be_unused(self):
        return not isinstance(self.turn, int) or self.turn > 0 and self.sorted_tile(0) >= TOPK * NTOK // T

    def wait(self, eng, sem, value):
        if not isinstance(value, int) or value > 0:
            eng.wait_ge(sem, value)

    def at(self, ap, n):
        s = self.tile(0)
        return ap[:, s:s + n] if isinstance(s, int) else ap[:, bass.ds(s, n)]

    def sorted_tile(self, d):
        turn, k = self.turn + (self.k + d) // RING, (self.k + d) % RING
        return turn + FRONT if k == RING - 1 else turn * (RING - 1) + k

    def rows(self, dram, d):
        s = self.sorted_tile(d)
        ap = dram.ap().rearrange("(j p) d -> j p d", p=T)
        return ap[s] if isinstance(s, int) else ap[bass.ds(s, 1)].rearrange("o p d -> (o p) d")


def run_steps(nc, eng, step):
    for k in range(RING):
        step(Step(0, k))
    with nc.Fori(1, (NT - 1) // RING, engines=[eng.engine]) as turn:
        for k in range(RING):
            step(Step(turn, k))
    for s in range((NT - 1) // RING * RING, NT + 1):
        step(Step(s // RING, s % RING))


def stage_final(nc, m, sb, sem, t, outs):
    mod_in, g_in, a_in, o_ok, out_done, sq, rt, chain = [sem("f_" + x) for x in ("mod_in", "g_in", "a_in", "o_ok", "out_done", "sq", "rt", "chain")]
    row_in = [[sem(f"f_row{c}{k}") for k in range(2)] for c in range(TOPK)]
    with ExitStack() as ctx:
        def tb(name, shape):
            return ctx.enter_context(nc.sbuf_tensor(name, shape, F32))
        mod = tb("mod_f", [P, 2, 1, D])
        fg = tb("fg", [P, D])
        rows = tb("rows", [P, TOPK, 2, D])
        junk = tb("junk_f", [P, D])
        ssq = tb("ssq_f", [P, 3, TILES])
        block = ctx.enter_context(nc.Block())

        @block.sync
        def _(sp):
            spread_rows(sp, m, mod, 5, 1, mod_in)
            sp.dma_start(fg[:, :], t["final_norm_g"].partition_broadcast(P)).then_inc(g_in, 16)
            for i in range(TILES):
                sp.wait_ge(o_ok, i + 1)
                if i < PT:
                    sp.dma_start(outs[0][0, i * P:(i + 1) * P, :], m.x2[:, i, :]).then_inc(out_done, 16)
                else:
                    sp.dma_start(outs[1].rearrange("b j d -> (b j) d"), m.x2[0:NB * TS, i, :]).then_inc(out_done, 16)
            sp.wait_ge(out_done, 16 * TILES)

        @block.gpsimd
        def _(pool):
            for i in range(TILES):
                r = ROWS[i]
                for c in range(TOPK):
                    if i >= 2:
                        pool.wait_ge(a_in, i - 1)
                    pool.indirect_dma_start(rows[0:r, c, i % 2, :], None, m.ys_dram.ap(),
                                            bass.IndirectOffsetOnAxis(ap=m.pos[0:r, c * TILES + i:c * TILES + i + 1], axis=0)).then_inc(row_in[c][i % 2], 16)

        @block.scalar
        def _(act):
            for i in range(TILES):
                r = ROWS[i]
                act.wait_ge(a_in, i + 1)
                nc.scalar.activation(junk[0:r, :], m.x2[0:r, i, :], ACT.Square, accum_out=ssq[0:r, 0, i:i + 1]).then_inc(sq, 1)
                act.wait_ge(sq, i + 1)
                nc.scalar.activation(ssq[0:r, 1, i:i + 1], ssq[0:r, 0, i:i + 1], ACT.Sqrt, scale=1.0 / D, bias=m.eps[0:r, 0:1]).then_inc(rt, 1)

        @block.vector
        def _(dve):
            V = nc.vector
            link = Chain(dve, chain)
            dve.wait_ge(mod_in, 16 * SPREAD_DMAS)
            dve.wait_ge(g_in, 16)

            def normalise(i):
                r = ROWS[i]
                dve.wait_ge(rt, i + 1)
                link(V.reciprocal(ssq[0:r, 2, i:i + 1], ssq[0:r, 1, i:i + 1]))
                V.scalar_tensor_tensor(out=m.x2[0:r, i, :], in0=m.x2[0:r, i, :], scalar=ssq[0:r, 2, i:i + 1], in1=fg[0:r, :], op0=ALU.mult, op1=ALU.mult).then_inc(o_ok, 1)

            for i in range(TILES):
                r, v = ROWS[i], VAR[i]
                for c in range(TOPK):
                    dve.wait_ge(row_in[c][i % 2], 16 * (i // 2 + 1))
                a = rows[0:r, 0, i % 2, :]
                link(V.tensor_scalar(a, a, m.choice[0:r, 0, i:i + 1], None, ALU.mult))
                link(V.scalar_tensor_tensor(out=a, in0=rows[0:r, 1, i % 2, :], scalar=m.choice[0:r, 1, i:i + 1], in1=a, op0=ALU.mult, op1=ALU.add))
                link(V.tensor_tensor(a, a, mod[0:r, v, 0, :], ALU.mult))
                V.tensor_tensor(m.x2[0:r, i, :], m.x2[0:r, i, :], a, ALU.add).then_inc(a_in, 1)
                if i:
                    normalise(i - 1)
            normalise(TILES - 1)


def build(nc, ins, outs):
    t = ins
    with ExitStack() as ctx:
        def sb(name, shape, dt=F32):
            return ctx.enter_context(nc.sbuf_tensor(name, shape, dt))

        held = []

        def sem(name):
            held.append(nc.alloc_semaphore(name))
            return held[-1]

        def stage(function):
            function(nc, m, sb, sem, t, outs)
            nc.clear_and_free_semaphores(held[:])
            held.clear()
            nc.all_engine_barrier()

        m = Bufs()
        m.PS = ctx.enter_context(nc.psum_tensor("PS", [P, 8, 512], F32))
        m.ident = sb("ident", [P, P])
        m.ones = sb("ones", [P, P])
        m.before = sb("before", [P, P])
        m.eps = sb("eps", [P, 3])
        m.seen = sb("seen", [P, 1])
        m.gate_dram = nc.dram_tensor("gate_dram", [NB * TS, 24], F32)
        m.xs_dram = nc.dram_tensor("xs_dram", [NT * T, D], F32)
        m.ys_dram = nc.dram_tensor("ys_dram", [NT * T, D], F32)
        m.pos = sb("pos", [P, TOPK * TILES], I32)
        m.choice = sb("choice", [P, TOPK, TILES])
        m.te = sb("te", [1, 2, TURNS * RING], I32)
        m.mixT = sb("mixT", [P, 8, NTOK])
        m.rb_dram = nc.dram_tensor("rb_dram", [2, H, RB_W], F32)
        m.rb_rep = nc.dram_tensor("rb_rep", [P + TS, H * RB_W], F32)
        m.mod_dram = nc.dram_tensor("mod_dram", [NSEQ, 6 * D], F32)
        stage(lambda *a: stage_modulation(*a[:5]))
        with ExitStack() as att:
            m.z = att.enter_context(nc.sbuf_tensor("z", [P, TILES, ZW], F32))
            m.qT = att.enter_context(nc.sbuf_tensor("qT", [P, G, NTOK], F32))
            with ExitStack() as dn:
                m.same = dn.enter_context(nc.sbuf_tensor("same", [P, 2, P], F32))
                m.upinc = dn.enter_context(nc.sbuf_tensor("upinc", [P, 2, P], F32))
                m.upneg = dn.enter_context(nc.sbuf_tensor("upneg", [P, 2, P], F32))
                m.chunk = dn.enter_context(nc.sbuf_tensor("chunk", [P, 2, P], F32))
                m.bmask = dn.enter_context(nc.sbuf_tensor("bmask", [P, NB], F32))
                m.level = dn.enter_context(nc.sbuf_tensor("level", [P, 6, P], F32))
                m.convwT = dn.enter_context(nc.sbuf_tensor("convwT", [P, 12, CW], F32))
                m.xc = dn.enter_context(nc.sbuf_tensor("xc", [P, 12, CW - 1 + SEQ + NB * (TS + CW - 1)], F32))
                stage(stage_projection)
                with nc.sbuf_tensor("yT", [P, 12, NPAD], F32) as m.yT, nc.sbuf_tensor("kvt", [P, TILES, 2 * DNH * HD], F32) as m.kvt:
                    stage(stage_conv)
                    stage(stage_delta)
            m.kcT = att.enter_context(nc.sbuf_tensor("kcT", [P, NSEQ * NCMP], F32))
            m.vc = att.enter_context(nc.sbuf_tensor("vc", [NCMP, NSEQ, P], F32))
            stage(stage_compress)
            m.KT = att.enter_context(nc.sbuf_tensor("KT", [P, 2, NSEQ, LS], F32))
            m.V = att.enter_context(nc.sbuf_tensor("V", [P, 2, NB * PAGES, P], F32))
            m.Vn = att.enter_context(nc.sbuf_tensor("Vn", [TS, 2, NB, P], F32))
            m.strip = att.enter_context(nc.sbuf_tensor("strip", [P, H, STRIP], F32))
            m.biasS = att.enter_context(nc.sbuf_tensor("biasS", [P, 2, LS], F32))
            stage(stage_keys)
            stage(stage_attention)
        m.x2 = sb("x2", [P, TILES, D])
        m.h2 = sb("h2", [P, TILES, D])
        stage(stage_route)
        stage(stage_experts)
        stage(stage_final)


_INS = ['x_prompt', 'x_sample', 'cache_cmp_k', 'cache_cmp_v', 'cache_sel_k', 'cache_sel_v', 'cache_win_k', 'cache_win_v',
        'state_delta', 'state_conv', 'page_table', 'c_prompt', 'c_sample', 'rel_bias', 'w_ada', 'b_ada', 'norm_mix_g',
        'norm_ffn_g', 'w_in', 'cmp_pos_k', 'cmp_w1_k', 'cmp_w2_k', 'cmp_pos_v', 'cmp_w1_v', 'cmp_w2_v', 'conv_w', 'dn_a_log',
        'dn_dt_bias', 'dn_norm_g', 'w_out', 'router_group_w', 'router_group_b', 'router_expert_w', 'router_expert_b',
        'expert_w_gate', 'expert_w_up', 'expert_w_down', 'final_norm_g']
_OUTS = ([(1, SEQ, D), (NB, TS, D)] + [(1, 1, SEQ, KV, HD)] * 6 + [(1, 1, DNH, HD, HD), (1, 1, CW - 1, CONVD)]
         + [(1, NB, TS, KV, HD)] * 4 + [(1, NB, PAST, KV, HD)] * 2 + [(1, NB, DNH, HD, HD), (1, NB, CW - 1, CONVD)])


def kernel(**inputs):
    import numpy as _np
    import concourse.bacc as _bacc
    from concourse import mybir as _mybir
    from concourse.bass_utils import run_bass_kernel_spmd as _run

    nc = _bacc.Bacc("TRN2", target_bir_lowering=False, num_devices=1)
    arrays, ins = {}, {}
    for name in _INS:
        a = _np.ascontiguousarray(inputs[name])
        arrays[f"in_{name}_dram"] = a
        ins[name] = nc.dram_tensor(f"in_{name}_dram", a.shape, _mybir.dt.from_np(a.dtype), kind="ExternalInput").ap()
    outs = [nc.dram_tensor(f"out_{i}_dram", s, _mybir.dt.float32, kind="ExternalOutput").ap() for i, s in enumerate(_OUTS)]
    build(nc, ins, outs)
    r = _run(nc, [arrays], core_ids=[0])
    return tuple(r.results[0][f"out_{i}_dram"] for i in range(len(_OUTS)))
```

```python
from contextlib import ExitStack
import math

import numpy as np
import concourse.bass as bass
from concourse import mybir

F32 = mybir.dt.float32
I32 = mybir.dt.int32
ALU = mybir.AluOpType
ACT = mybir.ActivationFunctionType
AX = mybir.AxisListType.X

P = 128
D = 1024
KD = D // P
SEQ = 512
NB = 8
TS = 8
NTOK = SEQ + NB * TS
TILES = 5
PT = SEQ // P
PAST = 512
LS = PAST + TS
PAGE = 128
PAGES = PAST // PAGE
NPOOL = NB * PAGES * 5 // 4
H = 8
KV = 2
G = H // KV
HD = 64
CMP_LEN = 32
CMP_STRIDE = 16
NCMP = (SEQ - CMP_LEN) // CMP_STRIDE + 1
assert NCMP == (LS - CMP_LEN) // CMP_STRIDE + 1
CMP_HIDDEN = 256
BUCKETS = 32
MAXDIST = 128
DNH = 8
CONVD = 3 * DNH * HD
CW = 4
NE = 32
NG = 4
EPG = NE // NG
DE = D // 4
EPS = 1e-6
NEG = -1e30
SCALE = HD ** -0.5
IN_DIM = 3368
Q0, KV0, GL0, QKV0, BETA0, GATE0 = 0, 512, 1280, 1304, 2840, 2856
ZA = QKV0 - KV0
ZB = IN_DIM - BETA0
ZW = ZA + ZB
Z_GL, Z_B, Z_A, Z_DG = 768, ZA, ZA + 8, ZA + 16
NSEQ = NB + 1
RB_C = 519
RB_W = 1040
STRIP = 896
VAR = [0] * PT + [1]
ROWS = [P] * PT + [NB * TS]


def bucket_edges():
    half = BUCKETS // 2
    edges, last = [], -1
    for n in range(RB_C + 1):
        b = n if n < half else min(BUCKETS - 1, half + int(math.log(n / half) / math.log(MAXDIST / half) * half + 1e-9))
        if b != last:
            assert b == last + 1
            edges.append(n)
            last = b
    assert len(edges) == BUCKETS
    return edges


class Chain:

    def __init__(self, eng, sem):
        self.eng, self.sem, self.n = eng, sem, 0

    def __call__(self, ins):
        self.n += 1
        ins.then_inc(self.sem, 1)
        self.eng.wait_ge(self.sem, self.n)


class Bufs:
    pass


def stage_modulation(nc, m, sb, sem, t):
    PS = m.PS
    c_in, const, ada_in, bada_in, rb_in = sem("c_in"), sem("const"), [sem(f"ada_in{i}") for i in range(4)], sem("bada_in"), sem("rb_in")
    ident_ok, silu_ok, cT_ps, cT_ok = sem("ident_ok"), sem("silu_ok"), sem("cT_ps"), sem("cT_ok")
    mod_ps, mod_ok, mod_out = sem("mod_ps"), sem("mod_ok"), sem("mod_out")
    rb_ok, rb_out, pchain, bias_in = sem("rb_ok"), sem("rb_out"), sem("m_pchain"), sem("bias_in")
    edges = bucket_edges()
    GROUPS = 6 * D // 512

    with ExitStack() as ctx:
        crow = ctx.enter_context(nc.sbuf_tensor("crow", [NSEQ, D], F32))
        cT = ctx.enter_context(nc.sbuf_tensor("cT", [P, KD, NSEQ], F32))
        bada = ctx.enter_context(nc.sbuf_tensor("bada", [NSEQ, 6 * D], F32))
        modrows = ctx.enter_context(nc.sbuf_tensor("modrows", [NSEQ, 6 * D], F32))
        wada = ctx.enter_context(nc.sbuf_tensor("wada", [P, 4, KD, 512], F32))
        gains = ctx.enter_context(nc.sbuf_tensor("gains", [NSEQ, 2, D], F32))
        rbT = ctx.enter_context(nc.sbuf_tensor("rbT", [H, BUCKETS], F32))
        rrow = ctx.enter_context(nc.sbuf_tensor("rrow", [H, 2, RB_W], F32))
        block = ctx.enter_context(nc.Block())

        @block.sync
        def _(sp):
            sp.dma_start(crow[0:1, :], t["c_prompt"]).then_inc(c_in, 16)
            sp.dma_start(crow[1:NSEQ, :], t["c_sample"]).then_inc(c_in, 16)
            with nc.allow_non_contiguous_dma(reason="256 words, transposed"):
                sp.dma_start(rbT[:, :], t["rel_bias"].rearrange("b h -> h b")).then_inc(rb_in, 16)
            wv = t["w_ada"][0].rearrange("(k p) n -> p k n", p=P)
            for g in range(GROUPS):
                if g >= 4:
                    sp.wait_ge(mod_ps, g - 3)
                sp.dma_start(wada[:, g % 4], wv[:, :, g * 512:(g + 1) * 512]).then_inc(ada_in[g % 4], 16)
                if g == 0:
                    sp.dma_start(bada[:, :], t["b_ada"][0].partition_broadcast(NSEQ)).then_inc(bada_in, 16)
                    sp.dma_start(gains[:, 0, :], t["norm_mix_g"][0].partition_broadcast(NSEQ)).then_inc(bada_in, 16)
                    sp.dma_start(gains[:, 1, :], t["norm_ffn_g"][0].partition_broadcast(NSEQ)).then_inc(bada_in, 16)
            sp.wait_ge(mod_ok, GROUPS + 4)
            sp.dma_start(m.mod_dram.ap(), modrows[:, :]).then_inc(mod_out, 16)
            sp.wait_ge(mod_out, 16)

        @block.gpsimd
        def _(pool):
            link = Chain(pool, pchain)
            link(nc.gpsimd.memset(m.ident[:], 0.0))
            nc.gpsimd.affine_select(out=m.ident[:], in_=m.ident[:], compare_op=ALU.not_equal, fill=1.0, base=0,
                                    pattern=[[-1, P]], channel_multiplier=1).then_inc(ident_ok, 1)
            link(nc.gpsimd.memset(m.ones[:], 1.0))
            link(nc.gpsimd.affine_select(out=m.before[:], in_=m.ones[:], compare_op=ALU.is_gt, fill=0.0, base=0,
                                         pattern=[[1, P]], channel_multiplier=-1))
            link(nc.gpsimd.affine_select(out=m.seen[:], in_=m.ones[:, 0:1], compare_op=ALU.is_ge, fill=0.0, base=1 - CMP_LEN,
                                         pattern=[[0, 1]], channel_multiplier=1))
            nc.gpsimd.memset(m.eps[:, 0:1], EPS)
            nc.gpsimd.memset(m.eps[:, 1:2], EPS * HD)
            nc.gpsimd.memset(m.eps[:, 2:3], 1.0).then_inc(const, 1)
            pool.wait_ge(rb_ok, 2 * (BUCKETS + 1) + 1)
            pool.dma_start(m.rb_dram.ap().rearrange("v h w -> h v w"), rrow[:, :, :]).then_inc(rb_out, 16)
            pool.wait_ge(rb_out, 16)
            rows = m.rb_dram.ap().rearrange("v h w -> v (h w)")
            pool.dma_start(m.rb_rep.ap()[0:P, :], rows[0].partition_broadcast(P)).then_inc(rb_out, 16)
            pool.dma_start(m.rb_rep.ap()[P:P + TS, :], rows[1].partition_broadcast(TS)).then_inc(rb_out, 16)
            pool.wait_ge(rb_out, 48)

        @block.tensor
        def _(pe):
            pe.wait_ge(silu_ok, 1)
            pe.wait_ge(ident_ok, 1)
            for k in range(KD):
                last = nc.tensor.transpose(PS[:, 6, k * NSEQ:(k + 1) * NSEQ], crow[:, k * P:(k + 1) * P], m.ident[0:NSEQ, 0:NSEQ])
            last.then_inc(cT_ps, 1)
            pe.wait_ge(cT_ok, 1)
            for g in range(GROUPS):
                pe.wait_ge(ada_in[g % 4], 16 * (g // 4 + 1))
                if g >= 2:
                    pe.wait_ge(mod_ok, g - 1)
                for k in range(KD):
                    last = nc.tensor.matmul(PS[0:NSEQ, g % 2, :], cT[:, k, :], wada[:, g % 4, k, :], start=(k == 0), stop=(k == KD - 1))
                last.then_inc(mod_ps, 1)

        @block.scalar
        def _(act):
            act.wait_ge(c_in, 32)
            nc.scalar.activation(crow[:, :], crow[:, :], ACT.Silu).then_inc(silu_ok, 1)

        @block.vector
        def _(dve):
            dve.wait_ge(cT_ps, 1)
            nc.vector.tensor_copy(cT[:, :, :], PS[:, 6, 0:KD * NSEQ].rearrange("p (k s) -> p k s", s=NSEQ)).then_inc(cT_ok, 1)
            dve.wait_ge(rb_in, 16)
            bias = Chain(dve, rb_ok)
            for v in range(2):
                bias(nc.vector.memset(rrow[:, v, :], NEG))
                for b in range(BUCKETS):
                    lo = edges[b]
                    hi = edges[b + 1] if b + 1 < BUCKETS else RB_C + 1
                    a, z = RB_C - hi + 1, RB_C - lo + 1
                    nc.vector.tensor_copy(rrow[:, v, a:z], rbT[:, b:b + 1].to_broadcast([H, z - a])).then_inc(rb_ok, 1)
                bias.n += BUCKETS
                dve.wait_ge(rb_ok, bias.n)
            bias(nc.vector.memset(rrow[:, 1, 0:RB_C - SEQ + 1], NEG))
            dve.wait_ge(bada_in, 48)
            for g in range(GROUPS):
                dve.wait_ge(mod_ps, g + 1)
                c = g * 512
                nc.vector.tensor_tensor(modrows[:, c:c + 512], PS[0:NSEQ, g % 2, :], bada[:, c:c + 512], ALU.add).then_inc(mod_ok, 1)
            dve.wait_ge(mod_ok, GROUPS)
            for g in (2, 3, 8, 9):
                c = g * 512
                nc.vector.scalar_tensor_tensor(out=modrows[:, c:c + 512], in0=modrows[:, c:c + 512], scalar=1.0,
                                               in1=gains[:, g // 6, (g % 2) * 512:(g % 2 + 1) * 512],
                                               op0=ALU.add, op1=ALU.mult).then_inc(mod_ok, 1)


def spread_rows(eng, m, dst, first, n, done):
    eng.dma_start(dst[:, 0].rearrange("p a d -> p (a d)"), m.mod_dram.ap()[0, first * D:(first + n) * D].partition_broadcast(P)).then_inc(done, 16)
    for b in range(NB):
        eng.dma_start(dst[b * TS:(b + 1) * TS, 1].rearrange("p a d -> p (a d)"),
                      m.mod_dram.ap()[1 + b, first * D:(first + n) * D].partition_broadcast(TS)).then_inc(done, 16)


SPREAD_DMAS = 1 + NB


def stage_projection(nc, m, sb, sem, t, outs):
    PS = m.PS
    x_in, h_ok, hT_ps, hT_ok = sem("x_in"), sem("h_ok"), sem("hT_ps"), sem("hT_ok")
    mod_in, masks, zeroed = sem("mod_in"), sem("masks"), sem("zeroed")
    w_in = [sem(f"w_in{i}") for i in range(3)]
    z_ps, z_v, z_a, sq, rt, dch, rows_out = sem("z_ps"), sem("z_v"), sem("z_a"), sem("sq"), sem("rt"), sem("p_dch"), sem("rows_out")
    hist_in, hist_ps, hist_ok = sem("hist_in"), sem("hist_ps"), sem("hist_ok")
    groups = [(KV0, ZA // 2, False), (KV0 + ZA // 2, ZA // 2, False), (BETA0, ZB, False),
              (QKV0, 512, True), (QKV0 + 512, 512, True), (QKV0 + 1024, 512, True), (Q0, 512, True)]
    QG = 6
    slot_dmas = [[], [], []]
    for g in range(len(groups)):
        slot_dmas[g % 3].append(KD * KV if g == QG else 1)
    units = []
    for g, (c, w, chan) in enumerate(groups):
        for i in range(4 if chan else TILES):
            units.append((g, i))
    last_unit = [max(n for n, u in enumerate(units) if u[0] == g) + 1 for g in range(len(groups))]
    own = ["v" if n % 2 else "a" for n in range(len(units))]
    before = lambda n, e: sum(o == e for o in own[:n + 1])

    with ExitStack() as ctx:
        wring = ctx.enter_context(nc.sbuf_tensor("wring", [P, 3, KD, ZB], F32))
        ssq = ctx.enter_context(nc.sbuf_tensor("ssq", [P, 3, TILES], F32))
        hT = ctx.enter_context(nc.sbuf_tensor("hT", [P, KD, NTOK], F32))
        hist = ctx.enter_context(nc.sbuf_tensor("hist", [NB * (CW - 1), CONVD], F32))
        x = ctx.enter_context(nc.sbuf_tensor("x", [P, TILES, D], F32))
        mod = ctx.enter_context(nc.sbuf_tensor("mod01", [P, 2, 2, D], F32))
        zero = m.mixT[0:T, :, :].rearrange("p c n -> p (c n)")[:, 0:D]
        convw = ctx.enter_context(nc.sbuf_tensor("convw", [CW, CONVD], F32))
        block = ctx.enter_context(nc.Block())

        def evacuate(eng, n, copy, done):
            g, i = units[n]
            c, w, chan = groups[g]
            b = 2 * (n % 3)
            if chan:
                if g == QG:
                    copy(m.qT[:, i, :], PS[:, b:b + 2, :].rearrange("p b n -> p (b n)")[:, 0:NTOK]).then_inc(done, 1)
                else:
                    ch = (g - 3) * 4 + i
                    copy(m.xc[:, ch, CW - 1:CW - 1 + SEQ], PS[:, b, :])
                    copy(m.xc[:, ch, CW - 1 + SEQ:].rearrange("p (b j) -> p b j", j=TS + CW - 1)[:, :, CW - 1:],
                         PS[:, b + 1, 0:NB * TS].rearrange("p (b j) -> p b j", j=TS)).then_inc(done, 1)
            else:
                r = ROWS[i]
                o = (0, ZA // 2, ZA)[g]
                src = PS[0:r, b, 0:w] if w <= 512 else PS[0:r, b:b + 2, 0:w // 2]
                dst = m.z[0:r, i, o:o + w]
                if w > 512:
                    dst = dst.rearrange("p (b n) -> p b n", b=2)
                copy(dst, src).then_inc(done, 1)

        def copy_hT(dve, i):
            r, b = ROWS[i], 2 * (i % 2)
            dve.wait_ge(hT_ps, i + 1)
            nc.vector.tensor_copy(hT[:, :, i * P:i * P + r], PS[:, b:b + 2, :].rearrange("p b (k n) -> p (b k) n", n=P)[:, :, 0:r]).then_inc(hT_ok, 1)

        @block.sync
        def _(sp):
            for i in range(PT):
                sp.dma_start(x[:, i, :], t["x_prompt"][0, i * P:(i + 1) * P, :]).then_inc(x_in, 16)
            sp.dma_start(x[0:NB * TS, PT, :], t["x_sample"].rearrange("b j d -> (b j) d")).then_inc(x_in, 16)
            spread_rows(sp, m, mod, 0, 2, mod_in)
            sp.dma_start(hist[:, :], t["state_conv"][0].rearrange("b j c -> (b j) c")).then_inc(hist_in, 16)
            sp.dma_start(convw[:, :], t["conv_w"][0]).then_inc(hist_in, 16)
            wv = t["w_in"][0].rearrange("(k p) n -> p k n", p=P)
            for g, (c, w, chan) in enumerate(groups):
                if g >= 3:
                    sp.wait_ge(z_ps, last_unit[g - 3])
                if g == QG:
                    for k in range(KD):
                        for v in range(KV):
                            sp.dma_start(wring[:, g % 3, k, 0:512].rearrange("p (g v d) -> p g v d", v=KV, g=G)[:, :, v],
                                         wv[:, k, v * G * HD:(v + 1) * G * HD].rearrange("p (g d) -> p g d", g=G)).then_inc(w_in[g % 3], 16)
                else:
                    sp.dma_start(wring[:, g % 3, :, 0:w], wv[:, :, c:c + w]).then_inc(w_in[g % 3], 16)

        @block.gpsimd
        def _(pool):
            link = Chain(pool, masks)
            link(nc.gpsimd.memset(zero, 0.0))
            xs = m.xs_dram.ap().rearrange("(j p) d -> j p d", p=T)
            for j in range(NT):
                pool.dma_start(xs[j], zero).then_inc(zeroed, 16)
            for i, c in enumerate((HD, TS)):
                nb = P // c
                u = m.same[:, i, :].rearrange("p (b j) -> p b j", j=c)
                link(nc.gpsimd.memset(m.same[:, i, :], 1.0))
                link(nc.gpsimd.affine_select(out=u, in_=u, compare_op=ALU.is_ge, fill=0.0, base=0,
                                             pattern=[[-c, nb], [0, c]], channel_multiplier=1))
                link(nc.gpsimd.affine_select(out=u, in_=u, compare_op=ALU.is_ge, fill=0.0, base=c - 1,
                                             pattern=[[c, nb], [0, c]], channel_multiplier=-1))
                link(nc.gpsimd.affine_select(out=m.upinc[:, i, :], in_=m.same[:, i, :], compare_op=ALU.is_ge,
                                             fill=0.0, base=0, pattern=[[1, P]], channel_multiplier=-1))
                link(nc.gpsimd.tensor_scalar(m.upneg[:, i, :], m.upinc[:, i, :], 1.0, 1e30, ALU.subtract, ALU.mult))
            for c in range(2):
                link(nc.gpsimd.tensor_copy(m.chunk[:, c, :].rearrange("p (a j) -> p a j", j=HD),
                                           m.same[:, 0, c * HD:(c + 1) * HD].unsqueeze(1).to_broadcast([P, 2, HD])))
            link(nc.gpsimd.tensor_copy(m.bmask[:, :], m.same[:, 1, 0:NB * TS:TS]))
            for l in range(6):
                w = 2 ** l
                nb = P // (2 * w)
                link(nc.gpsimd.memset(m.level[:, l, :], 1.0))
                u = m.level[:, l, :].rearrange("p (b s j) -> p b s j", s=2, j=w)
                link(nc.gpsimd.affine_select(out=u, in_=u, compare_op=ALU.is_ge, fill=0.0, base=-w,
                                             pattern=[[-2 * w, nb], [-P, 2], [0, w]], channel_multiplier=1))
                link(nc.gpsimd.affine_select(out=u, in_=u, compare_op=ALU.is_ge, fill=0.0, base=2 * w - 1,
                                             pattern=[[2 * w, nb], [0, 2], [0, w]], channel_multiplier=-1))
            pool.wait_ge(zeroed, 16 * NT)

        @block.scalar
        def _(act):
            for i in range(TILES):
                r = ROWS[i]
                act.wait_ge(x_in, 16 * TILES)
                nc.scalar.activation(PS[0:r, 6:8, :].rearrange("p b n -> p (b n)"), x[0:r, i, :], ACT.Square, accum_out=ssq[0:r, 0, i:i + 1]).then_inc(sq, 1)
                act.wait_ge(sq, i + 1)
                nc.scalar.activation(ssq[0:r, 1, i:i + 1], ssq[0:r, 0, i:i + 1], ACT.Sqrt, scale=1.0 / D, bias=m.eps[0:r, 0:1]).then_inc(rt, 1)
            for n, (g, i) in enumerate(units):
                if own[n] == "a":
                    act.wait_ge(z_ps, n + 1)
                    evacuate(act, n, nc.scalar.copy, z_a)
            act.wait_ge(z_v, before(9, "v"))
            act.wait_ge(z_a, before(9, "a"))
            for j in range(6):
                act.dma_start(outs[2 + j].rearrange("l b (i p) k d -> p (l b i) (k d)", p=P), m.z[:, 0:PT, j * P:(j + 1) * P]).then_inc(rows_out, 16)
                if j < 4:
                    act.dma_start(outs[10 + j].rearrange("l b s k d -> (l b s) (k d)"), m.z[0:NB * TS, PT, j * P:(j + 1) * P]).then_inc(rows_out, 16)
            for j in range(2):
                for b in range(NB):
                    act.dma_start(outs[14 + j][0, b, PAST - TS:PAST].rearrange("s k d -> s (k d)"),
                                  m.z[b * TS:(b + 1) * TS, PT, (4 + j) * P:(5 + j) * P]).then_inc(rows_out, 16)
                    act.dma_start(outs[14 + j][0, b, 0:PAST - TS].rearrange("s k d -> s (k d)"),
                                  t["cache_win_k" if j == 0 else "cache_win_v"][0, b, TS:PAST].rearrange("s k d -> s (k d)")).then_inc(rows_out, 16)
            act.wait_ge(rows_out, 16 * (10 + 4 * NB))

        @block.vector
        def _(dve):
            link = Chain(dve, dch)
            link(nc.vector.memset(m.xc[:, :, 0:CW - 1], 0.0))
            link(nc.vector.memset(m.z[:, PT, :], 0.0))
            dve.wait_ge(mod_in, 16 * SPREAD_DMAS)
            for i in range(TILES):
                r, v = ROWS[i], VAR[i]
                dve.wait_ge(rt, i + 1)
                link(nc.vector.reciprocal(ssq[0:r, 2, i:i + 1], ssq[0:r, 1, i:i + 1]))
                link(nc.vector.scalar_tensor_tensor(out=x[0:r, i, :], in0=x[0:r, i, :], scalar=ssq[0:r, 2, i:i + 1],
                                                    in1=mod[0:r, v, 1, :], op0=ALU.mult, op1=ALU.mult))
                nc.vector.tensor_tensor(x[0:r, i, :], x[0:r, i, :], mod[0:r, v, 0, :], ALU.add).then_inc(h_ok, 1)
                if i >= 1:
                    copy_hT(dve, i - 1)
            copy_hT(dve, TILES - 1)
            dve.wait_ge(hist_ps, 1)
            nh = NB * (CW - 1)
            for c in range(12):
                nc.vector.tensor_copy(m.xc[:, c, CW - 1 + SEQ:].rearrange("p (b j) -> p b j", j=TS + CW - 1)[:, :, 0:CW - 1],
                                      PS[:, 6, c * nh:(c + 1) * nh].rearrange("p (b j) -> p b j", j=CW - 1)).then_inc(hist_ok, 1)
            nc.vector.tensor_copy(m.convwT[:, :, :], PS[:, 7, 0:12 * CW].rearrange("p (c j) -> p c j", j=CW))
            for n, (g, i) in enumerate(units):
                if own[n] == "v":
                    dve.wait_ge(z_ps, n + 1)
                    evacuate(dve, n, nc.vector.tensor_copy, z_v)

        @block.tensor
        def _(pe):
            for i in range(TILES):
                r, b = ROWS[i], 2 * (i % 2)
                pe.wait_ge(h_ok, i + 1)
                if i >= 2:
                    pe.wait_ge(hT_ok, i - 1)
                for k in range(KD):
                    last = nc.tensor.transpose(PS[:, b + k // 4, (k % 4) * P:(k % 4) * P + r], x[0:r, i, k * P:(k + 1) * P], m.ident[0:r, 0:r])
                last.then_inc(hT_ps, 1)
            nh = NB * (CW - 1)
            pe.wait_ge(hist_in, 32)
            for c in range(12):
                last = nc.tensor.transpose(PS[:, 6, c * nh:(c + 1) * nh], hist[:, c * P:(c + 1) * P], m.ident[0:nh, 0:nh])
            for c in range(12):
                last = nc.tensor.transpose(PS[:, 7, c * CW:(c + 1) * CW], convw[:, c * P:(c + 1) * P], m.ident[0:CW, 0:CW])
            last.then_inc(hist_ps, 1)
            pe.wait_ge(hT_ok, TILES)
            for n, (g, i) in enumerate(units):
                c, w, chan = groups[g]
                b = 2 * (n % 3)
                if i == 0:
                    pe.wait_ge(w_in[g % 3], 16 * sum(slot_dmas[g % 3][:g // 3 + 1]))
                if n >= 3:
                    pe.wait_ge(z_v if own[n - 3] == "v" else z_a, before(n - 3, own[n - 3]))
                for k in range(KD):
                    s = dict(start=(k == 0), stop=(k == KD - 1))
                    if chan:
                        lhs = wring[:, g % 3, k, i * P:(i + 1) * P]
                        nc.tensor.matmul(PS[:, b, :], lhs, hT[:, k, 0:SEQ], **s)
                        last = nc.tensor.matmul(PS[:, b + 1, 0:NB * TS], lhs, hT[:, k, SEQ:NTOK], **s)
                    else:
                        r = ROWS[i]
                        lhs = hT[:, k, i * P:i * P + r]
                        if w <= 512:
                            last = nc.tensor.matmul(PS[0:r, b, 0:w], lhs, wring[:, g % 3, k, 0:w], **s)
                        else:
                            nc.tensor.matmul(PS[0:r, b, 0:w // 2], lhs, wring[:, g % 3, k, 0:w // 2], **s)
                            last = nc.tensor.matmul(PS[0:r, b + 1, 0:w // 2], lhs, wring[:, g % 3, k, w // 2:w], **s)
                last.then_inc(z_ps, 1)


NPAD = TILES * P
XS = CW - 1 + SEQ
XW = XS + NB * (TS + CW - 1)


def stage_conv(nc, m, sb, sem, t, outs):
    PS = m.PS
    conv_ok, silu_ok, sq_ok, ss_ps, ss_ok, rt_ok = sem("conv_ok"), sem("csilu_ok"), sem("csq_ok"), sem("ss_ps"), sem("ss_ok"), sem("crt_ok")
    y_ok, kv_ps, kv_ok, chain, chainp = sem("y_ok"), sem("kv_ps"), sem("kv_ok"), sem("c_chain"), sem("c_chainp")
    hc_ok, hc_ps, hc_rows, st_out = sem("hc_ok"), sem("hc_ps"), sem("hc_rows"), sem("st_out")
    gain_in, gate_ok, gated = sem("gain_in"), sem("gate_ok"), sem("gated")
    NC_ = CONVD // P
    QK = 2 * DNH * HD // P
    N = XW - CW + 1
    nh = NSEQ * (CW - 1)
    with ExitStack() as ctx:
        acc = ctx.enter_context(nc.sbuf_tensor("acc", [P, 2, XW], F32))
        sq = ctx.enter_context(nc.sbuf_tensor("sq", [P, 2, NPAD], F32))
        hc = ctx.enter_context(nc.sbuf_tensor("hc", [P, NC_, nh], F32))
        hrows = ctx.enter_context(nc.sbuf_tensor("hrows", [nh, CONVD], F32))
        grow = ctx.enter_context(nc.sbuf_tensor("grow", [P, HD], F32))
        ss = m.kvt[:, :, :].rearrange("p i n -> p (i n)").rearrange("p (c n) -> p c n", n=NPAD)
        block = ctx.enter_context(nc.Block())

        def take_sum(dve, c):
            dve.wait_ge(ss_ps, c + 1)
            b = 2 * (c % 2)
            nc.vector.tensor_copy(ss[:, c, :], PS[:, b:b + 2, :].rearrange("p b n -> p (b n)")[:, 0:NPAD]).then_inc(ss_ok, 1)

        @block.sync
        def _(sp):
            sp.dma_start(grow[:, :], t["dn_norm_g"][0].partition_broadcast(P)).then_inc(gain_in, 16)

        @block.gpsimd
        def _(pool):
            nc.gpsimd.tensor_copy(hc[:, :, 0:CW - 1], m.xc[:, :, SEQ:SEQ + CW - 1]).then_inc(hc_ok, 1)
            nc.gpsimd.tensor_copy(hc[:, :, CW - 1:].rearrange("p c (b j) -> p c b j", j=CW - 1),
                                  m.xc[:, :, XS:].rearrange("p c (b j) -> p c b j", j=TS + CW - 1)[:, :, :, TS:]).then_inc(hc_ok, 1)
            pool.wait_ge(gain_in, 16)
            pool.wait_ge(gate_ok, 1)
            for i in range(TILES):
                gt = m.z[:, i, Z_DG:Z_DG + 512].rearrange("p (h d) -> p h d", d=HD)
                nc.gpsimd.tensor_tensor(gt, gt, grow[:, :].unsqueeze(1).to_broadcast([P, DNH, HD]), ALU.mult).then_inc(gated, 1)

        @block.scalar
        def _(act):
            for c in range(NC_):
                act.wait_ge(conv_ok, c + 1)
                nc.scalar.activation(m.yT[:, c, 0:SEQ], acc[:, c % 2, 0:SEQ], ACT.Silu).then_inc(silu_ok, 1)
                nc.scalar.activation(m.yT[:, c, SEQ:NTOK].rearrange("p (b j) -> p b j", j=TS),
                                     acc[:, c % 2, XS:].rearrange("p (b j) -> p b j", j=TS + CW - 1)[:, :, 0:TS], ACT.Silu).then_inc(silu_ok, 1)
                if c < QK:
                    act.wait_ge(silu_ok, 2 * c + 2)
                    if c >= 2:
                        act.wait_ge(ss_ps, c - 1)
                    nc.scalar.activation(sq[:, c % 2, :], m.yT[:, c, :], ACT.Square).then_inc(sq_ok, 1)
            nc.scalar.activation(m.z[:, :, Z_DG:Z_DG + 512], m.z[:, :, Z_DG:Z_DG + 512], ACT.Silu).then_inc(gate_ok, 1)
            for c in range(QK):
                act.wait_ge(ss_ok, c + 1)
                s = float(HD) if c < QK // 2 else 1.0
                nc.scalar.activation(ss[:, c, :], ss[:, c, :], ACT.Sqrt, scale=s, bias=m.eps[:, 1:2] if c < QK // 2 else m.eps[:, 0:1]).then_inc(rt_ok, 1)
            act.wait_ge(hc_ps, 1)
            nc.scalar.activation(hrows[:, :], PS[0:nh, 4:7, :].rearrange("p b n -> p (b n)"), ACT.Copy).then_inc(hc_rows, 1)
            act.wait_ge(hc_rows, 1)
            act.dma_start(outs[9][0, 0], hrows[0:CW - 1, :]).then_inc(st_out, 16)
            act.dma_start(outs[17][0].rearrange("b j c -> (b j) c"), hrows[CW - 1:nh, :]).then_inc(st_out, 16)
            act.wait_ge(st_out, 32)

        @block.vector
        def _(dve):
            link = Chain(dve, chain)
            link(nc.vector.memset(m.yT[:, :, NTOK:NPAD], 0.0))
            for c in range(NC_):
                if c >= 2:
                    dve.wait_ge(silu_ok, 2 * (c - 1))
                a = acc[:, c % 2, 0:N]
                link(nc.vector.tensor_scalar(a, m.xc[:, c, 0:N], m.convwT[:, c, 0:1], None, ALU.mult))
                for j in range(1, CW):
                    ins = nc.vector.scalar_tensor_tensor(out=a, in0=m.xc[:, c, j:j + N], scalar=m.convwT[:, c, j:j + 1], in1=a, op0=ALU.mult, op1=ALU.add)
                    if j < CW - 1:
                        link(ins)
                    else:
                        ins.then_inc(conv_ok, 1)
                if 1 <= c < QK + 1:
                    take_sum(dve, c - 1)
            for c in range(QK):
                dve.wait_ge(rt_ok, c + 1)
                link(nc.vector.reciprocal(ss[:, c, :], ss[:, c, :]))
                nc.vector.tensor_tensor(m.yT[:, c, :], m.yT[:, c, :], ss[:, c, :], ALU.mult).then_inc(y_ok, 1)
            dve.wait_ge(y_ok, QK)
            for i in range(TILES):
                dve.wait_ge(kv_ps, i + 1)
                nc.vector.tensor_copy(m.kvt[:, i, :], PS[:, 2 * (i % 2):2 * (i % 2) + 2, :].rearrange("p b n -> p (b n)")).then_inc(kv_ok, 1)

        @block.tensor
        def _(pe):
            pe.wait_ge(hc_ok, 2)
            for c in range(NC_):
                last = nc.tensor.transpose(PS[0:nh, 4 + c // 4, (c % 4) * P:(c % 4 + 1) * P], hc[:, c, :], m.ident[:, :])
            last.then_inc(hc_ps, 1)
            for c in range(QK):
                pe.wait_ge(sq_ok, c + 1)
                if c >= 2:
                    pe.wait_ge(ss_ok, c - 1)
                b = 2 * (c % 2)
                nc.tensor.matmul(PS[:, b, :], m.same[:, 0, :], sq[:, c % 2, 0:512], start=True, stop=True)
                nc.tensor.matmul(PS[:, b + 1, 0:NPAD - 512], m.same[:, 0, :], sq[:, c % 2, 512:NPAD], start=True, stop=True).then_inc(ss_ps, 1)
            pe.wait_ge(y_ok, QK)
            pe.wait_ge(silu_ok, 2 * NC_)
            for i in range(TILES):
                if i >= 2:
                    pe.wait_ge(kv_ok, i - 1)
                for c in range(KD):
                    last = nc.tensor.transpose(PS[:, 2 * (i % 2) + c // 4, (c % 4) * P:(c % 4 + 1) * P], m.yT[:, QK // 2 + c, i * P:(i + 1) * P], m.ident[:, :])
                last.then_inc(kv_ps, 1)


def heads_em(ap):
    return ap.rearrange("p (m e n) -> p e m n", m=DNH // 2, e=2)


def stage_delta(nc, m, sb, sem, t, outs):
    PS = m.PS
    st_in, gates_a, gch = sem("st_in"), sem("gates_a"), sem("d_gch")
    chain, pchain = sem("d_chain"), sem("d_pchain")
    cum_ps, cum_ok, eg_ok, spread, cn_ok, gb_ps, bi_ps, kk_ps, qk_ps = [sem("d_" + x) for x in ("cum_ps", "cum_ok", "eg_ok", "spread", "cn_ok", "gb_ps", "bi_ps", "kk_ps", "qk_ps")]
    egb_ok, d_in, d_exp, bt_ok, qk_ok, kb_ok, kg_ok, qg_ok = [sem("d_" + x) for x in ("egb_ok", "d_in", "d_exp", "bt_ok", "qk_ok", "kb_ok", "kg_ok", "qg_ok")]
    lp_ps, lp_ok, lt_ps, lt_ok, wu_ps, w_ok, u_ok = [sem("d_" + x) for x in ("lp_ps", "lp_ok", "lt_ps", "lt_ok", "wu_ps", "w_ok", "u_ok")]
    ws_ps, v_ok, sk_ps, so_ps, s_ok, o_ok, vm_ok, zero_ok = [sem("d_" + x) for x in ("ws_ps", "v_ok", "sk_ps", "so_ps", "s_ok", "o_ok", "vm_ok", "zero_ok")]
    o_sq, o_ss, o_rt, o_fin, o_ps, o_T = [sem("d_" + x) for x in ("o_sq", "o_ss", "o_rt", "o_fin", "o_ps", "o_T")]
    sto, mask_ok, su_ps = sem("d_sto"), sem("d_mask_ok"), sem("d_su_ps")
    LEVELS = [6] * PT + [3]
    M4 = DNH // 2
    C2 = 2 * PT
    before = lambda i: sum(LEVELS[:i])
    scans = lambda i: min(2 * i, C2 + 1)

    with ExitStack() as ctx:
        def tb(name, shape):
            return ctx.enter_context(nc.sbuf_tensor(name, shape, F32))

        arow, dtrow = tb("arow", [P, DNH]), tb("dtrow", [P, DNH])
        beta, g, sp_, sp2 = tb("beta", [P, TILES, DNH]), tb("g", [P, TILES, DNH]), tb("sp_", [P, TILES, DNH]), tb("sp2", [P, TILES, DNH])
        cum = tb("cum", [P, 3, TILES, DNH])
        ecum = tb("ecum", [P, 3, TILES, DNH])
        bcum = tb("bcum", [P, TILES, DNH])
        egl = tb("egl", [P, 2, PT, DNH])
        gbm, egls = tb("gbm", [P, NB, DNH]), tb("egls", [P, NB, DNH])
        wide = [P, 2, M4 * P]
        dm, egb, bt, qk, T, Y, Pm = [tb("w_" + x, wide) for x in ("dm", "egb", "bt", "qk", "T", "Y", "Pm")]
        kb, vb, kg = tb("kb", [P, 512]), tb("vb", [P, 512]), tb("kg", [P, 512])
        wT, qgT = tb("wT", [P, M4, P]), tb("qgT", [P, M4, P])
        U, vf = tb("U", [P, 512]), tb("vf", [P, 512])
        S, Sd = tb("S", [P, M4, HD]), tb("Sd", [P, M4, HD])
        Ss = tb("Ss", [P, NB, M4, HD])
        osq, oss = tb("osq", [P, 512]), tb("oss", [P, 2, DNH])
        qgm = tb("qgm", [P, M4, NB * 72])
        xcf = m.xc[:, :, :].rearrange("p c n -> p (c n)")
        vm = xcf[:, 0:NB * 512].rearrange("p (b n) -> p b n", b=NB)
        wm = xcf[:, NB * 512:NB * 512 + M4 * NB * 72].rearrange("p (m n) -> p m n", m=M4)
        block = ctx.enter_context(nc.Block())
        sd = t["state_delta"][0]
        o = lambda i: m.kvt[:, i, 0:512]
        bc = lambda a: a.unsqueeze(2).to_broadcast([P, DNH, HD])
        r3 = lambda a: a.rearrange("p (h d) -> p h d", d=HD)
        pairs = lambda a: a.rearrange("p e (m n) -> p e m n", n=P)
        by_head = lambda a: a.rearrange("p (m e) -> p e m", e=2).unsqueeze(3).to_broadcast([P, 2, M4, P])
        every = lambda a, n: a.unsqueeze(1).to_broadcast([P, n, P])

        @block.sync
        def _(sp):
            sp.dma_start(arow[:, :], t["dn_a_log"][0].partition_broadcast(P)).then_inc(st_in, 16)
            sp.dma_start(dtrow[:, :], t["dn_dt_bias"][0].partition_broadcast(P)).then_inc(st_in, 16)
            for e in range(2):
                sp.dma_start(Ss[e * HD:(e + 1) * HD].rearrange("p b m v -> p (b m) v"),
                             sd.rearrange("b (m e) k v -> e k (b m) v", e=2)[e]).then_inc(st_in, 16)
            sp.wait_ge(s_ok, C2)
            for e in range(2):
                sp.dma_start(outs[8][0, 0].rearrange("(m e) k v -> e k m v", e=2)[e], S[e * HD:(e + 1) * HD]).then_inc(sto, 16)
            sp.wait_ge(s_ok, C2 + 2 * M4)
            for e in range(2):
                sp.dma_start(outs[16][0].rearrange("b (m e) k v -> e k (b m) v", e=2)[e],
                             Ss[e * HD:(e + 1) * HD].rearrange("p b m v -> p (b m) v")).then_inc(sto, 16)
            sp.wait_ge(sto, 64)

        @block.gpsimd
        def _(pool):
            G_ = nc.gpsimd
            link = Chain(pool, pchain)
            pool.wait_ge(mask_ok, 2)
            for i in range(TILES):
                v = VAR[i]
                if i:
                    pool.wait_ge(lt_ps, 2 * before(i))
                G_.tensor_copy(pairs(Pm[:, :, :]), by_head(g[:, i, :])).then_inc(spread, 1)
                G_.tensor_copy(pairs(T[:, :, :]), by_head(beta[:, i, :])).then_inc(spread, 1)
                if i == 0:
                    pool.wait_ge(cum_ok, 1)
                else:
                    pool.wait_ge(qk_ok, i)
                G_.tensor_tensor(pairs(dm[:, :, :]), by_head(cum[:, 0, i, :]),
                                 m.upneg[:, v, :].unsqueeze(1).unsqueeze(1).to_broadcast([P, 2, M4, P]), ALU.subtract).then_inc(cn_ok, 1)
                if i == 0:
                    link(G_.memset(qgm[:, :, :], 0.0))
                    G_.memset(wm[:, :, :], 0.0).then_inc(zero_ok, 1)
                    pool.wait_ge(eg_ok, 3)
                    link(G_.tensor_tensor(bcum[:, :, :], beta[:, :, :], ecum[:, 0], ALU.mult))
                else:
                    pool.wait_ge(wu_ps, i)
                k3, v3 = r3(m.kvt[:, i, 0:512]), r3(m.kvt[:, i, 512:1024])
                link(G_.tensor_tensor(r3(kb[:, :]), k3, bc(bcum[:, i, :]), ALU.mult))
                G_.tensor_tensor(r3(vb[:, :]), v3, bc(beta[:, i, :]), ALU.mult).then_inc(kb_ok, 1)
                if i:
                    pool.wait_ge(so_ps, scans(i))
                G_.tensor_tensor(r3(kg[:, :]), k3, bc(ecum[:, 2, i, :]), ALU.mult).then_inc(kg_ok, 1)
                pool.wait_ge(egb_ok, i + 1)
                pool.wait_ge(kg_ok, i + 1)
                for e in range(2):
                    rows = slice(e * HD, (e + 1) * HD)
                    last = G_.tensor_tensor(qgT[rows, :, :], m.yT[rows, 0:M4, i * P:(i + 1) * P], egb[rows, e, :].rearrange("p (m n) -> p m n", n=P), ALU.mult)
                    if e == 0 or v == 1:
                        link(last)
                    if v == 1:
                        last = G_.tensor_copy(qgm[rows, :, :].rearrange("p m (b x) -> p m b x", x=72)[:, :, :, 0:TS],
                                              qgT[rows, :, 0:NB * TS].rearrange("p m (b j) -> p m b j", j=TS))
                        if e == 0:
                            link(last)
                last.then_inc(qg_ok, 1)
                pool.wait_ge(qg_ok, i + 1)

        @block.scalar
        def _(act):
            link = Chain(act, gates_a)
            act.wait_ge(st_in, 16 * 4)
            act.wait_ge(gch, 3)
            link(nc.scalar.activation(beta[:, :, :], m.z[:, :, Z_B:Z_B + DNH], ACT.Exp, scale=-1.0))
            link(nc.scalar.activation(sp2[:, :, :], sp2[:, :, :], ACT.Exp, scale=-1.0))
            link(nc.scalar.activation(arow[:, :], arow[:, :], ACT.Exp))
            link(nc.scalar.activation(sp2[:, :, :], sp2[:, :, :], ACT.Ln, bias=m.eps[:, 2:3]))
            act.wait_ge(cum_ok, 1)
            nc.scalar.activation(ecum[:, :, :, :], cum[:, :, :, :], ACT.Exp).then_inc(eg_ok, 1)
            nc.scalar.activation(egl[:, :, :, :], egl[:, :, :, :], ACT.Exp).then_inc(eg_ok, 1)
            nc.scalar.activation(egls[:, :, :], egls[:, :, :], ACT.Exp).then_inc(eg_ok, 1)

            def query_decay(i):
                act.wait_ge(gb_ps, i + 1)
                if i:
                    act.wait_ge(qg_ok, i)
                nc.scalar.activation(egb[:, :, :], PS[:, 0:2, :], ACT.Exp).then_inc(egb_ok, 1)

            def pair_decay(i):
                act.wait_ge(d_in, i + 1)
                nc.scalar.activation(dm[:, :, :], dm[:, :, :], ACT.Exp).then_inc(d_exp, 1)

            def take_out(i, n, r):
                act.wait_ge(so_ps, n + 1)
                act.wait_ge(kg_ok, i + 1)
                for e in range(2):
                    last = nc.scalar.copy(heads_em(o(i)[r, :])[:, e], PS[r, 6 + e, 0:256].rearrange("p (m x) -> p m x", x=HD))
                last.then_inc(o_ok, 1)

            def square(i):
                if i:
                    act.wait_ge(o_ss, i)
                act.wait_ge(o_ok, scans(i + 1))
                nc.scalar.activation(osq[:, :], o(i), ACT.Square).then_inc(o_sq, 1)
                act.wait_ge(o_ss, i + 1)
                nc.scalar.activation(oss[:, 1, :], oss[:, 0, :], ACT.Sqrt, scale=1.0 / HD, bias=m.eps[:, 0:1]).then_inc(o_rt, 1)

            def out_T(i):
                w = ROWS[i]
                act.wait_ge(o_ps, i + 1)
                nc.scalar.copy(m.mixT[:, M4:2 * M4, i * P:i * P + w], PS[:, 0, :].rearrange("p (c n) -> p c n", n=P)[:, :, 0:w]).then_inc(o_T, 1)

            query_decay(0)
            pair_decay(0)
            for i in range(TILES):
                if i:
                    square(i - 1)
                    out_T(i - 1)
                act.wait_ge(wu_ps, i + 1)
                nc.scalar.copy(U[:, :], PS[:, 2, :]).then_inc(u_ok, 1)
                if i < PT:
                    query_decay(i + 1)
                    take_out(i, 2 * i, slice(0, HD))
                    pair_decay(i + 1)
                    take_out(i, 2 * i + 1, slice(HD, P))
                else:
                    take_out(i, C2, slice(0, NB * TS))
            square(PT)
            out_T(PT)

        @block.vector
        def _(dve):
            link = Chain(dve, chain)
            V = nc.vector
            al = m.z[:, :, Z_A:Z_A + DNH]
            dve.wait_ge(st_in, 16 * 4)
            link(V.tensor_tensor(sp_[:, :, :], al, dtrow[:, :].unsqueeze(1).to_broadcast([P, TILES, DNH]), ALU.add))
            V.tensor_scalar(sp2[:, :, :], sp_[:, :, :], -1.0, None, ALU.mult).then_inc(gch, 1)
            dve.wait_ge(gch, 1)
            V.tensor_tensor(sp2[:, :, :], sp2[:, :, :], sp_[:, :, :], ALU.max).then_inc(gch, 1)
            dve.wait_ge(gch, 2)
            V.tensor_scalar(sp_[:, :, :], sp_[:, :, :], 0.0, None, ALU.max).then_inc(gch, 1)
            dve.wait_ge(gates_a, 4)
            link(V.tensor_tensor(g[:, :, :], sp_[:, :, :], sp2[:, :, :], ALU.add))
            link(V.tensor_tensor(g[:, :, :], g[:, :, :], arow[:, :].unsqueeze(1).to_broadcast([P, TILES, DNH]), ALU.mult))
            link(V.tensor_scalar(g[:, :, :], g[:, :, :], -1.0, None, ALU.mult))
            link(V.memset(g[NB * TS:P, PT, :], 0.0))
            link(V.tensor_scalar(beta[:, :, :], beta[:, :, :], 1.0, None, ALU.add))
            V.reciprocal(beta[:, :, :], beta[:, :, :]).then_inc(mask_ok, 1)
            V.tensor_tensor(gbm[:, :, :], m.bmask[:, :].unsqueeze(2).to_broadcast([P, NB, DNH]),
                            g[:, PT, :].unsqueeze(1).to_broadcast([P, NB, DNH]), ALU.mult).then_inc(mask_ok, 1)
            dve.wait_ge(cum_ps, 1)
            flat = lambda a: a.rearrange("p i h -> p (i h)")
            link(V.tensor_copy(cum[:, 0:2].rearrange("p a i h -> p (a i h)"), PS[:, 6, 0:80]))
            link(V.tensor_copy(egl[:, :, :, :].rearrange("p c i h -> p (c i h)"), PS[:, 6, 80:144]))
            link(V.tensor_copy(flat(egls[:, :, :]), PS[:, 6, 144:208]))
            V.tensor_tensor(cum[:, 2], cum[:, 1], cum[:, 0], ALU.subtract).then_inc(cum_ok, 1)
            link(V.memset(S[:, :, :], 0.0))
            link(V.memset(vf[:, :], 0.0))

            def pair_decay(i):
                dve.wait_ge(egb_ok, i + 1)
                dve.wait_ge(cn_ok, i + 1)
                V.tensor_tensor(dm[:, :, :], PS[:, 0:2, :], dm[:, :, :], ALU.subtract).then_inc(d_in, 1)

            def couplings(i):
                dve.wait_ge(d_exp, i + 1)
                dve.wait_ge(bi_ps, i + 1)
                link(V.tensor_tensor(bt[:, :, :], PS[:, 4:6, :], dm[:, :, :], ALU.mult))
                dve.wait_ge(kk_ps, i + 1)
                V.tensor_tensor(bt[:, :, :], PS[:, 2:4, :], bt[:, :, :], ALU.mult).then_inc(bt_ok, 1)

            def query_keys(i):
                dve.wait_ge(qk_ps, i + 1)
                if i:
                    dve.wait_ge(so_ps, scans(i))
                V.tensor_tensor(qk[:, :, :], PS[:, 0:2, :], dm[:, :, :], ALU.mult).then_inc(qk_ok, 1)

            def norm(i, part):
                if part == 0:
                    dve.wait_ge(o_sq, i + 1)
                    V.reduce_sum(oss[:, 0, :], r3(osq[:, :]), AX).then_inc(o_ss, 1)
                elif part == 1:
                    dve.wait_ge(o_rt, i + 1)
                    link(V.reciprocal(oss[:, 1, :], oss[:, 1, :]))
                    link(V.tensor_tensor(r3(o(i)), r3(o(i)), bc(oss[:, 1, :]), ALU.mult))
                else:
                    V.tensor_tensor(o(i), o(i), m.z[:, i, Z_DG:Z_DG + 512], ALU.mult).then_inc(o_fin, 1)

            def levels(i):
                for l in range(LEVELS[i]):
                    n = before(i) + l
                    for e in range(2):
                        dve.wait_ge(lp_ps, 2 * n + e + 1)
                        V.tensor_tensor(Pm[:, e, :].rearrange("p (m n) -> p m n", n=P), PS[:, 2 + e, :].rearrange("p (m n) -> p m n", n=P),
                                        every(m.level[:, l, :], M4), ALU.mult).then_inc(lp_ok, 1)
                    if l == 0:
                        dve.wait_ge(lp_ok, 2 * n + 2)
                        V.tensor_tensor(T[:, :, :].rearrange("p e (m n) -> p (e m) n", n=P), every(m.ident[:, :], DNH),
                                        Pm[:, :, :].rearrange("p e (m n) -> p (e m) n", n=P), ALU.subtract)
                    if l == 1:
                        query_keys(i)
                    if i and 0 <= l - (LEVELS[i] - 3) < 3:
                        norm(i - 1, l - (LEVELS[i] - 3))
                    for e in range(2):
                        dve.wait_ge(lt_ps, 2 * n + e + 1)
                        if l == 0:
                            V.tensor_tensor(Y[:, e, :].rearrange("p (m n) -> p m n", n=P), every(m.ident[:, :], M4),
                                            PS[:, 6 + e, :].rearrange("p (m n) -> p m n", n=P), ALU.subtract).then_inc(lt_ok, 1)
                        else:
                            if l < LEVELS[i] - 1:
                                V.tensor_tensor(T[:, e, :], T[:, e, :], PS[:, 4 + e, :], ALU.subtract)
                            V.tensor_tensor(Y[:, e, :], Y[:, e, :], PS[:, 6 + e, :], ALU.subtract).then_inc(lt_ok, 1)

            pair_decay(0)
            couplings(0)
            for i in range(TILES):
                levels(i)
                dve.wait_ge(wu_ps, i + 1)
                if i == PT:
                    dve.wait_ge(zero_ok, 1)
                for e in range(2):
                    rows = slice(e * HD, (e + 1) * HD)
                    src = PS[rows, e, :].rearrange("p (m n) -> p m n", n=P)
                    last = V.tensor_copy(wT[rows, :, :], src)
                    if i == PT:
                        last = V.tensor_copy(wm[rows, :, :].rearrange("p m (b x) -> p m b x", x=72)[:, :, :, 0:TS],
                                             src[:, :, 0:NB * TS].rearrange("p m (b j) -> p m b j", j=TS))
                last.then_inc(w_ok, 1)
                if i < PT:
                    for c in range(2):
                        n = 2 * i + c
                        r = slice(c * HD, (c + 1) * HD)
                        if n:
                            dve.wait_ge(so_ps, n)
                        link(V.memset(vf[(1 - c) * HD:(2 - c) * HD, :], 0.0))
                        if i == 0 and c == 0:
                            dve.wait_ge(eg_ok, 3)
                        for e in range(2):
                            rows = slice(e * HD, (e + 1) * HD)
                            last = V.tensor_tensor(Sd[rows], S[rows], egl[rows, c, i, e::2].unsqueeze(2).to_broadcast([HD, M4, HD]), ALU.mult)
                        link(last)
                        dve.wait_ge(ws_ps, n + 1)
                        dve.wait_ge(u_ok, i + 1)
                        V.tensor_tensor(vf[r, :].rearrange("p (e x) -> p e x", e=2), U[r, :].rearrange("p (e x) -> p e x", e=2), PS[r, 4:6, 0:256], ALU.subtract).then_inc(v_ok, 1)
                        dve.wait_ge(sk_ps, n + 1)
                        for e in range(2):
                            rows = slice(e * HD, (e + 1) * HD)
                            last = V.tensor_tensor(S[rows], Sd[rows], PS[rows, 3, :].rearrange("p (m x) -> p m x", x=P)[:, :, e * HD:(e + 1) * HD], ALU.add)
                        last.then_inc(s_ok, 1)
                        if c == 0:
                            pair_decay(i + 1)
                        else:
                            couplings(i + 1)
                else:
                    r = slice(0, NB * TS)
                    dve.wait_ge(so_ps, C2)
                    link(V.memset(vf[NB * TS:P, :], 0.0))
                    dve.wait_ge(ws_ps, C2 + 1)
                    dve.wait_ge(u_ok, i + 1)
                    V.tensor_tensor(vf[r, :].rearrange("p (e x) -> p e x", e=2), U[r, :].rearrange("p (e x) -> p e x", e=2), PS[r, 4:6, 0:256], ALU.subtract).then_inc(v_ok, 1)
                    dve.wait_ge(v_ok, C2 + 1)
                    V.tensor_tensor(vm[:, :, :], vf[:, :].unsqueeze(1).to_broadcast([P, NB, 512]),
                                    m.bmask[:, :].unsqueeze(2).to_broadcast([P, NB, 512]), ALU.mult).then_inc(vm_ok, 1)
                    dve.wait_ge(so_ps, C2 + 1)
                    for e in range(2):
                        rows = slice(e * HD, (e + 1) * HD)
                        link(V.tensor_tensor(Ss[rows], Ss[rows], egls[rows, :, e::2].unsqueeze(3).to_broadcast([HD, NB, M4, HD]), ALU.mult))
                    for mm in range(M4):
                        dve.wait_ge(su_ps, mm + 1)
                        for e in range(2):
                            rows = slice(e * HD, (e + 1) * HD)
                            V.tensor_tensor(Ss[rows, :, mm, :], Ss[rows, :, mm, :],
                                            PS[rows, 2 * (mm % 2):2 * (mm % 2) + 2, :].rearrange("p a (b x) -> p (a b) x", x=P)[:, :, e * HD:(e + 1) * HD],
                                            ALU.add).then_inc(s_ok, 1)
                    for part in range(3):
                        norm(PT, part)

        @block.tensor
        def _(pe):
            MM = nc.tensor.matmul
            col = lambda mm: slice(mm * P, (mm + 1) * P)
            wide_cols = lambda x: x.rearrange("p i h -> p (i h)")
            heads = [(h, h % 2, h // 2, slice(h % 2 * HD, (h % 2 + 1) * HD)) for h in range(DNH)]
            pe.wait_ge(mask_ok, 2)
            gp, gs = wide_cols(g[:, 0:PT, :]), g[:, PT, :]
            np_ = PT * DNH
            for a, mask in enumerate((m.upinc, m.same)):
                MM(PS[:, 6, 40 * a:40 * a + np_], mask[:, 0, :], gp, start=True, stop=True)
                MM(PS[:, 6, 40 * a + np_:40 * (a + 1)], mask[:, 1, :], gs, start=True, stop=True)
            for c in range(2):
                MM(PS[:, 6, 80 + np_ * c:80 + np_ * (c + 1)], m.chunk[:, c, :], gp, start=True, stop=True)
            MM(PS[:, 6, 144:208], m.ones[:, :], gbm[:, :, :].rearrange("p b h -> p (b h)"), start=True, stop=True).then_inc(cum_ps, 1)

            def spread_beta(i):
                pe.wait_ge(spread, 2 * i + 2)
                for h, e, mm, rows in heads:
                    last = MM(PS[:, 4 + e, col(mm)], T[:, e, col(mm)], m.ident[:, :], start=True, stop=True)
                last.then_inc(bi_ps, 1)

            def spread_sums(i):
                pe.wait_ge(spread, 2 * i + 1)
                for h, e, mm, rows in heads:
                    last = MM(PS[:, e, col(mm)], Pm[:, e, col(mm)], m.upinc[:, VAR[i], :], start=True, stop=True)
                last.then_inc(gb_ps, 1)

            def key_products(i):
                tok = slice(i * P, (i + 1) * P)
                if i:
                    pe.wait_ge(u_ok, i)
                for h, e, mm, rows in heads:
                    kT = m.yT[rows, M4 + mm, tok]
                    last = MM(PS[:, 2 + e, col(mm)], kT, kT, start=True, stop=True)
                last.then_inc(kk_ps, 1)

            def query_products(i):
                tok = slice(i * P, (i + 1) * P)
                pe.wait_ge(egb_ok, i + 1)
                pe.wait_ge(d_in, i + 1)
                for h, e, mm, rows in heads:
                    last = MM(PS[:, e, col(mm)], m.yT[rows, M4 + mm, tok], m.yT[rows, mm, tok], start=True, stop=True)
                last.then_inc(qk_ps, 1)

            def turn_out(i):
                pe.wait_ge(o_fin, i + 1)
                if i == PT:
                    pe.wait_ge(s_ok, C2 + 2 * M4)
                for c in range(M4):
                    last = nc.tensor.transpose(PS[:, 0, col(c)], o(i)[:, col(c)], m.ident[:, :])
                last.then_inc(o_ps, 1)

            def levels(i):
                pe.wait_ge(bt_ok, i + 1)
                for l in range(LEVELS[i]):
                    n = before(i) + l
                    for e in range(2):
                        if l:
                            pe.wait_ge(lt_ok, 2 * n - 1 + e)
                        for mm in range(M4):
                            if l == 0:
                                last = nc.tensor.transpose(PS[:, 2 + e, col(mm)], bt[:, e, col(mm)], m.ident[:, :])
                            else:
                                last = MM(PS[:, 2 + e, col(mm)], bt[:, e, col(mm)], T[:, e, col(mm)], start=True, stop=True)
                        last.then_inc(lp_ps, 1)
                    if l == 0 and i:
                        pe.wait_ge(o_ok, scans(i))
                    for e in range(2):
                        pe.wait_ge(lp_ok, 2 * n + e + 1)
                        for mm in range(M4):
                            if l == 0:
                                last = nc.tensor.transpose(PS[:, 6 + e, col(mm)], Pm[:, e, col(mm)], m.ident[:, :])
                            else:
                                if l < LEVELS[i] - 1:
                                    MM(PS[:, 4 + e, col(mm)], Y[:, e, col(mm)], Pm[:, e, col(mm)], start=True, stop=True)
                                last = MM(PS[:, 6 + e, col(mm)], Pm[:, e, col(mm)], Y[:, e, col(mm)], start=True, stop=True)
                        last.then_inc(lt_ps, 1)

            spread_sums(0)
            spread_beta(0)
            key_products(0)
            query_products(0)
            for i in range(TILES):
                levels(i)
                pe.wait_ge(kb_ok, i + 1)
                pe.wait_ge(qk_ok, i + 1)
                if i:
                    turn_out(i - 1)
                pe.wait_ge(lt_ok, 2 * before(i + 1))
                for h, e, mm, rows in heads:
                    last = MM(PS[:, 2, (e * M4 + mm) * HD:(e * M4 + mm + 1) * HD], Y[:, e, col(mm)], vb[:, h * HD:(h + 1) * HD], start=True, stop=True)
                if i:
                    pe.wait_ge(o_T, i)
                for h, e, mm, rows in heads:
                    last = MM(PS[:, e, col(mm)], kb[:, mm * P:(mm + 1) * P], Y[:, e, col(mm)], start=True, stop=True)
                last.then_inc(wu_ps, 1)
                pe.wait_ge(w_ok, i + 1)
                if i < PT:
                    for c in range(2):
                        n = 2 * i + c
                        if n:
                            pe.wait_ge(s_ok, n)
                        for h, e, mm, rows in heads:
                            last = MM(PS[:, 4 + e, mm * HD:(mm + 1) * HD], wT[rows, mm, :], S[rows, mm, :], start=True, stop=True)
                        last.then_inc(ws_ps, 1)
                        pe.wait_ge(qg_ok, i + 1)
                        if n:
                            pe.wait_ge(o_ok, n)
                        for h, e, mm, rows in heads:
                            MM(PS[:, 6 + e, mm * HD:(mm + 1) * HD], qgT[rows, mm, :], S[rows, mm, :], start=(mm == 0), stop=False, skip_group_check=True)
                        if c == 0:
                            spread_sums(i + 1)
                        pe.wait_ge(kg_ok, i + 1)
                        pe.wait_ge(v_ok, n + 1)
                        for mm in range(M4):
                            last = MM(PS[:, 3, col(mm)], kg[:, col(mm)], vf[:, :].rearrange("p (e m x) -> p m e x", e=2, m=M4)[:, mm], start=True, stop=True)
                        last.then_inc(sk_ps, 1)
                        if c == 1:
                            spread_beta(i + 1)
                            pe.wait_ge(s_ok, n + 1)
                            key_products(i + 1)
                        for h, e, mm, rows in heads:
                            last = MM(PS[:, 6 + e, mm * HD:(mm + 1) * HD], qk[:, e, col(mm)], vf[:, (e * M4 + mm) * HD:(e * M4 + mm + 1) * HD],
                                      start=False, stop=True, skip_group_check=True)
                        last.then_inc(so_ps, 1)
                    query_products(i + 1)
                else:
                    R = NB * TS
                    for h, e, mm, rows in heads:
                        for b in range(NB):
                            last = MM(PS[0:R, 4 + e, mm * HD:(mm + 1) * HD], wm[rows, mm, b * R:(b + 1) * R], Ss[rows, b, mm, :], start=(b == 0), stop=(b == NB - 1))
                    last.then_inc(ws_ps, 1)
                    pe.wait_ge(qg_ok, i + 1)
                    pe.wait_ge(v_ok, C2 + 1)
                    for h, e, mm, rows in heads:
                        dst = PS[0:R, 6 + e, mm * HD:(mm + 1) * HD]
                        for b in range(NB):
                            MM(dst, qgm[rows, mm, b * R:(b + 1) * R], Ss[rows, b, mm, :], start=(b == 0), stop=False)
                        last = MM(dst, qk[:, e, mm * P:mm * P + R], vf[:, (e * M4 + mm) * HD:(e * M4 + mm + 1) * HD], start=False, stop=True)
                    last.then_inc(so_ps, 1)
                    pe.wait_ge(kg_ok, i + 1)
                    pe.wait_ge(vm_ok, 1)
                    pe.wait_ge(u_ok, i + 1)
                    for mm in range(M4):
                        if mm >= 2:
                            pe.wait_ge(s_ok, C2 + 2 * (mm - 1))
                        for half in range(2):
                            last = MM(PS[:, 2 * (mm % 2) + half, :], kg[:, col(mm)],
                                      vm[:, 4 * half:4 * half + 4, :].rearrange("p b (e m x) -> p m b e x", e=2, m=M4)[:, mm], start=True, stop=True)
                        last.then_inc(su_ps, 1)
            turn_out(PT)


NHC = CMP_HIDDEN // P
LP = CMP_LEN // 2
NPAIR = PAST // 2
assert (NCMP - 1) * CMP_STRIDE + CMP_LEN <= PAST
CMP_K, SEL_K, WIN_K = 0, 1, 0
NCOL = NSEQ * NCMP


def load_pages(nc, eng, part, pt_sb, pool_rows, dst, done):
    with nc.Fori(part * NB // 2, (part + 1) * NB // 2, engines=[eng.engine]) as b:
        for pg in range(PAGES):
            page = eng.value_load(pt_sb[0:1, bass.ds(b * PAGES + pg, 1)], min_val=0, max_val=NPOOL - 1)
            eng.dma_start(dst[:, bass.ds(b * PAGES + pg, 1), :].rearrange("p o n -> p (o n)"),
                          pool_rows[0, bass.ds(page, 1)].rearrange("o p k d -> (o p) (k d)")).then_inc(done, 16)


def stage_compress(nc, m, sb, sem, t, outs):
    PS = m.PS
    pt_in, raw_in, w_in = sem("c_pt_in"), [sem(f"c_raw_in{s}") for s in range(2)], [sem(f"c_w_in{s}") for s in range(2)]
    sel_in, win_in, bias_in = sem("sel_in"), sem("win_in"), sem("bias_in1")
    pos_ps, pos_ok, tr_ps, tr_a, tr_v = sem("pos_ps"), sem("pos_ok"), sem("tr_ps"), sem("tr_a"), sem("tr_v")
    hid_ps, hb_ok, hid_ok, out_ps, out_ok = sem("hid_ps"), sem("hb_ok"), sem("hid_ok"), sem("out_ps"), sem("out_ok")
    with ExitStack() as ctx:
        def tb(name, shape, dt=F32):
            return ctx.enter_context(nc.sbuf_tensor(name, shape, dt))
        pt = tb("pt", [1, NB * PAGES], I32)
        raw = (m.pages[:, CMP_K], tb("cmp_v_pages", [P, NB * PAGES, P])[:, :, :])
        xT = tb("xT", [P, 2, NSEQ, NPAIR])
        w1 = tb("w1", [P, LP, CMP_HIDDEN])
        w1v = tb("w1v", [P, LP, CMP_HIDDEN])
        w2 = tb("w2", [P, NHC, 2 * HD])
        w2v = tb("w2v", [P, NHC, HD])
        pos = tb("cmp_pos", [LP, 2, P])
        posT = tb("posT", [P, 2, LP])
        hb = tb("hb", [P, 2, NHC])
        hid = m.z[:, :, ZA:]
        W1 = (w1, w1v)
        NU = NSEQ
        block = ctx.enter_context(nc.Block())
        pools = [t["cache_cmp_k"], t["cache_cmp_v"]]

        def pages(eng, part):
            eng.wait_ge(pt_in, 16)
            for s in range(2):
                load_pages(nc, eng, part, pt, pools[s], raw[s], raw_in[s])

        @block.sync
        def _(sp):
            sp.dma_start(pt[:, :], t["page_table"].rearrange("b p -> (b p)").unsqueeze(0)).then_inc(pt_in, 16)
            for s in range(2):
                sp.dma_start(pos[:, s, :], t["cmp_pos_k" if s == 0 else "cmp_pos_v"][0].rearrange("(l e) d -> l (e d)", e=2)).then_inc(w_in[0], 16)
            for s in range(2):
                sp.dma_start(W1[s][:, :, :], t["cmp_w1_k" if s == 0 else "cmp_w1_v"][0].rearrange("(l p) n -> p l n", p=P)).then_inc(w_in[s], 16)
            w2k = t["cmp_w2_k"][0].rearrange("(c p) d -> p c d", p=P)
            sp.dma_start(w2[:, :, 0:HD], w2k).then_inc(w_in[1], 16)
            sp.dma_start(w2[:, :, HD:2 * HD], w2k).then_inc(w_in[1], 16)
            sp.dma_start(w2v[:, :, :], t["cmp_w2_v"][0].rearrange("(c p) d -> p c d", p=P)).then_inc(w_in[1], 16)
            pages(sp, 0)
            for s, name in enumerate(("cache_sel_k", "cache_sel_v")):
                for part in range(2):
                    load_pages(nc, sp, part, pt, t[name], m.pages[:, SEL_K] if s == 0 else m.V[:, 0], sel_in)
            sp.wait_ge(sel_in, 16 * NB * PAGES * 2)

        @block.gpsimd
        def _(pool):
            window = lambda name: t[name][0].rearrange("b (g p) k d -> p (b g) (k d)", p=P)
            pool.dma_start(m.V[:, 1], window("cache_win_v")).then_inc(win_in, 16)
            for r in range(2):
                for v in range(2):
                    for h in range(H):
                        pool.dma_start(m.biasS[64 * r + TS * h:64 * r + TS * h + TS, v, :],
                                       bass.AP(m.rb_rep, v * P * H * RB_W + h * RB_W + RB_C - PAST, [[H * RB_W - 1, TS], [1, LS]])).then_inc(bias_in, 16)
            pool.dma_start(m.Vn[:, 0], outs[13][0].rearrange("b s k d -> s b (k d)")).then_inc(win_in, 16)
            pool.dma_start(m.Vn[:, 1], outs[15][0, :, PAST - TS:PAST].rearrange("b s k d -> s b (k d)")).then_inc(win_in, 16)
            pool.wait_ge(tr_ps, NU)
            pool.dma_start(m.pages[:, WIN_K], window("cache_win_k")).then_inc(win_in, 16)
            pool.wait_ge(win_in, 64)
            pool.wait_ge(bias_in, 16 * 32)

        def evacuate(copy, v, u, done):
            for e in range(2):
                last = copy(xT[e * HD:(e + 1) * HD, v, u % NU, :], PS[v * HD:(v + 1) * HD, u % 4, e::2])
            last.then_inc(done, 1)

        @block.tensor
        def _(pe):
            MM = nc.tensor.matmul
            pe.wait_ge(w_in[0], 16 * 3)
            for s in range(2):
                last = nc.tensor.transpose(PS[:, 7, s * LP:(s + 1) * LP], pos[:, s, :], m.ident[0:LP, 0:LP])
            last.then_inc(pos_ps, 1)
            pe.wait_ge(pos_ok, 1)
            for s in range(2):
                if s == 1:
                    pe.wait_ge(w_in[1], 16 * 4)
                for c in range(NHC):
                    for l in range(LP):
                        last = MM(PS[:, 6, s * NHC + c:s * NHC + c + 1], W1[s][:, l, c * P:(c + 1) * P], posT[:, s, l:l + 1], start=(l == 0), stop=(l == LP - 1))
            last.then_inc(pos_ps, 1)
            for s in range(2):
                for n in range(NU):
                    u = s * NU + n
                    if u >= 4:
                        pe.wait_ge(tr_v, u - 3)
                        pe.wait_ge(tr_a, u - 3)
                    if n == 1:
                        pe.wait_ge(raw_in[s], 16 * NB * PAGES)
                    for j in range(4):
                        src = m.z[:, j, s * P:(s + 1) * P] if n == 0 else raw[s][:, (n - 1) * PAGES + j, :]
                        last = nc.tensor.transpose(PS[:, u % 4, j * P:(j + 1) * P], src, m.ident[:, :])
                    last.then_inc(tr_ps, 1)
                if s == 1:
                    pe.wait_ge(hid_ok, KV * NHC)
                    pe.wait_ge(hb_ok, 1)
                    for v in range(KV):
                        for c in range(NHC):
                            last = MM(PS[:, 6 + v, 0:NCOL], w2[:, c, :], hid[:, v * NHC + c, 0:NCOL], start=(c == 0), stop=(c == NHC - 1))
                    last.then_inc(out_ps, 1)
                pe.wait_ge(tr_v, (s + 1) * NU)
                pe.wait_ge(tr_a, (s + 1) * NU)
                for v in range(KV):
                    for c in range(NHC):
                        u = (s * KV + v) * NHC + c
                        if u >= 2:
                            pe.wait_ge(hid_ok, u - 1)
                        for l in range(LP):
                            last = MM(PS[:, 4 + u % 2, 0:NCOL], W1[s][:, l, c * P:(c + 1) * P],
                                      xT[:, v, :, l:l + (CMP_STRIDE // 2) * (NCMP - 1) + 1:CMP_STRIDE // 2], start=(l == 0), stop=(l == LP - 1))
                        last.then_inc(hid_ps, 1)
            pe.wait_ge(hid_ok, 2 * KV * NHC)
            for q in range(NSEQ):
                for v in range(KV):
                    for c in range(NHC):
                        last = MM(PS[0:NCMP, 2 + q // 4, (q % 4) * P + v * HD:(q % 4) * P + (v + 1) * HD], hid[:, v * NHC + c, q * NCMP:(q + 1) * NCMP], w2v[:, c, :],
                                  start=(c == 0), stop=(c == NHC - 1))
            last.then_inc(out_ps, 1)

        @block.scalar
        def _(act):
            pages(act, 1)
            for s in range(2):
                for n in range(NU):
                    act.wait_ge(tr_ps, s * NU + n + 1)
                    if s == 1 and n == 0:
                        act.wait_ge(hid_ps, KV * NHC)
                    evacuate(nc.scalar.copy, 1, s * NU + n, tr_a)
                if s == 0:
                    act.wait_ge(hb_ok, 1)
                else:
                    act.wait_ge(out_ps, 1)
                for v in range(KV):
                    for c in range(NHC):
                        u = (s * KV + v) * NHC + c
                        act.wait_ge(hid_ps, u + 1)
                        nc.scalar.activation(hid[:, v * NHC + c, 0:NCOL], PS[:, 4 + u % 2, 0:NCOL], ACT.Silu, bias=hb[:, s, c:c + 1]).then_inc(hid_ok, 1)

        @block.vector
        def _(dve):
            dve.wait_ge(pos_ps, 1)
            nc.vector.tensor_copy(posT[:, :, :], PS[:, 7, 0:2 * LP].rearrange("p (s l) -> p s l", s=2)).then_inc(pos_ok, 1)
            dve.wait_ge(pos_ps, 2)
            nc.vector.tensor_copy(hb[:, :, :], PS[:, 6, 0:2 * NHC].rearrange("p (s c) -> p s c", s=2)).then_inc(hb_ok, 1)
            for s in range(2):
                for n in range(NU):
                    dve.wait_ge(tr_ps, s * NU + n + 1)
                    if s == 1 and n == 0:
                        dve.wait_ge(hid_ps, KV * NHC)
                    evacuate(nc.vector.tensor_copy, 0, s * NU + n, tr_v)
            dve.wait_ge(out_ps, 1)
            for v in range(KV):
                nc.vector.tensor_copy(m.kcT[v * HD:(v + 1) * HD, :], PS[v * HD:(v + 1) * HD, 6 + v, 0:NCOL])
            dve.wait_ge(out_ps, 2)
            nc.vector.tensor_copy(m.vc[:, :, :], PS[0:NCMP, 2:5, :].rearrange("p a (q n) -> p (a q) n", n=P)[:, 0:NSEQ, :]).then_inc(out_ok, 1)


def stage_keys(nc, m, sb, sem, t, outs):
    PS = m.PS
    bias_in = sem("bias_in2")
    k_ps, k_a, k_v = sem("k_ps"), sem("k_a"), sem("k_v")
    with ExitStack() as ctx:
        block = ctx.enter_context(nc.Block())
        units = [(br, q) for br in range(2) for q in range(NSEQ + 1)]

        @block.sync
        def _(sp):
            sp.dma_start(m.strip[:, :, :], bass.AP(m.rb_rep, RB_C - (SEQ - P), [[H * RB_W - 1, P], [RB_W, H], [1, STRIP]])).then_inc(bias_in, 16)
            sp.wait_ge(bias_in, 16)

        def evacuate(copy, n, done):
            br, q = units[n]
            bank = PS[:, n % 6, :]
            if q < NSEQ:
                copy(m.KT[:, br, q, 0:512], bank).then_inc(done, 1)
            else:
                copy(m.KT[:, br, 1:, PAST:], bank[:, 0:NB * TS].rearrange("p (b j) -> p b j", j=TS)).then_inc(done, 1)

        @block.tensor
        def _(pe):
            for n, (br, q) in enumerate(units):
                zc = 256 if br == 0 else 512
                if n >= 6:
                    pe.wait_ge(k_v if (n - 6) % 2 else k_a, (n - 6) // 2 + 1)
                if q == NSEQ:
                    last = nc.tensor.transpose(PS[:, n % 6, 0:NB * TS], m.z[0:NB * TS, PT, zc:zc + P], m.ident[0:NB * TS, 0:NB * TS])
                else:
                    for j in range(4):
                        src = m.z[:, j, zc:zc + P] if q == 0 else m.pages[:, (SEL_K, WIN_K)[br], (q - 1) * PAGES + j, :]
                        last = nc.tensor.transpose(PS[:, n % 6, j * P:(j + 1) * P], src, m.ident[:, :])
                last.then_inc(k_ps, 1)

        @block.scalar
        def _(act):
            for n in range(0, len(units), 2):
                act.wait_ge(k_ps, n + 1)
                evacuate(nc.scalar.copy, n, k_a)

        @block.vector
        def _(dve):
            for n in range(1, len(units), 2):
                dve.wait_ge(k_ps, n + 1)
                evacuate(nc.vector.tensor_copy, n, k_v)


def stage_attention(nc, m, sb, sem, t, outs):
    PS = m.PS
    gate_out, gate_in, sg, qs_ok = sem("a_gate_out"), sem("a_gate_in"), sem("a_sg"), sem("a_qs_ok")
    s_ps, s_ok, mx_ok, e_ok, pt_ps, pt_a = [sem("a_" + x) for x in ("s_ps", "s_ok", "mx_ok", "e_ok", "pt_ps", "pt_a")]
    o_ps, o_ok, chain, pn_ok = [sem("a_" + x) for x in ("o_ps", "o_ok", "chain", "pn_ok")]
    CMP, SEL, WIN = 0, 1, 2
    units = [("p", br, v, i) for i in range(PT) for v in range(KV) for br in range(3)] + [("s", br, q, 0) for q in range(NB // 2) for br in range(3)]
    NPU = PT * KV * 3
    keys = []
    for kind, br, a, i in units:
        if br == CMP:
            keys.append([NCMP])
        elif kind == "p":
            keys.append([P] * (i + 1))
        else:
            keys.append([P] * 4 + [TS])
    ends = lambda u: units[u][1] == WIN and (units[u][0] == "s" or units[u][2] == KV - 1)
    pieces = []
    for s in range(len(units) + 2):
        if s >= 2 and ends(s - 2):
            pieces.append(("o", s - 2))
        if 1 <= s <= len(units):
            u = s - 1
            groups = [[j] for j in range(len(keys[u]))] if units[u][0] == "p" else [list(range(len(keys[u])))[:4], list(range(len(keys[u])))[4:]]
            pieces += [("k", u, g) for g in groups if g]
    of = lambda kind, u: [n for n, p in enumerate(pieces) if p[0] == kind and p[1] == u]

    with ExitStack() as ctx:
        def tb(name, shape):
            return ctx.enter_context(nc.sbuf_tensor(name, shape, F32))
        gate = tb("gate", [P, TILES, 24])
        gateS = tb("gateS", [P, NB // 2, 3])
        spare = [m.pages[:, x].rearrange("p j n -> p (j n)") for x in range(2)]
        pr = spare[0].rearrange("p (u n) -> p u n", u=2)
        pT = spare[1][:, 0:5 * 4 * P].rearrange("p (j n) -> p j n", j=5)
        Qs = spare[1][:, 5 * 4 * P:5 * 4 * P + NB * P].rearrange("p (b n) -> p b n", b=NB)
        mx, l, gr = tb("mx", [P, 2, 4]), tb("l", [P, 2, 4]), tb("gr", [P, 4])
        o, tmp = tb("o_att", [P, 2, 512]), tb("o_tmp", [P, 256])
        oS = tb("oS", [NB * TS, 2, 2, HD])
        block = ctx.enter_context(nc.Block())

        @block.sync
        def _(sp):
            sp.wait_ge(sg, 3)
            sp.dma_start(m.gate_dram.ap(), gate[0:NB * TS, PT, :]).then_inc(gate_out, 16)
            sp.wait_ge(gate_out, 16)
            for r in range(2):
                for h in range(H):
                    sp.dma_start(gateS[64 * r + TS * h:64 * r + TS * h + TS, :, :],
                                 m.gate_dram.ap().rearrange("(q r t) (h c) -> r h t q c", r=2, t=TS, c=3)[r, h]).then_inc(gate_in, 16)

        @block.scalar
        def _(act):
            gates = Chain(act, sg)
            gates(nc.scalar.activation(gate[:, :, :], m.z[:, :, Z_GL:Z_GL + 24], ACT.Exp, scale=-1.0))

            def softmax(u):
                kind, br, a, i = units[u]
                w = sum(keys[u])
                act.wait_ge(mx_ok, u + 1)
                if u >= 2:
                    act.wait_ge(pt_ps, of("k", u - 2)[-1] + 1)
                if kind == "p":
                    for g in range(G):
                        row = pr[:, u % 2, g * 512:g * 512 + w]
                        ins = nc.scalar.activation(row, row, ACT.Exp, bias=mx[:, u % 2, g:g + 1], accum_out=l[:, u % 2, g:g + 1])
                else:
                    row = pr[:, u % 2, 0:w]
                    ins = nc.scalar.activation(row, row, ACT.Exp, bias=mx[:, u % 2, 0:1], accum_out=l[:, u % 2, 0:1])
                ins.then_inc(e_ok, 1)

            def take_pieces(u):
                for n in of("k", u):
                    group = pieces[n][2]
                    kw = keys[u][group[0]]
                    act.wait_ge(pt_ps, n + 1)
                    if u:
                        act.wait_ge(o_ps, u)
                    if units[u][0] == "p":
                        nc.scalar.copy(pT[0:kw, group[0], :], PS[0:kw, 4 + n % 2, :]).then_inc(pt_a, 1)
                    else:
                        nc.scalar.copy(pT[0:kw, group[0]:group[-1] + 1, 0:P], PS[0:kw, 4 + n % 2, 0:len(group) * P].rearrange("p (j n) -> p j n", n=P)).then_inc(pt_a, 1)

            def take_outputs(u):
                kind, br, a, i = units[u]
                n = of("o", u)[0]
                act.wait_ge(pt_ps, n + 1)
                if kind == "p":
                    nc.scalar.copy(m.mixT[:, 0:4, i * P:(i + 1) * P], PS[:, 4 + n % 2, :].rearrange("p (c n) -> p c n", n=P)).then_inc(pt_a, 1)
                else:
                    for e in range(2):
                        rows = slice(e * HD, (e + 1) * HD)
                        last = nc.scalar.copy(m.mixT[rows, 0:4, SEQ + 2 * a * TS:SEQ + 2 * (a + 1) * TS].rearrange("p m (b t) -> p b m t", b=2),
                                              PS[rows, 4 + n % 2, 0:2 * NB * TS].rearrange("p (b m e t) -> p e b m t", b=2, e=2, t=TS)[:, e])
                    last.then_inc(pt_a, 1)

            for s in range(len(units) + 2):
                if s >= 2 and ends(s - 2):
                    take_outputs(s - 2)
                if 1 <= s <= len(units):
                    take_pieces(s - 1)
                if s < len(units):
                    softmax(s)

        @block.vector
        def _(dve):
            V = nc.vector
            link = Chain(dve, chain)
            link(V.memset(Qs[:, :, :], 0.0))
            for v in range(KV):
                rows = slice(v * HD, (v + 1) * HD)
                for r in range(2):
                    base = r * 64 + v * G * TS
                    src = m.qT[rows, :, SEQ:].rearrange("p g (q r t) -> p r q g t", r=2, t=TS)[:, r]
                    for q in range(NB // 2):
                        last = V.tensor_copy(Qs[rows, 2 * q + r, base:base + G * TS].rearrange("p (g t) -> p g t", g=G), src[:, q])
            last.then_inc(qs_ok, 1)
            dve.wait_ge(sg, 1)
            V.tensor_scalar(gate[:, :, :], gate[:, :, :], 1.0, None, ALU.add).then_inc(sg, 1)
            dve.wait_ge(sg, 2)
            V.reciprocal(gate[:, :, :], gate[:, :, :]).then_inc(sg, 1)
            dve.wait_ge(sg, 3)

            def scores(u):
                kind, br, a, i = units[u]
                w = sum(keys[u])
                dve.wait_ge(s_ps, u + 1)
                if u >= 2:
                    dve.wait_ge(pt_ps, of("k", u - 2)[-1] + 1)
                if kind == "p":
                    dst = pr[:, u % 2, :].rearrange("p (g n) -> p g n", g=G)[:, :, 0:w]
                    c = SEQ - P - i * P
                    b = m.strip[:, a * G:(a + 1) * G, c:c + w] if br != CMP else \
                        m.strip[:, a * G:(a + 1) * G, c + CMP_LEN - 1:c + CMP_LEN + CMP_STRIDE * (NCMP - 1):CMP_STRIDE]
                    V.scalar_tensor_tensor(out=dst, in0=PS[:, 0:4, 0:w], scalar=SCALE, in1=b, op0=ALU.mult, op1=ALU.add).then_inc(s_ok, 1)
                    dve.wait_ge(s_ok, u + 1)
                    link(V.tensor_reduce(mx[:, u % 2, :], dst, AX, ALU.max))
                    V.tensor_scalar(mx[:, u % 2, :], mx[:, u % 2, :], -1.0, None, ALU.mult).then_inc(mx_ok, 1)
                else:
                    dst = pr[:, u % 2, 0:w]
                    src = PS[:, 2 * (u % 2):2 * (u % 2) + 2, :].rearrange("p b n -> p (b n)")[:, 0:w]
                    b = m.biasS[:, 1 if br == WIN else 0, 0:w] if br != CMP else \
                        m.biasS[:, 0, CMP_LEN - 1:CMP_LEN + CMP_STRIDE * (NCMP - 1):CMP_STRIDE]
                    V.scalar_tensor_tensor(out=dst, in0=src, scalar=SCALE, in1=b, op0=ALU.mult, op1=ALU.add).then_inc(s_ok, 1)
                    dve.wait_ge(s_ok, u + 1)
                    link(V.tensor_reduce(mx[:, u % 2, 0:1], dst, AX, ALU.max))
                    V.tensor_scalar(mx[:, u % 2, 0:1], mx[:, u % 2, 0:1], -1.0, None, ALU.mult).then_inc(mx_ok, 1)

            def normalise_sample(u):
                kind, br, q, _ = units[u]
                dve.wait_ge(e_ok, u + 1)
                if u == NPU:
                    dve.wait_ge(gate_in, 16 * 2 * H)
                w = sum(keys[u])
                link(V.reciprocal(gr[:, 0:1], l[:, u % 2, 0:1]))
                link(V.tensor_tensor(gr[:, 1:2], gr[:, 0:1], gateS[:, q, br:br + 1], ALU.mult))
                V.tensor_scalar(pr[:, u % 2, 0:w], pr[:, u % 2, 0:w], gr[:, 1:2], None, ALU.mult).then_inc(pn_ok, 1)

            def outputs(u):
                kind, br, a, i = units[u]
                if kind == "p":
                    dve.wait_ge(e_ok, u + 1)
                    link(V.reciprocal(gr[:, :], l[:, u % 2, :]))
                    gt = gate[:, i, :].rearrange("p (h c) -> p h c", c=3)[:, a * G:(a + 1) * G, br]
                    link(V.tensor_tensor(gr[:, :], gr[:, :], gt, ALU.mult))
                    if br == CMP and i == 0:
                        link(V.tensor_scalar(gr[:, :], gr[:, :], m.seen[:, 0:1], None, ALU.mult))
                    dve.wait_ge(o_ps, u + 1)
                    if br == CMP and i >= 2:
                        dve.wait_ge(pt_ps, of("o", u - 2 * 3 * KV + (KV - 1 - a) * 3 + WIN)[0] + 1)
                    oo = o[:, i % 2, a * 256:(a + 1) * 256].rearrange("p (g d) -> p g d", g=G)
                    src = PS[:, 6 + u % 2, 0:256].rearrange("p (g d) -> p g d", g=G)
                    bc = gr[:, :].unsqueeze(2).to_broadcast([P, G, HD])
                    if br == CMP:
                        link_or(V.tensor_tensor(oo, src, bc, ALU.mult), False)
                    else:
                        tt = tmp[:, :].rearrange("p (g d) -> p g d", g=G)
                        link(V.tensor_tensor(tt, src, bc, ALU.mult))
                        link_or(V.tensor_tensor(oo, oo, tt, ALU.add), br == WIN and a == KV - 1)
                elif br == WIN:
                    dve.wait_ge(o_ps, u + 1)
                    if a:
                        dve.wait_ge(pt_ps, of("o", u - 3)[0] + 1)
                    b0 = PS[0:NB * TS, 6 + a % 2, 0:256].rearrange("p (b k d) -> p b k d", b=2, k=KV)
                    for v in range(KV):
                        rows = slice(v * G * TS, (v + 1) * G * TS)
                        for dup in range(2):
                            last = V.tensor_copy(oS[rows, :, dup, :], b0[rows, :, v, :])
                    last.then_inc(o_ok, 1)

            def link_or(ins, signal):
                if signal:
                    ins.then_inc(o_ok, 1)
                else:
                    link(ins)

            for s in range(len(units) + 1):
                if s and units[s - 1][0] == "s":
                    normalise_sample(s - 1)
                if s < len(units):
                    scores(s)
                if s:
                    outputs(s - 1)

        @block.tensor
        def _(pe):
            MM = nc.tensor.matmul

            def scores(u):
                kind, br, a, i = units[u]
                if kind == "p" or u == NPU:
                    if u:
                        pe.wait_ge(s_ok, u)
                else:
                    pe.wait_ge(s_ok, u - 1)
                b0 = 2 * (u % 2)
                if kind == "p":
                    rows = slice(a * HD, (a + 1) * HD)
                    w = sum(keys[u])
                    rhs = m.kcT[rows, 0:NCMP] if br == CMP else m.KT[rows, br - 1, 0, 0:w]
                    for g in range(G):
                        last = MM(PS[:, g, 0:w], m.qT[rows, g, i * P:(i + 1) * P], rhs, start=True, stop=True)
                else:
                    if u == NPU:
                        pe.wait_ge(qs_ok, 1)
                    for r in range(2):
                        b = 2 * a + r
                        s = dict(start=(r == 0), stop=(r == 1))
                        if br == CMP:
                            last = MM(PS[:, b0, 0:NCMP], Qs[:, b, :], m.kcT[:, (1 + b) * NCMP:(2 + b) * NCMP], **s)
                        else:
                            MM(PS[:, b0, :], Qs[:, b, :], m.KT[:, br - 1, 1 + b, 0:512], **s)
                            last = MM(PS[:, b0 + 1, 0:TS], Qs[:, b, :], m.KT[:, br - 1, 1 + b, 512:LS], **s)
                last.then_inc(s_ps, 1)

            def turn(u):
                kind, br, a, i = units[u]
                if kind == "p":
                    pe.wait_ge(e_ok, u + 1)
                else:
                    pe.wait_ge(pn_ok, u - NPU + 1)
                for n in of("k", u):
                    if n >= 2:
                        pe.wait_ge(pt_a, n - 1)
                    for x, j in enumerate(pieces[n][2]):
                        kw = keys[u][j]
                        if kind == "p":
                            for g in range(G):
                                last = nc.tensor.transpose(PS[0:kw, 4 + n % 2, g * P:(g + 1) * P], pr[:, u % 2, g * 512 + j * P:g * 512 + j * P + kw], m.ident[:, :])
                        else:
                            last = nc.tensor.transpose(PS[0:kw, 4 + n % 2, x * P:(x + 1) * P], pr[:, u % 2, j * P:j * P + kw], m.ident[:, :])
                    last.then_inc(pt_ps, 1)

            def values(u):
                kind, br, a, i = units[u]
                pe.wait_ge(pt_a, of("k", u)[-1] + 1)
                pe.wait_ge(s_ok, u + 1)
                nk = len(keys[u])
                if kind == "p":
                    for g in range(G):
                        for j, kw in enumerate(keys[u]):
                            rhs = m.vc[:, 0, a * HD:(a + 1) * HD] if br == CMP else m.z[:, j, (384 if br == SEL else 640) + a * HD:(384 if br == SEL else 640) + (a + 1) * HD]
                            last = MM(PS[:, 6 + u % 2, g * HD:(g + 1) * HD], pT[0:kw, j, g * P:(g + 1) * P], rhs, start=(j == 0), stop=(j == nk - 1))
                else:
                    if a >= 2 and br == CMP:
                        pe.wait_ge(o_ok, PT + a - 1)
                    for r in range(2):
                        b = 2 * a + r
                        for j, kw in enumerate(keys[u]):
                            if br == CMP:
                                rhs = m.vc[:, 1 + b, :]
                            else:
                                rhs = m.V[:, br - 1, b * PAGES + j, :] if j < 4 else m.Vn[:, br - 1, b, :]
                            last = MM(PS[0:64, 6 + a % 2, r * P:(r + 1) * P], pT[0:kw, j, r * 64:(r + 1) * 64], rhs,
                                      start=(br == CMP and r == 0 and j == 0), stop=(br == WIN and j == nk - 1), skip_group_check=True)
                last.then_inc(o_ps, 1)

            def finish(u):
                kind, br, a, i = units[u]
                n = of("o", u)[0]
                pe.wait_ge(pt_a, n - 1)
                pe.wait_ge(o_ok, (i if kind == "p" else PT + a) + 1)
                if kind == "p":
                    for c in range(4):
                        last = nc.tensor.transpose(PS[:, 4 + n % 2, c * P:(c + 1) * P], o[:, i % 2, c * P:(c + 1) * P], m.ident[:, :])
                else:
                    for r in range(2):
                        last = nc.tensor.transpose(PS[:, 4 + n % 2, r * 64:(r + 1) * 64], oS[:, r, :, :].rearrange("p u d -> p (u d)"), m.ident[0:64, 0:64])
                last.then_inc(pt_ps, 1)

            for s in range(len(units) + 2):
                if s < len(units):
                    scores(s)
                if s >= 2 and ends(s - 2):
                    finish(s - 2)
                if 1 <= s <= len(units):
                    turn(s - 1)
                    values(s - 1)


T = 128
TOPK = 2
NT = (TOPK * NTOK + NE * (T - 1)) // T
RING = 4
TURNS = -(-NT // RING)
FRONT = NT - NT // RING


def stage_route(nc, m, sb, sem, t, outs):
    PS = m.PS
    w_in, x_in, mod_in, r_in = sem("r_w_in"), sem("r_x_in"), sem("r_mod_in"), sem("r_r_in")
    y_ps, x2_ok, sq_ok, rt_ok, h_ok, hT_ps, hT_ok, lg_ps = [sem("r_" + x) for x in ("y_ps", "x2_ok", "sq_ok", "rt_ok", "h_ok", "hT_ps", "hT_ok", "lg_ps")]
    chain, pch, exp_in, exp_ok, cnt_ok, cnt_ps = [sem("r_" + x) for x in ("chain", "pch", "exp_in", "exp_ok", "cnt_ok", "cnt_ps")]
    KMAX = -(-NTOK // T)
    with ExitStack() as ctx:
        def tb(name, shape, dt=F32):
            return ctx.enter_context(nc.sbuf_tensor(name, shape, dt))
        wo = tb("wo", [P, 8, D])
        mod = tb("mod_r", [P, 2, 3, D])
        h2 = m.h2
        hT = tb("h2T", [P, 2, KD, P])
        rw = tb("rw", [P, KD, NG + NE])
        rb = tb("rb", [P, NG + NE])
        ssq = tb("ssq_r", [P, 3, TILES])
        lg = tb("lg", [P, TILES, NG + NE])
        it = tb("it", [P, NE], I32)
        down = tb("down", [P, NE])
        kt = tb("kt", [P, KMAX])
        iti = tb("iti", [1, TURNS, RING], I32)
        itf = tb("itf", [1, TURNS * RING])
        a4, oh4, e4 = tb("a4", [P, TILES, NG]), tb("oh4", [P, TILES, NG]), tb("e4", [P, TILES, NG])
        s1, wgt = tb("s1", [P, TILES]), tb("wgt", [P, TILES])
        le, pe8, a8 = tb("le", [P, TILES, EPG]), tb("pe8", [P, TILES, EPG]), tb("a8", [P, TILES, EPG])
        oh8 = tb("oh8", [P, 2, TILES, EPG])
        p12 = tb("p12", [P, 2, TILES])
        E = tb("E", [P, 2, TILES, NE])
        C = tb("C", [P, TILES, NE])
        tmp = tb("tmp_r", [P, TILES, NE])
        big = tb("big", [P, NE, KMAX])
        ends = tb("ends", [P, 2, NE])
        base = tb("base", [P, NE])
        posf = tb("posf", [P, 2, TILES])
        tef = tb("tef", [1, TURNS * RING])
        bige = tb("bige", [1, TURNS * RING, NE])
        block = ctx.enter_context(nc.Block())

        @block.sync
        def _(sp):
            for half in range(2):
                sp.dma_start(wo[:, :, half * 512:(half + 1) * 512], t["w_out"][0].rearrange("(c p) n -> p c n", p=P)[:, :, half * 512:(half + 1) * 512]).then_inc(w_in, 16)
            for i in range(PT):
                sp.dma_start(m.x2[:, i, :], t["x_prompt"][0, i * P:(i + 1) * P, :]).then_inc(x_in, 16)
            sp.dma_start(m.x2[0:NB * TS, PT, :], t["x_sample"].rearrange("b j d -> (b j) d")).then_inc(x_in, 16)
            spread_rows(sp, m, mod, 2, 3, mod_in)
            sp.dma_start(rw[:, :, 0:NG], t["router_group_w"][0].rearrange("(k p) n -> p k n", p=P)).then_inc(r_in, 16)
            sp.dma_start(rw[:, :, NG:], t["router_expert_w"][0].rearrange("(k p) n -> p k n", p=P)).then_inc(r_in, 16)
            sp.dma_start(rb[:, 0:NG], t["router_group_b"][0].partition_broadcast(P)).then_inc(r_in, 16)
            sp.dma_start(rb[:, NG:], t["router_expert_b"][0].partition_broadcast(P)).then_inc(r_in, 16)

        @block.gpsimd
        def _(pool):
            link = Chain(pool, pch)
            link(nc.gpsimd.iota(it[:, :], pattern=[[-1, NE]], base=NE, channel_multiplier=0))
            link(nc.gpsimd.tensor_copy(down[:, :], it[:, :]))
            link(nc.gpsimd.iota(it[:, 0:KMAX], pattern=[[T, KMAX]], base=0, channel_multiplier=0))
            link(nc.gpsimd.tensor_copy(kt[:, :], it[:, 0:KMAX]))
            link(nc.gpsimd.iota(iti[:, :, 0:RING - 1], pattern=[[RING - 1, TURNS], [1, RING - 1]], base=0, channel_multiplier=0))
            link(nc.gpsimd.iota(iti[:, :, RING - 1], pattern=[[1, TURNS]], base=FRONT, channel_multiplier=0))
            link(nc.gpsimd.tensor_copy(itf[:, :], iti[:, :, :].rearrange("p t k -> p (t k)")))

        @block.tensor
        def _(pe):
            MM = nc.tensor.matmul
            pe.wait_ge(w_in, 32)
            for i in range(TILES + 1):
                if i < TILES:
                    r, b = ROWS[i], 2 * (i % 2)
                    if i >= 2:
                        pe.wait_ge(x2_ok, i - 1)
                    for half in range(2):
                        for c in range(8):
                            last = MM(PS[0:r, b + half, :], m.mixT[:, c, i * P:i * P + r], wo[:, c, half * 512:(half + 1) * 512], start=(c == 0), stop=(c == 7))
                    last.then_inc(y_ps, 1)
                if i:
                    j = i - 1
                    r = ROWS[j]
                    pe.wait_ge(h_ok, j + 1)
                    if j:
                        pe.wait_ge(hT_ok, j)
                    for k in range(KD):
                        last = nc.tensor.transpose(PS[:, 4 + k // 4, (k % 4) * P:(k % 4) * P + r], h2[0:r, j, k * P:(k + 1) * P], m.ident[0:r, 0:r])
                    last.then_inc(hT_ps, 1)
                    pe.wait_ge(hT_ok, j + 1)
                    if j == 0:
                        pe.wait_ge(r_in, 64)
                    for k in range(KD):
                        last = MM(PS[0:r, 6, j * 40:j * 40 + NG + NE], hT[:, j % 2, k, 0:r], rw[:, k, :], start=(k == 0), stop=(k == KD - 1))
                    last.then_inc(lg_ps, 1)
            pe.wait_ge(cnt_ok, 1)
            for i in range(TILES):
                for j in range(i + 1):
                    MM(PS[:, 7, i * NE:(i + 1) * NE], m.before[:, :] if j == i else m.ones[:, :], C[:, j, :], start=(j == 0), stop=(j == i))
            for j in range(TILES):
                last = MM(PS[:, 7, TILES * NE:(TILES + 1) * NE], m.ones[:, :], C[:, j, :], start=(j == 0), stop=(j == TILES - 1))
            last.then_inc(cnt_ps, 1)

        @block.scalar
        def _(act):
            for i in range(TILES):
                r = ROWS[i]
                act.wait_ge(x2_ok, i + 1)
                nc.scalar.activation(h2[0:r, i, :], m.x2[0:r, i, :], ACT.Square, accum_out=ssq[0:r, 0, i:i + 1]).then_inc(sq_ok, 1)
                act.wait_ge(sq_ok, i + 1)
                nc.scalar.activation(ssq[0:r, 1, i:i + 1], ssq[0:r, 0, i:i + 1], ACT.Sqrt, scale=1.0 / D, bias=m.eps[0:r, 0:1]).then_inc(rt_ok, 1)
            act.wait_ge(exp_in, 1)
            nc.scalar.activation(e4[:, :, :], e4[:, :, :], ACT.Exp).then_inc(exp_ok, 1)
            act.wait_ge(exp_in, 2)
            nc.scalar.activation(pe8[:, :, :], pe8[:, :, :], ACT.Exp).then_inc(exp_ok, 1)

        @block.vector
        def _(dve):
            V = nc.vector
            link = Chain(dve, chain)
            dve.wait_ge(x_in, 16 * TILES)
            dve.wait_ge(mod_in, 16 * SPREAD_DMAS)
            link(V.memset(lg[:, :, :], 0.0))
            for i in range(TILES):
                r, b, v = ROWS[i], 2 * (i % 2), VAR[i]
                dve.wait_ge(y_ps, i + 1)
                link(V.tensor_tensor(h2[0:r, i, :], PS[0:r, b:b + 2, :].rearrange("p b n -> p (b n)"), mod[0:r, v, 0, :], ALU.mult))
                V.tensor_tensor(m.x2[0:r, i, :], m.x2[0:r, i, :], h2[0:r, i, :], ALU.add).then_inc(x2_ok, 1)
                dve.wait_ge(rt_ok, i + 1)
                link(V.reciprocal(ssq[0:r, 2, i:i + 1], ssq[0:r, 1, i:i + 1]))
                link(V.scalar_tensor_tensor(out=h2[0:r, i, :], in0=m.x2[0:r, i, :], scalar=ssq[0:r, 2, i:i + 1], in1=mod[0:r, v, 2, :], op0=ALU.mult, op1=ALU.mult))
                V.tensor_tensor(h2[0:r, i, :], h2[0:r, i, :], mod[0:r, v, 1, :], ALU.add).then_inc(h_ok, 1)
                dve.wait_ge(hT_ps, i + 1)
                V.tensor_copy(hT[:, i % 2, :, 0:r], PS[:, 4:6, :].rearrange("p b (k n) -> p (b k) n", n=P)[:, :, 0:r]).then_inc(hT_ok, 1)
            dve.wait_ge(lg_ps, TILES)
            for i in range(TILES):
                r = ROWS[i]
                link(V.tensor_tensor(lg[0:r, i, :], PS[0:r, 6, i * 40:i * 40 + NG + NE], rb[0:r, :], ALU.add))
            dve.wait_ge(pch, 7)
            g4 = lg[:, :, 0:NG]
            bc = lambda a, n: a.unsqueeze(2).to_broadcast([P, TILES, n])
            dn = lambda n: down[:, NE - n:].unsqueeze(1).to_broadcast([P, TILES, n])

            def first_of(dst, val, top, tmp_, n):
                link(V.tensor_tensor(tmp_, val, bc(top, n), ALU.is_equal))
                link(V.tensor_tensor(tmp_, tmp_, dn(n), ALU.mult))
                link(V.tensor_reduce(s1[:, :], tmp_, AX, ALU.max))
                link(V.tensor_tensor(dst, tmp_, bc(s1[:, :], n), ALU.is_equal))

            link(V.tensor_reduce(wgt[:, :], g4, AX, ALU.max))
            first_of(oh4[:, :, :], g4, wgt[:, :], a4[:, :, :], NG)
            V.tensor_tensor(e4[:, :, :], g4, bc(wgt[:, :], NG), ALU.subtract).then_inc(exp_in, 1)
            l32 = lg[:, :, NG:].rearrange("p i (g e) -> p i g e", g=NG)
            link(V.tensor_tensor(tmp[:, :, :].rearrange("p i (g e) -> p i g e", g=NG), l32, oh4[:, :, :].unsqueeze(3).to_broadcast([P, TILES, NG, EPG]), ALU.mult))
            link(V.tensor_reduce(le[:, :, :], tmp[:, :, :].rearrange("p i (g e) -> p i e g", g=NG), AX, ALU.add))
            link(V.tensor_reduce(s1[:, :], le[:, :, :], AX, ALU.max))
            V.tensor_tensor(pe8[:, :, :], le[:, :, :], bc(s1[:, :], EPG), ALU.subtract).then_inc(exp_in, 1)
            dve.wait_ge(exp_ok, 1)
            link(V.tensor_reduce(wgt[:, :], e4[:, :, :], AX, ALU.add))
            link(V.reciprocal(wgt[:, :], wgt[:, :]))
            dve.wait_ge(exp_ok, 2)
            link(V.tensor_reduce(s1[:, :], pe8[:, :, :], AX, ALU.add))
            link(V.reciprocal(s1[:, :], s1[:, :]))
            link(V.tensor_tensor(pe8[:, :, :], pe8[:, :, :], bc(s1[:, :], EPG), ALU.mult))
            for c in range(TOPK):
                link(V.tensor_reduce(p12[:, c, :], pe8[:, :, :], AX, ALU.max))
                first_of(oh8[:, c], pe8[:, :, :], p12[:, c, :], a8[:, :, :], EPG)
                if c == 0:
                    link(V.scalar_tensor_tensor(out=pe8[:, :, :], in0=oh8[:, 0], scalar=-2.0, in1=pe8[:, :, :], op0=ALU.mult, op1=ALU.add))
            link(V.tensor_tensor(s1[:, :], p12[:, 0, :], p12[:, 1, :], ALU.add))
            link(V.reciprocal(s1[:, :], s1[:, :]))
            link(V.tensor_tensor(s1[:, :], s1[:, :], wgt[:, :], ALU.mult))
            for c in range(TOPK):
                link(V.tensor_tensor(m.choice[:, c, :], p12[:, c, :], s1[:, :], ALU.mult))
                link(V.tensor_tensor(E[:, c].rearrange("p i (g e) -> p i g e", g=NG), oh4[:, :, :].unsqueeze(3).to_broadcast([P, TILES, NG, EPG]),
                                     oh8[:, c].unsqueeze(2).to_broadcast([P, TILES, NG, EPG]), ALU.mult))
            link(V.memset(E[NB * TS:P, :, PT, :], 0.0))
            V.tensor_tensor(C[:, :, :], E[:, 0], E[:, 1], ALU.add).then_inc(cnt_ok, 1)
            dve.wait_ge(cnt_ps, 1)
            link(V.tensor_tensor(big[:, :, :], PS[:, 7, TILES * NE:(TILES + 1) * NE].unsqueeze(2).to_broadcast([P, NE, KMAX]),
                                 kt[:, :].unsqueeze(1).to_broadcast([P, NE, KMAX]), ALU.is_gt))
            link(V.tensor_reduce(base[:, :], big[:, :, :], AX, ALU.add))
            link(V.tensor_copy(ends[:, 0, :], base[:, :]))
            a = 0
            for s in (1, 2, 4, 8, 16):
                link(V.tensor_copy(ends[:, 1 - a, 0:s], ends[:, a, 0:s]))
                link(V.tensor_tensor(ends[:, 1 - a, s:NE], ends[:, a, s:NE], ends[:, a, 0:NE - s], ALU.add))
                a = 1 - a
            link(V.tensor_tensor(base[:, :], ends[:, a, :], base[:, :], ALU.subtract))
            link(V.tensor_scalar(base[:, :], base[:, :], float(T), None, ALU.mult))
            for c in range(TOPK):
                link(V.tensor_tensor(tmp[:, :, :], PS[:, 7, 0:TILES * NE].rearrange("p (i e) -> p i e", e=NE), base[:, :].unsqueeze(1).to_broadcast([P, TILES, NE]), ALU.add))
                link(V.tensor_tensor(tmp[:, :, :], tmp[:, :, :], E[:, c], ALU.mult))
                link(V.tensor_reduce(posf[:, c, :], tmp[:, :, :], AX, ALU.add))
            link(V.tensor_copy(m.pos[:, :], posf[:, :, :].rearrange("p c i -> p (c i)")))
            link(V.tensor_tensor(bige[:, :, :], ends[0:1, a, :].unsqueeze(1).to_broadcast([1, TURNS * RING, NE]), itf[:, :].unsqueeze(2).to_broadcast([1, TURNS * RING, NE]), ALU.is_le))
            link(V.tensor_reduce(tef[:, :], bige[:, :, :], AX, ALU.add))
            link(V.tensor_scalar(itf[:, :], tef[:, :], float(NE), None, ALU.is_lt))
            link(V.tensor_copy(m.te[:, 1, :], itf[:, :]))
            link(V.tensor_scalar(tef[:, :], tef[:, :], float(NE - 1), None, ALU.min))
            link(V.tensor_copy(m.te[:, 0, :], tef[:, :]))


def stage_experts(nc, m, sb, sem, t, outs):
    PS = m.PS
    w_in = [sem(f"e_w_in{i}") for i in range(RING)]
    xs_out = sem("e_xs_out")
    x_in, y_out = [sem(f"e_x_in{i}") for i in range(2)], [sem(f"e_y_out{i}") for i in range(2)]
    t_ps, t_ok, gu_ps, silu_ok, he_ok, dn_ps, y_a, y_v = [sem("e_" + x) for x in ("t_ps", "t_ok", "gu_ps", "silu_ok", "he_ok", "dn_ps", "y_a", "y_v")]
    DC = DE // P
    with ExitStack() as ctx:
        def tb(name, shape):
            return ctx.enter_context(nc.sbuf_tensor(name, shape, F32))
        wg, wu, wd = tb("wg", [P, RING, KD, DE]), tb("wu", [P, RING, KD, DE]), tb("wd", [P, RING, DC, D])
        xr, xT = tb("xr", [T, 2, D]), tb("xsT", [P, 2, KD, T])
        sg, he = tb("sg", [P, 2, DC * T]), tb("he", [P, 2, DC * T])
        yr = tb("yr", [T, 2, D])
        block = ctx.enter_context(nc.Block())

        @block.sync
        def _(sp):
            def step(s):
                if not s.exists(0):
                    return
                if s.is_step(1):
                    sp.wait_ge(xs_out, 16 * TILES * TOPK)
                s.wait(sp, dn_ps, s.tile(-RING + 1))
                e = sp.value_load(s.at(m.te[0:1, 0, :], 1), min_val=0, max_val=NE - 1)
                skip = {}
                if s.may_be_unused():
                    used = sp.value_load(s.at(m.te[0:1, 1, :], 1), min_val=0, max_val=1)
                    skip = dict(cond=used > 0, cond_hint=True)
                k = s.slot(0, RING)
                sp.dma_start(wg[:, k], t["expert_w_gate"][0, bass.ds(e, 1)].rearrange("o (k p) n -> p (o k) n", p=P), **skip).then_inc(w_in[k], 16)
                sp.dma_start(wu[:, k], t["expert_w_up"][0, bass.ds(e, 1)].rearrange("o (k p) n -> p (o k) n", p=P), **skip).then_inc(w_in[k], 16)
                sp.dma_start(wd[:, k], t["expert_w_down"][0, bass.ds(e, 1)].rearrange("o (c p) n -> p (o c) n", p=P), **skip).then_inc(w_in[k], 16)
            run_steps(nc, sp, step)

        @block.gpsimd
        def _(pool):
            for i in range(TILES):
                r = ROWS[i]
                for c in range(TOPK):
                    pool.indirect_dma_start(m.xs_dram.ap(), bass.IndirectOffsetOnAxis(ap=m.pos[0:r, c * TILES + i:c * TILES + i + 1], axis=0),
                                            m.h2[0:r, i, :], None).then_inc(xs_out, 16)
            pool.wait_ge(xs_out, 16 * TILES * TOPK)

            def step(s):
                if not s.exists(0):
                    return
                s.wait(pool, t_ps, s.tile(-1))
                k = s.slot(0, 2)
                pool.dma_start(xr[:, k, :], s.rows(m.xs_dram, 0)).then_inc(x_in[k], 16)
            run_steps(nc, pool, step)

        @block.tensor
        def _(pe):
            MM = nc.tensor.matmul

            def rows_in(s, d):
                s.wait(pe, x_in[s.slot(d, 2)], s.fills(d, 2) * 16)

            def turn(s, d):
                k = s.slot(d, 2)
                for c in range(KD):
                    last = nc.tensor.transpose(PS[:, c // 4, (c % 4) * P:(c % 4) * P + T], xr[:, k, c * P:(c + 1) * P], m.ident[0:T, 0:T])
                last.then_inc(t_ps, 1)

            def gate_up(s):
                k, k2 = s.slot(0, RING), s.slot(0, 2)
                s.wait(pe, t_ok, s.tile(1))
                s.wait(pe, w_in[k], s.fills(0, RING) * 48)
                s.wait(pe, he_ok, s.tile(-1))
                for j, w in enumerate((wg, wu)):
                    for c in range(DC):
                        for q in range(KD):
                            last = MM(PS[:, 2 + k2, (j * DC + c) * T:(j * DC + c + 1) * T], w[:, k, q, c * P:(c + 1) * P], xT[:, k2, q, :], start=(q == 0), stop=(q == KD - 1))
                last.then_inc(gu_ps, 1)

            def down(s):
                k, k2 = s.slot(-1, RING), s.slot(-1, 2)
                s.wait(pe, he_ok, s.tile(0))
                s.wait(pe, y_a, s.tile(-2))
                s.wait(pe, y_v, s.tile(-2))
                for half in range(2):
                    for c in range(DC):
                        last = MM(PS[0:T, 4 + 2 * k2 + half, :], he[:, k2, c * T:(c + 1) * T], wd[:, k, c, half * 512:(half + 1) * 512], start=(c == 0), stop=(c == DC - 1))
                last.then_inc(dn_ps, 1)

            def step(s):
                if s.is_step(0):
                    rows_in(s, 0)
                    turn(s, 0)
                if s.exists(0):
                    gate_up(s)
                if s.exists(1):
                    rows_in(s, 1)
                    turn(s, 1)
                if s.exists(-1):
                    down(s)
            run_steps(nc, pe, step)

        @block.scalar
        def _(act):
            def step(s):
                if s.exists(0):
                    k = s.slot(0, 2)
                    s.wait(act, gu_ps, s.tile(1))
                    s.wait(act, he_ok, s.tile(-1))
                    nc.scalar.activation(sg[:, k, :], PS[:, 2 + k, 0:DC * T], ACT.Silu).then_inc(silu_ok, 1)
                if s.exists(-1):
                    k = s.slot(-1, 2)
                    s.wait(act, dn_ps, s.tile(0))
                    s.wait(act, y_out[k], (s.fills(-1, 2) - 1) * 16)
                    nc.scalar.copy(yr[:, k, 0:512], PS[0:T, 4 + 2 * k, :]).then_inc(y_a, 1)
                    s.wait(act, y_a, s.tile(0))
                    s.wait(act, y_v, s.tile(0))
                    act.dma_start(s.rows(m.ys_dram, -1), yr[:, k, :]).then_inc(y_out[k], 16)
            run_steps(nc, act, step)
            for k in range(2):
                act.wait_ge(y_out[k], 16 * ((NT - k + 1) // 2))

        @block.vector
        def _(dve):
            V = nc.vector

            def take_x(s, d):
                k = s.slot(d, 2)
                s.wait(dve, t_ps, s.tile(d + 1))
                s.wait(dve, gu_ps, s.tile(d - 1))
                V.tensor_copy(xT[:, k], PS[:, 0:2, :].rearrange("p b (c n) -> p (b c) n", n=P)[:, :, 0:T]).then_inc(t_ok, 1)

            def step(s):
                if s.is_step(0):
                    take_x(s, 0)
                if s.exists(0):
                    k = s.slot(0, 2)
                    s.wait(dve, silu_ok, s.tile(1))
                    s.wait(dve, dn_ps, s.tile(-1))
                    V.tensor_tensor(he[:, k, :], sg[:, k, :], PS[:, 2 + k, DC * T:2 * DC * T], ALU.mult).then_inc(he_ok, 1)
                if s.exists(1):
                    take_x(s, 1)
                if s.exists(-1):
                    k = s.slot(-1, 2)
                    s.wait(dve, dn_ps, s.tile(0))
                    s.wait(dve, y_out[k], (s.fills(-1, 2) - 1) * 16)
                    V.tensor_copy(yr[:, k, 512:], PS[0:T, 5 + 2 * k, :]).then_inc(y_v, 1)
            run_steps(nc, dve, step)


class Step:

    def __init__(self, turn, k):
        self.turn, self.k = turn, k

    def tile(self, d):
        return self.turn * RING + (self.k + d)

    def slot(self, d, ring):
        return (self.k + d) % ring

    def fills(self, d, ring):
        return self.turn * (RING // ring) + ((self.k + d) // ring + 1)

    def is_step(self, n):
        return isinstance(self.turn, int) and self.tile(0) == n

    def exists(self, d):
        return not isinstance(self.turn, int) or 0 <= self.tile(d) < NT

    def may_be_unused(self):
        return not isinstance(self.turn, int) or self.turn > 0 and self.sorted_tile(0) >= TOPK * NTOK // T

    def wait(self, eng, sem, value):
        if not isinstance(value, int) or value > 0:
            eng.wait_ge(sem, value)

    def at(self, ap, n):
        s = self.tile(0)
        return ap[:, s:s + n] if isinstance(s, int) else ap[:, bass.ds(s, n)]

    def sorted_tile(self, d):
        turn, k = self.turn + (self.k + d) // RING, (self.k + d) % RING
        return turn + FRONT if k == RING - 1 else turn * (RING - 1) + k

    def rows(self, dram, d):
        s = self.sorted_tile(d)
        ap = dram.ap().rearrange("(j p) d -> j p d", p=T)
        return ap[s] if isinstance(s, int) else ap[bass.ds(s, 1)].rearrange("o p d -> (o p) d")


def run_steps(nc, eng, step):
    for k in range(RING):
        step(Step(0, k))
    with nc.Fori(1, (NT - 1) // RING, engines=[eng.engine]) as turn:
        for k in range(RING):
            step(Step(turn, k))
    for s in range((NT - 1) // RING * RING, NT + 1):
        step(Step(s // RING, s % RING))


def stage_final(nc, m, sb, sem, t, outs):
    mod_in, g_in, a_in, o_ok, out_done, sq, rt, chain = [sem("f_" + x) for x in ("mod_in", "g_in", "a_in", "o_ok", "out_done", "sq", "rt", "chain")]
    row_in = [[sem(f"f_row{c}{k}") for k in range(2)] for c in range(TOPK)]
    with ExitStack() as ctx:
        def tb(name, shape):
            return ctx.enter_context(nc.sbuf_tensor(name, shape, F32))
        mod = tb("mod_f", [P, 2, 1, D])
        fg = tb("fg", [P, D])
        rows = tb("rows", [P, TOPK, 2, D])
        junk = tb("junk_f", [P, D])
        ssq = tb("ssq_f", [P, 3, TILES])
        block = ctx.enter_context(nc.Block())

        @block.sync
        def _(sp):
            spread_rows(sp, m, mod, 5, 1, mod_in)
            sp.dma_start(fg[:, :], t["final_norm_g"].partition_broadcast(P)).then_inc(g_in, 16)
            for i in range(TILES):
                sp.wait_ge(o_ok, i + 1)
                if i < PT:
                    sp.dma_start(outs[0][0, i * P:(i + 1) * P, :], m.x2[:, i, :]).then_inc(out_done, 16)
                else:
                    sp.dma_start(outs[1].rearrange("b j d -> (b j) d"), m.x2[0:NB * TS, i, :]).then_inc(out_done, 16)
            sp.wait_ge(out_done, 16 * TILES)

        @block.gpsimd
        def _(pool):
            for i in range(TILES):
                r = ROWS[i]
                for c in range(TOPK):
                    if i >= 2:
                        pool.wait_ge(a_in, i - 1)
                    pool.indirect_dma_start(rows[0:r, c, i % 2, :], None, m.ys_dram.ap(),
                                            bass.IndirectOffsetOnAxis(ap=m.pos[0:r, c * TILES + i:c * TILES + i + 1], axis=0)).then_inc(row_in[c][i % 2], 16)

        @block.scalar
        def _(act):
            for i in range(TILES):
                r = ROWS[i]
                act.wait_ge(a_in, i + 1)
                nc.scalar.activation(junk[0:r, :], m.x2[0:r, i, :], ACT.Square, accum_out=ssq[0:r, 0, i:i + 1]).then_inc(sq, 1)
                act.wait_ge(sq, i + 1)
                nc.scalar.activation(ssq[0:r, 1, i:i + 1], ssq[0:r, 0, i:i + 1], ACT.Sqrt, scale=1.0 / D, bias=m.eps[0:r, 0:1]).then_inc(rt, 1)

        @block.vector
        def _(dve):
            V = nc.vector
            link = Chain(dve, chain)
            dve.wait_ge(mod_in, 16 * SPREAD_DMAS)
            dve.wait_ge(g_in, 16)

            def normalise(i):
                r = ROWS[i]
                dve.wait_ge(rt, i + 1)
                link(V.reciprocal(ssq[0:r, 2, i:i + 1], ssq[0:r, 1, i:i + 1]))
                V.scalar_tensor_tensor(out=m.x2[0:r, i, :], in0=m.x2[0:r, i, :], scalar=ssq[0:r, 2, i:i + 1], in1=fg[0:r, :], op0=ALU.mult, op1=ALU.mult).then_inc(o_ok, 1)

            for i in range(TILES):
                r, v = ROWS[i], VAR[i]
                for c in range(TOPK):
                    dve.wait_ge(row_in[c][i % 2], 16 * (i // 2 + 1))
                a = rows[0:r, 0, i % 2, :]
                link(V.tensor_scalar(a, a, m.choice[0:r, 0, i:i + 1], None, ALU.mult))
                link(V.scalar_tensor_tensor(out=a, in0=rows[0:r, 1, i % 2, :], scalar=m.choice[0:r, 1, i:i + 1], in1=a, op0=ALU.mult, op1=ALU.add))
                link(V.tensor_tensor(a, a, mod[0:r, v, 0, :], ALU.mult))
                V.tensor_tensor(m.x2[0:r, i, :], m.x2[0:r, i, :], a, ALU.add).then_inc(a_in, 1)
                if i:
                    normalise(i - 1)
            normalise(TILES - 1)


def build(nc, ins, outs):
    t = ins
    with ExitStack() as ctx:
        def sb(name, shape, dt=F32):
            return ctx.enter_context(nc.sbuf_tensor(name, shape, dt))

        held = []

        def sem(name):
            held.append(nc.alloc_semaphore(name))
            return held[-1]

        def stage(function):
            function(nc, m, sb, sem, t, outs)
            nc.clear_and_free_semaphores(held[:])
            held.clear()
            nc.all_engine_barrier()

        m = Bufs()
        m.PS = ctx.enter_context(nc.psum_tensor("PS", [P, 8, 512], F32))
        m.ident = sb("ident", [P, P])
        m.ones = sb("ones", [P, P])
        m.before = sb("before", [P, P])
        m.eps = sb("eps", [P, 3])
        m.seen = sb("seen", [P, 1])
        m.gate_dram = nc.dram_tensor("gate_dram", [NB * TS, 24], F32)
        m.xs_dram = nc.dram_tensor("xs_dram", [NT * T, D], F32)
        m.ys_dram = nc.dram_tensor("ys_dram", [NT * T, D], F32)
        m.pos = sb("pos", [P, TOPK * TILES], I32)
        m.choice = sb("choice", [P, TOPK, TILES])
        m.te = sb("te", [1, 2, TURNS * RING], I32)
        m.mixT = sb("mixT", [P, 8, NTOK])
        m.rb_dram = nc.dram_tensor("rb_dram", [2, H, RB_W], F32)
        m.rb_rep = nc.dram_tensor("rb_rep", [P + TS, H * RB_W], F32)
        m.mod_dram = nc.dram_tensor("mod_dram", [NSEQ, 6 * D], F32)
        stage(lambda *a: stage_modulation(*a[:5]))
        with ExitStack() as att:
            m.z = att.enter_context(nc.sbuf_tensor("z", [P, TILES, ZW], F32))
            m.qT = att.enter_context(nc.sbuf_tensor("qT", [P, G, NTOK], F32))
            with ExitStack() as dn:
                m.same = dn.enter_context(nc.sbuf_tensor("same", [P, 2, P], F32))
                m.upinc = dn.enter_context(nc.sbuf_tensor("upinc", [P, 2, P], F32))
                m.upneg = dn.enter_context(nc.sbuf_tensor("upneg", [P, 2, P], F32))
                m.chunk = dn.enter_context(nc.sbuf_tensor("chunk", [P, 2, P], F32))
                m.bmask = dn.enter_context(nc.sbuf_tensor("bmask", [P, NB], F32))
                m.level = dn.enter_context(nc.sbuf_tensor("level", [P, 6, P], F32))
                m.convwT = dn.enter_context(nc.sbuf_tensor("convwT", [P, 12, CW], F32))
                m.xc = dn.enter_context(nc.sbuf_tensor("xc", [P, 12, CW - 1 + SEQ + NB * (TS + CW - 1)], F32))
                stage(stage_projection)
                with nc.sbuf_tensor("yT", [P, 12, NPAD], F32) as m.yT, nc.sbuf_tensor("kvt", [P, TILES, 2 * DNH * HD], F32) as m.kvt:
                    stage(stage_conv)
                    stage(stage_delta)
            m.kcT = att.enter_context(nc.sbuf_tensor("kcT", [P, NSEQ * NCMP], F32))
            m.vc = att.enter_context(nc.sbuf_tensor("vc", [NCMP, NSEQ, P], F32))
            m.V = att.enter_context(nc.sbuf_tensor("V", [P, 2, NB * PAGES, P], F32))
            m.Vn = att.enter_context(nc.sbuf_tensor("Vn", [TS, 2, NB, P], F32))
            m.biasS = att.enter_context(nc.sbuf_tensor("biasS", [P, 2, LS], F32))
            m.pages = att.enter_context(nc.sbuf_tensor("pages", [P, 2, NB * PAGES, P], F32))
            stage(stage_compress)
            m.KT = att.enter_context(nc.sbuf_tensor("KT", [P, 2, NSEQ, LS], F32))
            m.strip = att.enter_context(nc.sbuf_tensor("strip", [P, H, STRIP], F32))
            stage(stage_keys)
            stage(stage_attention)
        m.x2 = sb("x2", [P, TILES, D])
        m.h2 = sb("h2", [P, TILES, D])
        stage(stage_route)
        stage(stage_experts)
        stage(stage_final)


_INS = ['x_prompt', 'x_sample', 'cache_cmp_k', 'cache_cmp_v', 'cache_sel_k', 'cache_sel_v', 'cache_win_k', 'cache_win_v',
        'state_delta', 'state_conv', 'page_table', 'c_prompt', 'c_sample', 'rel_bias', 'w_ada', 'b_ada', 'norm_mix_g',
        'norm_ffn_g', 'w_in', 'cmp_pos_k', 'cmp_w1_k', 'cmp_w2_k', 'cmp_pos_v', 'cmp_w1_v', 'cmp_w2_v', 'conv_w', 'dn_a_log',
        'dn_dt_bias', 'dn_norm_g', 'w_out', 'router_group_w', 'router_group_b', 'router_expert_w', 'router_expert_b',
        'expert_w_gate', 'expert_w_up', 'expert_w_down', 'final_norm_g']
_OUTS = ([(1, SEQ, D), (NB, TS, D)] + [(1, 1, SEQ, KV, HD)] * 6 + [(1, 1, DNH, HD, HD), (1, 1, CW - 1, CONVD)]
         + [(1, NB, TS, KV, HD)] * 4 + [(1, NB, PAST, KV, HD)] * 2 + [(1, NB, DNH, HD, HD), (1, NB, CW - 1, CONVD)])


def kernel(**inputs):
    import numpy as _np
    import concourse.bacc as _bacc
    from concourse import mybir as _mybir
    from concourse.bass_utils import run_bass_kernel_spmd as _run

    nc = _bacc.Bacc("TRN2", target_bir_lowering=False, num_devices=1)
    arrays, ins = {}, {}
    for name in _INS:
        a = _np.ascontiguousarray(inputs[name])
        arrays[f"in_{name}_dram"] = a
        ins[name] = nc.dram_tensor(f"in_{name}_dram", a.shape, _mybir.dt.from_np(a.dtype), kind="ExternalInput").ap()
    outs = [nc.dram_tensor(f"out_{i}_dram", s, _mybir.dt.float32, kind="ExternalOutput").ap() for i, s in enumerate(_OUTS)]
    build(nc, ins, outs)
    r = _run(nc, [arrays], core_ids=[0])
    return tuple(r.results[0][f"out_{i}_dram"] for i in range(len(_OUTS)))
```
